# Optimizing a Trainium2 kernel written in Bass

```python
import jax, jax.numpy as jnp
from jax import lax
import numpy as np
import math

D_MODEL = 1024
BATCH = 1
SEQ = 512
DEPTH = 2

CHUNK = 64
N_A_LAYERS = DEPTH // 2
N_B_LAYERS = DEPTH - N_A_LAYERS
MLA_HEADS = 8
Q_LORA = 384
KV_LORA = 256
NOPE_DIM = 128
ROPE_DIM = 64
V_DIM = 128
ROPE_THETA = 10000.0
Q_BLOCK = 128
B_HEADS = 16
B_HEAD_DIM = 64
LEFT_CHUNKS = 8
BAND = (LEFT_CHUNKS + 1) * CHUNK
MAX_REL = 256
REL_TABLE = MAX_REL + CHUNK
D_FF = -(-8 * D_MODEL // (3 * 256)) * 256
EPS = 1e-6


def rms_norm(x, g):
    xf = x.astype(jnp.float32)
    y = xf * lax.rsqrt(jnp.mean(xf * xf, axis=-1, keepdims=True) + EPS)
    return (y * g.astype(jnp.float32)).astype(x.dtype)

def rope_tables(positions, dtype):
    inv = 1.0 / (ROPE_THETA ** (jnp.arange(0, ROPE_DIM, 2, dtype=jnp.float32) / ROPE_DIM))
    ang = positions.astype(jnp.float32)[..., None] * inv
    return jnp.cos(ang).astype(dtype), jnp.sin(ang).astype(dtype)

def apply_rope(t, cos, sin):
    t1, t2 = jnp.split(t, 2, axis=-1)
    return jnp.concatenate([t1 * cos - t2 * sin, t2 * cos + t1 * sin], axis=-1)

def swiglu(h, w_gate, w_up, w_down):
    return (jax.nn.silu(h @ w_gate) * (h @ w_up)) @ w_down

def mla_mixer(h, cos, sin, w_a, g_q, w_uq, g_kv, w_ukv, w_o):
    B, S, _ = h.shape
    a = h @ w_a
    cq, ckv, kr = jnp.split(a, [Q_LORA, Q_LORA + KV_LORA], axis=-1)
    q = (rms_norm(cq, g_q) @ w_uq).reshape(B, S, MLA_HEADS, NOPE_DIM + ROPE_DIM)
    q_nope = q[..., :NOPE_DIM]
    q_rope = apply_rope(q[..., NOPE_DIM:], cos[:, :, None], sin[:, :, None])
    kv = (rms_norm(ckv, g_kv) @ w_ukv).reshape(B, S, MLA_HEADS, NOPE_DIM + V_DIM)
    k_nope, v = kv[..., :NOPE_DIM], kv[..., NOPE_DIM:]
    k_rope = apply_rope(kr, cos, sin)
    scale = (NOPE_DIM + ROPE_DIM) ** -0.5
    n_blk = S // Q_BLOCK
    key_chunk = jnp.arange(S) // CHUNK

    def to_blocks(t):
        return jnp.moveaxis(t.reshape(B, n_blk, Q_BLOCK, *t.shape[2:]), 1, 0)

    def block_attn(args):
        qn, qr, blk = args
        s = (jnp.einsum('bqhd,bkhd->bhqk', qn, k_nope, preferred_element_type=jnp.float32)
             + jnp.einsum('bqhr,bkr->bhqk', qr, k_rope, preferred_element_type=jnp.float32)) * scale
        q_chunk = (blk * Q_BLOCK + jnp.arange(Q_BLOCK)) // CHUNK
        mask = key_chunk[None, :] <= q_chunk[:, None]
        s = jnp.where(mask[None, None], s, -jnp.inf)
        p = jax.nn.softmax(s, axis=-1).astype(v.dtype)
        return jnp.einsum('bhqk,bkhd->bqhd', p, v)

    o = lax.map(block_attn, (to_blocks(q_nope), to_blocks(q_rope), jnp.arange(n_blk)))
    o = jnp.moveaxis(o, 0, 1).reshape(B, S, MLA_HEADS * V_DIM)
    return o @ w_o

def gather_band(t):
    B, S = t.shape[:2]
    n_c = S // CHUNK
    tp = jnp.pad(t, ((0, 0), (LEFT_CHUNKS * CHUNK, 0), (0, 0), (0, 0)))
    tp = tp.reshape(B, n_c + LEFT_CHUNKS, CHUNK, *t.shape[2:])
    band = jnp.stack([tp[:, j:j + n_c] for j in range(LEFT_CHUNKS + 1)], axis=2)
    return band.reshape(B, n_c, BAND, *t.shape[2:])

def shared_kv(x, g_src, w_kv):
    B, S, _ = x.shape
    kv = (rms_norm(x, g_src) @ w_kv).reshape(B, S, 2, B_HEADS, B_HEAD_DIM)
    return gather_band(kv[:, :, 0]), gather_band(kv[:, :, 1])

def chunked_mixer(h, k_band, v_band, w_q, rel_table, w_o):
    B, S, _ = h.shape
    n_c = S // CHUNK
    q = (h @ w_q).reshape(B, n_c, CHUNK, B_HEADS, B_HEAD_DIM)
    dist = LEFT_CHUNKS * CHUNK + jnp.arange(CHUNK)[:, None] - jnp.arange(BAND)[None, :]
    idx = jnp.clip(dist, -(CHUNK - 1), MAX_REL) + (CHUNK - 1)
    bias = rel_table.astype(jnp.float32)[:, idx]
    valid = (jnp.arange(n_c)[:, None] - LEFT_CHUNKS + jnp.arange(BAND)[None, :] // CHUNK) >= 0
    s = jnp.einsum('bnqhd,bnkhd->bnhqk', q, k_band, preferred_element_type=jnp.float32)
    s = s * (B_HEAD_DIM ** -0.5) + bias[None, None]
    s = jnp.where(valid[None, :, None, None, :], s, -jnp.inf)
    p = jax.nn.softmax(s, axis=-1).astype(v_band.dtype)
    o = jnp.einsum('bnhqk,bnkhd->bnqhd', p, v_band).reshape(B, S, B_HEADS * B_HEAD_DIM)
    return o @ w_o

def first_inputs(seed: int = 0) -> dict:
    key = jax.random.key(seed)
    ks = iter(jax.random.split(key, 32))
    f32 = jnp.float32

    def w(shape, fan_in):
        return jax.random.normal(next(ks), shape, f32) * (fan_in ** -0.5)

    def gain(shape):
        return 1.0 + 0.05 * jax.random.normal(next(ks), shape, f32)

    x = jax.random.normal(next(ks), (BATCH, SEQ, D_MODEL), f32)
    offsets = jax.random.randint(next(ks), (BATCH, 1), 0, 4096, dtype=jnp.int32)
    positions = (jnp.arange(SEQ, dtype=jnp.int32)[None, :] + offsets).astype(jnp.int32)
    return {
        "x": x,
        "positions": positions,
        "attn_pre_g": gain((DEPTH, D_MODEL)),
        "attn_post_g": gain((DEPTH, D_MODEL)),
        "ffn_pre_g": gain((DEPTH, D_MODEL)),
        "ffn_post_g": gain((DEPTH, D_MODEL)),
        "ffn_w_gate": w((DEPTH, D_MODEL, D_FF), D_MODEL),
        "ffn_w_up": w((DEPTH, D_MODEL, D_FF), D_MODEL),
        "ffn_w_down": w((DEPTH, D_FF, D_MODEL), D_FF),
        "mla_w_a": w((N_A_LAYERS, D_MODEL, Q_LORA + KV_LORA + ROPE_DIM), D_MODEL),
        "mla_g_q": gain((N_A_LAYERS, Q_LORA)),
        "mla_w_uq": w((N_A_LAYERS, Q_LORA, MLA_HEADS * (NOPE_DIM + ROPE_DIM)), Q_LORA),
        "mla_g_kv": gain((N_A_LAYERS, KV_LORA)),
        "mla_w_ukv": w((N_A_LAYERS, KV_LORA, MLA_HEADS * (NOPE_DIM + V_DIM)), KV_LORA),
        "mla_w_o": w((N_A_LAYERS, MLA_HEADS * V_DIM, D_MODEL), MLA_HEADS * V_DIM),
        "kv_src_g": gain((D_MODEL,)),
        "w_kv_shared": w((D_MODEL, 2 * B_HEADS * B_HEAD_DIM), D_MODEL),
        "b_w_q": w((N_B_LAYERS, D_MODEL, B_HEADS * B_HEAD_DIM), D_MODEL),
        "b_rel_table": 0.2 * jax.random.normal(next(ks), (N_B_LAYERS, B_HEADS, REL_TABLE), f32),
        "b_w_o": w((N_B_LAYERS, B_HEADS * B_HEAD_DIM, D_MODEL), B_HEADS * B_HEAD_DIM),
    }

def first_block(x, positions, attn_pre_g, attn_post_g, ffn_pre_g, ffn_post_g,
              ffn_w_gate, ffn_w_up, ffn_w_down,
              mla_w_a, mla_g_q, mla_w_uq, mla_g_kv, mla_w_ukv, mla_w_o,
              kv_src_g, w_kv_shared, b_w_q, b_rel_table, b_w_o):
    cos, sin = rope_tables(positions, x.dtype)
    k_band = v_band = None
    for layer in range(DEPTH):
        h = rms_norm(x, attn_pre_g[layer])
        if layer < N_A_LAYERS:
            a = layer
            y = mla_mixer(h, cos, sin, mla_w_a[a], mla_g_q[a], mla_w_uq[a],
                          mla_g_kv[a], mla_w_ukv[a], mla_w_o[a])
        else:
            b = layer - N_A_LAYERS
            y = chunked_mixer(h, k_band, v_band, b_w_q[b], b_rel_table[b], b_w_o[b])
        x = x + rms_norm(y, attn_post_g[layer])
        h = rms_norm(x, ffn_pre_g[layer])
        f = swiglu(h, ffn_w_gate[layer], ffn_w_up[layer], ffn_w_down[layer])
        x = x + rms_norm(f, ffn_post_g[layer])
        if layer == N_A_LAYERS - 1:
            k_band, v_band = shared_kv(x, kv_src_g, w_kv_shared)
    return x


DEPTH_2 = 1

N_HEADS = 8
HEAD_DIM = 64
N_KV_GROUPS = 2
HEADS_PER_GROUP = N_HEADS // N_KV_GROUPS
ATTN_WIDTH = N_HEADS * HEAD_DIM
KV_WIDTH = N_KV_GROUPS * HEAD_DIM
CMP_BLOCK = 32
CMP_STRIDE = 16
CMP_HIDDEN = 128
SEL_BLOCK = 64
SEL_TOP = 16
WINDOW = 512
Q_CHUNK = 64
FORCE_BONUS = 1.0e4
NEG_INF = -1.0e30
CONV_CH = 512
CONV_WIDTH = 31
FFN_DIM = 2816
FFN_CONV_WIDTH = 3
NORM_EPS = 1e-6

IN_SIZES = (ATTN_WIDTH, KV_WIDTH, KV_WIDTH, KV_WIDTH, KV_WIDTH, KV_WIDTH, KV_WIDTH,
            3 * N_HEADS, 2 * CONV_CH, 2 * D_MODEL)
N_IN = sum(IN_SIZES)


def rms_norm_2(x, g):
    xf = x.astype(jnp.float32)
    y = xf * lax.rsqrt(jnp.mean(xf * xf, axis=-1, keepdims=True) + NORM_EPS)
    return (y * g.astype(jnp.float32)).astype(x.dtype)

def layer_norm(x, g, b):
    xf = x.astype(jnp.float32)
    mu = jnp.mean(xf, axis=-1, keepdims=True)
    var = jnp.mean(jnp.square(xf - mu), axis=-1, keepdims=True)
    y = (xf - mu) * lax.rsqrt(var + NORM_EPS)
    return (y * g.astype(jnp.float32) + b.astype(jnp.float32)).astype(x.dtype)

def causal_dwconv(x, w):
    k, c = w.shape
    return lax.conv_general_dilated(x, w[:, None, :], window_strides=(1,), padding=[(k - 1, 0)],
                                    dimension_numbers=('NWC', 'WIO', 'NWC'), feature_group_count=c)

def alibi_slopes():
    return jnp.power(2.0, -8.0 * jnp.arange(1, N_HEADS + 1, dtype=jnp.float32) / N_HEADS)

def compress(kv, pe, w1, w2):
    b, s, g, dh = kv.shape
    ncmp = (s - CMP_BLOCK) // CMP_STRIDE + 1
    idx = np.arange(ncmp)[:, None] * CMP_STRIDE + np.arange(CMP_BLOCK)[None, :]
    blk = kv[:, idx] + pe[None, None, :, None, :]
    blk = jnp.transpose(blk, (0, 1, 3, 2, 4)).reshape(b, ncmp, g, CMP_BLOCK * dh)
    return jax.nn.gelu(blk @ w1) @ w2

def cmp_to_sel_map(s):
    ncmp = (s - CMP_BLOCK) // CMP_STRIDE + 1
    nsel = s // SEL_BLOCK
    cs = np.arange(ncmp) * CMP_STRIDE
    ce = cs + CMP_BLOCK - 1
    ss = np.arange(nsel) * SEL_BLOCK
    se = ss + SEL_BLOCK - 1
    ov = np.minimum(ce[:, None], se[None, :]) - np.maximum(cs[:, None], ss[None, :]) + 1
    return jnp.asarray(np.clip(ov, 0, None).astype(np.float32) / CMP_BLOCK)

def nsa_attention(q, k_cmp, v_cmp, k_sel, v_sel, k_win, v_win, gate_logits, pe_k, pe_v, ck1, ck2, cv1, cv2):
    b, s, _ = q.shape
    G, J, Dh = N_KV_GROUPS, HEADS_PER_GROUP, HEAD_DIM
    f32 = jnp.float32
    q = q.reshape(b, s, G, J, Dh)
    kv = lambda t: t.reshape(b, s, G, Dh)
    k_cmp, v_cmp, k_sel, v_sel, k_win, v_win = map(kv, (k_cmp, v_cmp, k_sel, v_sel, k_win, v_win))
    slopes = alibi_slopes().reshape(G, J)
    pos = jnp.arange(s)
    scale = HEAD_DIM ** -0.5

    kc = compress(k_cmp, pe_k, ck1, ck2)
    vc = compress(v_cmp, pe_v, cv1, cv2)
    ncmp = kc.shape[1]
    c_end = jnp.arange(ncmp) * CMP_STRIDE + CMP_BLOCK - 1
    dist_c = pos[:, None] - c_end[None, :]
    valid_c = dist_c >= 0
    s_c = jnp.einsum('btgjd,bngd->bgjtn', q, kc).astype(f32) * scale - slopes[:, :, None, None] * dist_c
    s_c = jnp.where(valid_c, s_c, NEG_INF)
    p_c = jax.nn.softmax(s_c, axis=-1) * valid_c
    o_c = jnp.einsum('bgjtn,bngd->btgjd', p_c.astype(vc.dtype), vc)

    nsel = s // SEL_BLOCK
    n_top = min(SEL_TOP, nsel)
    imp = jnp.einsum('bgjtn,nk->bgtk', p_c, cmp_to_sel_map(s))
    blk_id = jnp.arange(nsel)[None, :]
    cur = (pos // SEL_BLOCK)[:, None]
    forced = (blk_id == 0) | (blk_id == cur) | (blk_id == cur - 1)
    imp = jnp.where(blk_id <= cur, imp + FORCE_BONUS * forced, NEG_INF)
    _, sel_idx = lax.top_k(imp, n_top)

    ks_blocks = k_sel.reshape(b, nsel, SEL_BLOCK, G, Dh).transpose(0, 3, 1, 2, 4)
    vs_blocks = v_sel.reshape(b, nsel, SEL_BLOCK, G, Dh).transpose(0, 3, 1, 2, 4)
    gather = jax.vmap(jax.vmap(lambda blocks, ids: blocks[ids]))
    kw_pad = jnp.pad(k_win, ((0, 0), (WINDOW, 0), (0, 0), (0, 0)))
    vw_pad = jnp.pad(v_win, ((0, 0), (WINDOW, 0), (0, 0), (0, 0)))
    m_sel = n_top * SEL_BLOCK

    def chunk(c):
        t0 = c * Q_CHUNK
        qc = lax.dynamic_slice_in_dim(q, t0, Q_CHUNK, axis=1)
        tq = t0 + jnp.arange(Q_CHUNK)
        ids = lax.dynamic_slice_in_dim(sel_idx, t0, Q_CHUNK, axis=2)
        ksg = gather(ks_blocks, ids).reshape(b, G, Q_CHUNK, m_sel, Dh)
        vsg = gather(vs_blocks, ids).reshape(b, G, Q_CHUNK, m_sel, Dh)
        kpos = (ids[..., None] * SEL_BLOCK + jnp.arange(SEL_BLOCK)).reshape(b, G, Q_CHUNK, m_sel)
        dist_s = (tq[None, None, :, None] - kpos)[:, :, None]
        s_s = jnp.einsum('btgjd,bgtmd->bgjtm', qc, ksg).astype(f32) * scale \
            - slopes[None, :, :, None, None] * dist_s
        p_s = jax.nn.softmax(jnp.where(dist_s >= 0, s_s, NEG_INF), axis=-1)
        o_s = jnp.einsum('bgjtm,bgtmd->btgjd', p_s.astype(vsg.dtype), vsg)
        kw = lax.dynamic_slice_in_dim(kw_pad, t0, Q_CHUNK + WINDOW, axis=1)
        vw = lax.dynamic_slice_in_dim(vw_pad, t0, Q_CHUNK + WINDOW, axis=1)
        kpos_w = t0 - WINDOW + jnp.arange(Q_CHUNK + WINDOW)
        dist_w = tq[:, None] - kpos_w[None, :]
        valid_w = (dist_w >= 0) & (dist_w < WINDOW) & (kpos_w[None, :] >= 0)
        s_w = jnp.einsum('btgjd,bsgd->bgjts', qc, kw).astype(f32) * scale - slopes[:, :, None, None] * dist_w
        p_w = jax.nn.softmax(jnp.where(valid_w, s_w, NEG_INF), axis=-1)
        o_w = jnp.einsum('bgjts,bsgd->btgjd', p_w.astype(vw.dtype), vw)
        return o_s, o_w

    o_s, o_w = lax.map(chunk, jnp.arange(s // Q_CHUNK))
    o_s = jnp.moveaxis(o_s, 0, 1).reshape(b, s, G, J, Dh)
    o_w = jnp.moveaxis(o_w, 0, 1).reshape(b, s, G, J, Dh)

    g = jax.nn.sigmoid(gate_logits).reshape(b, s, G, J, 3)
    o = g[..., 0:1] * o_c + g[..., 1:2] * o_s + g[..., 2:3] * o_w
    return o.reshape(b, s, ATTN_WIDTH)

def conformer_conv(u, dw_w, dw_b, ln_g, ln_b, w_proj):
    a, gate = jnp.split(u, 2, axis=-1)
    z = a * jax.nn.sigmoid(gate)
    z = causal_dwconv(z, dw_w) + dw_b
    z = jax.nn.silu(layer_norm(z, ln_g, ln_b))
    return z @ w_proj

def conv_ffn(h, w_up, dw_w, dw_b, w_down):
    u = causal_dwconv(h @ w_up, dw_w) + dw_b
    a, v = jnp.split(u, 2, axis=-1)
    return (jax.nn.silu(a) * v) @ w_down

def second_inputs(seed: int = 0) -> dict:
    key = jax.random.key(seed)
    keys = jax.random.split(key, 32)
    counter = [0]
    f32 = jnp.float32

    def nxt():
        k = keys[counter[0]]
        counter[0] += 1
        return k

    def dense(shape, fan_in):
        return jax.random.normal(nxt(), shape, f32) * fan_in ** -0.5

    def gain(shape):
        return 1.0 + 0.05 * jax.random.normal(nxt(), shape, f32)

    def small(shape, scale=0.02):
        return scale * jax.random.normal(nxt(), shape, f32)

    L = DEPTH_2
    return {
        "x": jax.random.normal(nxt(), (BATCH, SEQ, D_MODEL), f32),
        "norm1_g": gain((L, D_MODEL)),
        "w_in": dense((L, D_MODEL, N_IN), D_MODEL),
        "cmp_pe_k": small((L, CMP_BLOCK, HEAD_DIM), 0.1),
        "cmp_pe_v": small((L, CMP_BLOCK, HEAD_DIM), 0.1),
        "cmp_k_w1": dense((L, CMP_BLOCK * HEAD_DIM, CMP_HIDDEN), CMP_BLOCK * HEAD_DIM),
        "cmp_k_w2": dense((L, CMP_HIDDEN, HEAD_DIM), CMP_HIDDEN),
        "cmp_v_w1": dense((L, CMP_BLOCK * HEAD_DIM, CMP_HIDDEN), CMP_BLOCK * HEAD_DIM),
        "cmp_v_w2": dense((L, CMP_HIDDEN, HEAD_DIM), CMP_HIDDEN),
        "w_attn_br": dense((L, ATTN_WIDTH, D_MODEL), ATTN_WIDTH),
        "conv_dw_w": dense((L, CONV_WIDTH, CONV_CH), CONV_WIDTH),
        "conv_dw_b": small((L, CONV_CH)),
        "conv_ln_g": gain((L, CONV_CH)),
        "conv_ln_b": small((L, CONV_CH)),
        "w_conv_br": dense((L, CONV_CH, D_MODEL), CONV_CH),
        "w_out": dense((L, D_MODEL, D_MODEL), D_MODEL),
        "norm2_g": gain((L, D_MODEL)),
        "ffn_w_up": dense((L, D_MODEL, 2 * FFN_DIM), D_MODEL),
        "ffn_dw_w": dense((L, FFN_CONV_WIDTH, 2 * FFN_DIM), FFN_CONV_WIDTH),
        "ffn_dw_b": small((L, 2 * FFN_DIM)),
        "ffn_w_down": dense((L, FFN_DIM, D_MODEL), FFN_DIM),
        "final_g": gain((D_MODEL,)),
    }

def second_block(x, norm1_g, w_in, cmp_pe_k, cmp_pe_v, cmp_k_w1, cmp_k_w2, cmp_v_w1, cmp_v_w2,
              w_attn_br, conv_dw_w, conv_dw_b, conv_ln_g, conv_ln_b, w_conv_br, w_out,
              norm2_g, ffn_w_up, ffn_dw_w, ffn_dw_b, ffn_w_down, final_g):
    split_points = list(np.cumsum(IN_SIZES)[:-1])
    for l in range(DEPTH_2):
        h = rms_norm_2(x, norm1_g[l])
        proj = h @ w_in[l]
        (q, k_c, v_c, k_s, v_s, k_w, v_w, g_nsa, u_conv, g_merge) = jnp.split(proj, split_points, axis=-1)
        y_attn = nsa_attention(q, k_c, v_c, k_s, v_s, k_w, v_w, g_nsa, cmp_pe_k[l], cmp_pe_v[l],
                               cmp_k_w1[l], cmp_k_w2[l], cmp_v_w1[l], cmp_v_w2[l]) @ w_attn_br[l]
        y_conv = conformer_conv(u_conv, conv_dw_w[l], conv_dw_b[l], conv_ln_g[l], conv_ln_b[l], w_conv_br[l])
        g_a, g_b = jnp.split(jax.nn.sigmoid(g_merge), 2, axis=-1)
        x = x + (g_a * y_attn + g_b * y_conv) @ w_out[l]
        x = x + conv_ffn(rms_norm_2(x, norm2_g[l]), ffn_w_up[l], ffn_dw_w[l], ffn_dw_b[l], ffn_w_down[l])
    return rms_norm_2(x, final_g)


def setup_inputs(seed=0):
    out = dict(first_inputs(seed))
    for name, value in second_inputs(seed + 1).items():
        if name != "x":
            out[name + "_2"] = value
    return out


def reference(
    x, positions, attn_pre_g, attn_post_g, ffn_pre_g, ffn_post_g, ffn_w_gate, ffn_w_up,
    ffn_w_down, mla_w_a, mla_g_q, mla_w_uq, mla_g_kv, mla_w_ukv, mla_w_o, kv_src_g, w_kv_shared,
    b_w_q, b_rel_table, b_w_o, norm1_g_2, w_in_2, cmp_pe_k_2, cmp_pe_v_2, cmp_k_w1_2,
    cmp_k_w2_2, cmp_v_w1_2, cmp_v_w2_2, w_attn_br_2, conv_dw_w_2, conv_dw_b_2, conv_ln_g_2,
    conv_ln_b_2, w_conv_br_2, w_out_2, norm2_g_2, ffn_w_up_2, ffn_dw_w_2, ffn_dw_b_2,
    ffn_w_down_2, final_g_2,
):
    x = first_block(
        x, positions, attn_pre_g, attn_post_g, ffn_pre_g, ffn_post_g, ffn_w_gate, ffn_w_up,
        ffn_w_down, mla_w_a, mla_g_q, mla_w_uq, mla_g_kv, mla_w_ukv, mla_w_o, kv_src_g,
        w_kv_shared, b_w_q, b_rel_table, b_w_o,
    )
    return second_block(
        x, norm1_g_2, w_in_2, cmp_pe_k_2, cmp_pe_v_2, cmp_k_w1_2, cmp_k_w2_2, cmp_v_w1_2,
        cmp_v_w2_2, w_attn_br_2, conv_dw_w_2, conv_dw_b_2, conv_ln_g_2, conv_ln_b_2,
        w_conv_br_2, w_out_2, norm2_g_2, ffn_w_up_2, ffn_dw_w_2, ffn_dw_b_2, ffn_w_down_2,
        final_g_2,
    )


_drawn_inputs = setup_inputs


def setup_inputs(seed=0):
    import zlib

    import numpy as np

    out = dict(_drawn_inputs(seed))
    spreads = {}
    factors = {'norm1_g_2': 4.783,
     'cmp_pe_k_2': 8.0,
     'cmp_pe_v_2': 7.585,
     'cmp_k_w1_2': 5.377,
     'cmp_k_w2_2': 5.47,
     'conv_dw_b_2': 8.0,
     'conv_ln_g_2': 5.845,
     'conv_ln_b_2': 22.098,
     'norm2_g_2': 2.827,
     'ffn_dw_b_2': 7.447}
    for name, (base, spread) in spreads.items():
        noise = np.random.default_rng([zlib.crc32(name.encode()), seed]).standard_normal(out[name].shape)
        drawn = base * np.exp(spread * noise) if base else spread * noise
        out[name] = __import__('jax').numpy.asarray(drawn.astype(out[name].dtype))
    for name, factor in factors.items():
        out[name] = (out[name] * factor).astype(out[name].dtype)
    return out
```

```python
import numpy as np
import concourse.bass as bass
from concourse import mybir
from concourse.alu_op_type import AluOpType as ALU

F32 = mybir.dt.float32
F32R = mybir.dt.float32r
I32 = mybir.dt.int32
ACT = mybir.ActivationFunctionType
AX = mybir.AxisListType

P = 128
T = 512
D = 1024
KD = D // P
FF = 2816
KF = FF // P
QL, KVL = 384, 256
HEADS_A, NOPE, ROPE = 8, 128, 64
PAIRS_B = 8
PAIRS_C = 4
QT = T // P
EPS = 1e-6
CHUNK = 64
N_CMP, CMP_STRIDE, CMP_BLOCK = 31, 16, 32
CONV_C, TAPS = 512, 31
MAX_REL, REL_TABLE = 256, 320
MASKED = -1.0e30
HUGE = 3.0e38
SLOPES = [2.0 ** -(h + 1) for h in range(8)]


def _block(w, k, cols):
    out = np.zeros((P, P), np.float32)
    at = 0
    for a, b in cols:
        b = min(b, w.shape[1])
        out[:, at:at + b - a] = w[k * P:(k + 1) * P, a:b]
        at += b - a
    return out


def weight_units(w):
    def tile(name, m, ks):
        return [(name, k, [(m * P, (m + 1) * P)]) for k in range(ks)]

    def ffn_units(gate, up, down):
        for j in range(KF):
            yield tile(gate, j, KD)
            yield tile(up, j, KD)
        for half in range(2):
            for kk in range(KF // 2):
                yield [(down, 2 * kk + r, [((4 * half + m) * P, (4 * half + m + 1) * P)])
                       for r in range(2) for m in range(4)]

    def plan():
        for m in range(5):
            yield tile("mla_a", m, KD)
        kr = (QL + KVL, QL + KVL + ROPE)
        yield [("mla_a", k, [kr, kr]) for k in range(KD)]
        for p in range(HEADS_A // 2):
            h0, h1 = 2 * p, 2 * p + 1
            q = lambda h: [("mla_uq", k, [(h * 192, h * 192 + 128)]) for k in range(3)]
            kn = lambda h: [("mla_ukv", k, [(h * 256, h * 256 + 128)]) for k in range(2)]
            v = lambda h: [("mla_ukv", k, [(h * 256 + 128, h * 256 + 256)]) for k in range(2)]
            qr = [("mla_uq", k, [(h * 192 + 128, h * 192 + 192) for h in (h0, h1)]) for k in range(3)]
            yield q(h0) + q(h1)
            yield qr + kn(h0)
            yield kn(h1) + v(h0) + v(h1)
        for m in range(KD):
            yield tile("mla_o", m, KD)
        yield from ffn_units("gate0", "up0", "down0")
        for p in range(PAIRS_B):
            yield tile("kv", KD + p, KD)
            yield tile("kv", p, KD)
            yield tile("b_q", p, KD)
        for m in range(KD):
            yield tile("b_o", m, KD)
        yield from ffn_units("gate1", "up1", "down1")
        c0 = 512 + 6 * 128 + 24
        for c in range(4):
            yield tile_at("w_in", c0 + c * P)
            yield tile_at("w_in", c0 + CONV_C + c * P)
            for j in range(4):
                yield tile_at("w_in", c0 + 2 * CONV_C + (4 * c + j) * P)
        yield [("w_in", k, [(512 + 768, 512 + 768 + 24)]) for k in range(KD)]
        for s in range(6):
            yield tile_at("w_in", 512 + s * P)
        for p in range(PAIRS_C):
            yield tile_at("w_in", p * P)
        for m in range(KD):
            yield tile("attn_br", m, 4) + tile("conv_br", m, 4)
        for m in range(KD):
            yield tile("w_out", m, KD)
        for j in range(KF):
            yield tile("ffn_up", j, KD)
            yield tile("ffn_up", KF + j, KD)
        for half in range(2):
            for kk in range(KF // 2):
                yield [("ffn_down", 2 * kk + r, [((4 * half + m) * P, (4 * half + m + 1) * P)])
                       for r in range(2) for m in range(4)]

    def tile_at(name, c):
        return [(name, k, [(c, c + P)]) for k in range(KD)]

    units = list(plan())
    n = len(units) + len(units) % 2
    if w is None:
        return len(units), n
    stream = np.zeros((n, P, KD * P), np.float32)
    for u, blocks in enumerate(units):
        for i, (name, k, cols) in enumerate(blocks):
            stream[u, :, i * P:(i + 1) * P] = _block(w[name], k, cols)
    return stream


def column_map(items):
    at, where = 0, {}
    for name, n in items:
        where[name] = (at, n)
        at += n
    return where, at


GAINS = [("pre0", 8), ("post0", 8), ("fpre0", 8), ("fpost0", 8), ("gq", 3), ("gkv", 2), ("kvsrc", 8),
         ("pre1", 8), ("post1", 8), ("fpre1", 8), ("fpost1", 8), ("norm1", 8), ("norm2", 8), ("final", 8),
         ("dw", 4 * TAPS), ("dwb", 4), ("lng", 4), ("lnb", 4), ("fdw", 2 * KF * 3), ("fdwb", 2 * KF),
         ("pek", 16), ("pev", 16), ("w2k", P), ("w2v", 64)]
GAIN_AT, N_GAIN = column_map(GAINS)
CONSTS = [("ident", P), ("ones", P), ("cdist", 4 * 32), ("cmask", 4 * 32), ("cvalid", 4 * 32), ("inv", 1),
          ("sgn", 1), ("maskA", T), ("dist", T), ("maskC", T)]
CONST_AT, N_CONST = column_map(CONSTS)


def shape_constants():
    c = np.zeros((P, N_CONST), np.float32)

    def put(name, a):
        at, n = CONST_AT[name]
        c[:, at:at + n] = np.asarray(a, np.float32).reshape(P, n)
    q = np.arange(P)[:, None]
    j = np.arange(T)[None, :]
    put("ident", np.eye(P))
    put("ones", np.ones((P, P)))
    put("maskA", np.where((q < CHUNK) & (j >= T - CHUNK), MASKED, 0.0))
    dist = q + (T - P) - j
    put("dist", dist)
    put("maskC", np.where(dist < 0, MASKED, 0.0))
    end = np.arange(32) * CMP_STRIDE + CMP_BLOCK - 1
    cd = np.stack([q + P * t - end[None, :] for t in range(QT)], 1)
    put("cdist", cd)
    put("cmask", np.where(cd < 0, MASKED, 0.0))
    put("cvalid", cd >= 0)
    half = ROPE // 2
    freq = np.float32(1) / (np.float32(10000) ** (np.arange(0, ROPE, 2, dtype=np.float32) / np.float32(ROPE)))
    put("inv", freq[np.arange(P) % half])
    put("sgn", np.where(np.arange(P) % ROPE < half, -1.0, 1.0))
    return c


class Event:
    def __init__(self, chan, loop, n):
        self.chan, self.loop, self.n = chan, loop, n


class Carried:
    def __init__(self, before):
        self.before, self.last = before, None


class Chan:
    def __init__(self, sem, unit=1, start=0):
        self.sem, self.unit, self.count, self.start = sem, unit, start, start


class Loop:
    def __init__(self, turns, chans):
        self.turns, self.base = turns, {c: c.count for c in chans}
        self.per, self.before = {}, {}


def flat(x):
    if x is None:
        return []
    if isinstance(x, (list, tuple)):
        return [e for y in x for e in flat(y)]
    return [x]


class Queue:
    def __init__(self, engines):
        self.chans = dict(engines)
        self.items = {k: [] for k in engines}
        self.loop = None
        self.free = {}
        self.extra = []

    def all_chans(self):
        return list(self.chans.values()) + self.extra

    def tick(self, chan):
        chan.count += 1
        return Event(chan, self.loop, chan.count)

    def step(self, engine, fn, *waits, chan=None, apart=False):
        chan = chan or self.chans[engine]
        waits = flat(waits)
        if self.loop:
            for w in waits:
                if isinstance(w, Carried):
                    self.loop.before.setdefault(engine, []).extend(flat(w.before))
        ev = self.tick(chan)
        self.items[engine].append((fn, waits, ev, apart))
        return ev

    def start_loop(self, turns):
        chans = self.all_chans()
        self.loop = Loop(turns, chans)
        self.outer = self.items
        self.items = {k: [] for k in self.outer}
        self.carried = {k: Carried(v) for k, v in self.free.items()}
        self.free.update(self.carried)

    def end_loop(self):
        lp = self.loop
        for c in self.all_chans():
            lp.per[c] = c.count - lp.base[c]
            c.count = lp.base[c] + lp.turns * lp.per[c]
        for k, c in self.carried.items():
            if self.free[k] is c:
                self.free[k] = c.before
            else:
                c.last = self.free[k]
        body, self.items, self.loop = self.items, self.outer, None
        for k in body:
            self.items[k].append((lp, body[k]))

    def play(self, engine, e, items=None, loop=None, i=0, seen=None):
        seen = {} if seen is None else seen
        for item in (self.items[engine] if items is None else items):
            if isinstance(item[0], Loop):
                lp, body = item
                self.emit_waits(e, lp.before.get(engine, []), None, 0, seen)
                if body:
                    with e.Fori(0, lp.turns) as turn:
                        self.play(engine, e, body, lp, turn, dict(seen))
                continue
            fn, waits, ev, apart = item
            self.emit_waits(e, waits, loop, i, seen)
            if apart and loop:
                e.sem_inc(self.pads[engine], 1)
            fn(e, i).then_inc(ev.chan.sem, ev.chan.unit)

    def emit_waits(self, e, waits, loop, i, seen):
        fixed, here, back = {}, {}, {}
        for w in waits:
            if isinstance(w, Carried):
                for ev in flat(w.last):
                    if isinstance(ev, Event) and ev.loop is loop:
                        back[ev.chan] = max(back.get(ev.chan, 0), ev.n)
                continue
            if w.loop is not None and w.loop is loop:
                here[w.chan] = max(here.get(w.chan, 0), w.n)
            else:
                n = w.n if w.loop is None else w.n + (w.loop.turns - 1) * w.loop.per[w.chan]
                fixed[w.chan] = max(fixed.get(w.chan, 0), n)
        for c, n in fixed.items():
            if c not in here and seen.get((c, "fixed"), 0) < n:
                seen[c, "fixed"] = n
                e.wait_ge(c.sem, n * c.unit)
        for c, n in back.items():
            if c not in here and (c, "here") not in seen and seen.get((c, "back"), 0) < n:
                seen[c, "back"] = n
                e.wait_ge(c.sem, (i * loop.per[c] + (n - loop.per[c])) * c.unit)
        for c, n in here.items():
            if seen.get((c, "here"), 0) < n:
                seen[c, "here"] = n
                e.wait_ge(c.sem, (i * loop.per[c] + n) * c.unit)


def one(i):
    return bass.ds(i, 1) if not isinstance(i, int) else slice(i, i + 1)


def tile_of(buf, i):
    if isinstance(i, int):
        return buf[:, i, :]
    return buf[:, one(i), :].rearrange("p a t -> p (a t)")


def build(nc, x_in, pos_in, stream, gains_in, consts_in, rel_in, w1_in, out):
    n_used, n_units = weight_units(None)
    KB = 1024
    at = {}

    def sb(name, shape, offset, dt=F32):
        return nc.alloc_sbuf_tensor_at(name, shape, dt, offset=offset)

    base = 16512
    X = base
    HH, HL = X + 16 * KB, X + 32 * KB
    WR = X + 48 * KB
    Y = WR + 24 * KB
    R = Y + 16 * KB
    C = R + 88 * KB
    x = sb("x", [P, KD, T], X)
    hh = sb("hh", [P, KD, T], HH, F32R)
    hl = sb("hl", [P, KD, T], HL, F32R)
    raw = [sb(f"raw{j}", [P, 1024], WR + 4 * KB * j) for j in range(2)]
    whi = [sb(f"whi{j}", [P, 1024], WR + 8 * KB + 4 * KB * j, F32R) for j in range(2)]
    wlo = [sb(f"wlo{j}", [P, 1024], WR + 16 * KB + 4 * KB * j, F32R) for j in range(2)]
    y = sb("y", [P, KD, T], Y)
    fh = sb("fh", [P, KF, T], R, F32R)
    fl = sb("fl", [P, KF, T], R + 44 * KB, F32R)
    oh = sb("oh", [P, KD, T], R, F32R)
    ol = sb("ol", [P, KD, T], R + 16 * KB, F32R)
    R2 = R + 32 * KB
    cqh = sb("cqh", [P, 5, T], R2, F32R)
    cql = sb("cql", [P, 5, T], R2 + 10 * KB, F32R)
    krope = sb("krope", [P, T], R2 + 20 * KB)
    cosT = sb("cosT", [P, T], R2 + 22 * KB)
    sinT = sb("sinT", [P, T], R2 + 24 * KB)
    probsA = [sb(f"probsA{j}", [P, 1280], R2 + 26 * KB + 5 * KB * j) for j in range(2)]
    swapA = sb("swapA", [P, T], R2 + 36 * KB)
    qn = [[sb(f"qn{b}{e}", [P, T], HH + 2 * KB * (2 * b + e)) for e in range(2)] for b in range(2)]
    kn = [[sb(f"kn{b}{e}", [P, T], HH + 8 * KB + 2 * KB * (2 * b + e)) for e in range(2)] for b in range(2)]
    vA = [[sb(f"vA{b}{e}", [P, QT, P], HH + 16 * KB + 2 * KB * (2 * b + e)) for e in range(2)] for b in range(2)]
    qr = [sb(f"qr{b}", [P, T], HH + 24 * KB + 2 * KB * b) for b in range(2)]
    PT = sb("PT", [P, QT, T], Y)
    vtmp = sb("vtmp", [P, T], Y + 8 * KB)
    h2h = sb("h2h", [P, KD, T], R2, F32R)
    h2l = sb("h2l", [P, KD, T], R2 + 16 * KB, F32R)
    R3 = R2 + 32 * KB
    qB = [sb(f"qB{b}", [P, T], R3 + 2 * KB * b) for b in range(2)]
    kB = [sb(f"kB{b}", [P, T], R3 + 4 * KB + 2 * KB * b) for b in range(2)]
    vB = [sb(f"vB{b}", [P, QT, P], R3 + 8 * KB + 2 * KB * b) for b in range(2)]
    probsB = [sb(f"probsB{j}", [P, 1280], R3 + 12 * KB + 5 * KB * j) for j in range(2)]
    biasB = [sb(f"biasB{j}", [P, T], Y + 10 * KB + 2 * KB * j) for j in range(2)]
    gsig = sb("gsig", [P, 16, T], R2)
    kd = [[sb(f"kd{br}{g}", [P, T], R3 + 2 * KB * (2 * br + g)) for g in range(2)] for br in range(2)]
    vC = [sb(f"vC{br}", [P, QT, P], R3 + 8 * KB + 2 * KB * br) for br in range(2)]
    qC = [sb(f"qC{b}", [P, T], R3 + 12 * KB + 2 * KB * b) for b in range(2)]
    R4 = R3 + 16 * KB
    kp = sb("kp", [P, 2, T], R4)
    w1 = sb("w1", [P, 16, P], Y)
    kp2 = sb("kp2", [P, 2, T], R4 + 4 * KB)
    w1v = sb("w1v", [P, 16, P], Y + 8 * KB)
    biasC = sb("biasC", [P, T], Y + 10 * KB)
    probsC = [sb("probsC0", [P, 1280], R4), sb("probsC1", [P, 1280], C + 4 * KB)]
    zpad = [sb(f"zpad{j}", [P, TAPS - 1 + T], (Y, R4)[j]) for j in range(2)]
    zc = sb("zc", [P, 4, T], Y + 4 * KB)
    tmp = [sb(f"tmp{j}", [P, T], C + 2 * KB * j) for j in range(8)]
    rs = [sb(f"rs{j}", [P, T], C + 16 * KB + 2 * KB * j) for j in range(3)]
    C2 = C + 22 * KB
    n_fixed = CONST_AT["maskA"][0]
    cst = sb("cst", [P, n_fixed], C2)
    gn = sb("gn", [P, N_GAIN], C2 + ((n_fixed * 4 + 31) // 32) * 32)
    C3 = C2 + ((n_fixed * 4 + 31) // 32) * 32 + ((N_GAIN * 4 + 31) // 32) * 32
    pos_i = sb("positions", [P, T], Y + 8 * KB, I32)[:, :]
    rope_tmp = [sb(f"rope_tmp{j}", [P, T], Y + 10 * KB + 2 * KB * j) for j in range(3)]
    maskA = sb("maskA", [P, T], R2 + 38 * KB)
    dist = sb("dist", [P, T], Y + 12 * KB)
    maskC = sb("maskC", [P, T], Y + 14 * KB)
    stat = sb("stat", [P, 64], C3)
    gtok = sb("gtok", [P, QT, 24], C3 + 256)
    pC = sb("pC", [P, QT, 64], Y + 8 * KB)
    vcb = [sb(f"vcb{g}", [64, P], Y + 9 * KB + 512 * g) for g in range(2)]
    kcd = sb("kcd", [P, 2, 32], C3 + 640)
    hid = [sb(f"hid{j}", [P, 64], C3 + 896 + 256 * j) for j in range(2)]
    rel = sb("rel", [16, 640], Y)
    end = C3 + 896 + 512
    assert end <= 229344, end
    bias_dram = nc.dram_tensor("bias_scratch", (16, P, T), F32, kind="Internal").ap()
    rel_dram = nc.dram_tensor("rel_scratch", (16, 640), F32, kind="Internal").ap()

    def cc(name, a=0, n=None):
        o, w = CONST_AT[name]
        return cst[:, o + a:o + a + (w if n is None else n)]

    def gg(name, k=0, n=1):
        return gn[:, GAIN_AT[name][0] + k:GAIN_AT[name][0] + k + n]

    def gdyn(name, k):
        if isinstance(k, int):
            return gg(name, k)
        return gn[:, bass.ds(k + GAIN_AT[name][0], 1)]

    ident = cc("ident")
    ones = cc("ones")

    bank = [nc.alloc_psum_tensor(f"bank{j}", [P, T], F32) for j in range(8)]

    sem = lambda n: nc.alloc_semaphore(n)
    START = 4096
    chans = {k: Chan(sem(f"steps_{k}"), 1, START) for k in ("pe", "act", "dve")}
    q = Queue(chans)
    q.pads = {k: sem(f"apart_{k}") for k in chans}
    raw_in = [Chan(sem(f"raw_loaded{j}"), 16) for j in range(2)]
    hi_done = Chan(sem("weight_hi"))
    lo_done = Chan(sem("weight_lo"))
    c_x = [Chan(sem(f"x_loaded{j}"), 16) for j in range(2)]
    c_small = Chan(sem("small_loaded"), 16)
    c_consts = Chan(sem("consts_loaded"), 16)
    c_pos = Chan(sem("positions_loaded"), 16)
    c_rel = Chan(sem("rel_table"), 16)
    c_mask = Chan(sem("masks_loaded"), 16)
    c_bias = [Chan(sem(f"bias_loaded{j}"), 16) for j in range(2)]
    c_w1 = Chan(sem("w1_loaded"), 16)
    c_out = Chan(sem("out_stored"), 16)
    q.extra = raw_in + [c_mask, hi_done, lo_done, c_rel, c_w1, c_out] + c_bias
    free = q.free

    def pe(fn, *w):
        return q.step("pe", fn, *w)

    def act(fn, *w, **k):
        return q.step("act", fn, *w, **k)

    def dve(fn, *w, **k):
        return q.step("dve", fn, *w, **k)

    def func(o, i_, f, *w, scale=1.0, bias=0.0, accum=None):
        def fn(e, i):
            g = lambda a: a(i) if callable(a) else a
            kw = {} if accum is None else {"accum_out": accum}
            return e.activation(g(o), g(i_), f, bias=g(bias), scale=g(scale), **kw)
        return act(fn, *w, apart=callable(o) or callable(i_) or callable(scale) or callable(bias))

    def tt(o, a, b, op, *w):
        g = lambda v, i: v(i) if callable(v) else v
        return dve(lambda e, i: e.tensor_tensor(g(o, i), g(a, i), g(b, i), op), *w)

    def stt(o, a, s, b, op0, op1, *w):
        g = lambda v, i: v(i) if callable(v) else v
        return dve(lambda e, i: e.scalar_tensor_tensor(g(o, i), g(a, i), g(s, i), g(b, i), op0, op1), *w)

    def ts(o, a, s1, s2, op0, op1, *w):
        g = lambda v, i: v(i) if callable(v) else v
        if s2 is None:
            return dve(lambda e, i: e.tensor_scalar(g(o, i), g(a, i), g(s1, i), None, op0), *w)
        return dve(lambda e, i: e.tensor_scalar(g(o, i), g(a, i), g(s1, i), g(s2, i), op0, op1), *w)

    def round_unit(j, used):
        if q.loop is None and hi_done.count == n_units:
            return
        loaded = q.tick(raw_in[j])
        act(lambda e, i: e.activation(whi[j][:, :], raw[j][:, :], ACT.Copy), loaded, used, chan=hi_done)

    unit_no = [0]

    def use_unit(parts):
        j = unit_no[0] % 2
        unit_no[0] += 1
        ready = q.tick(lo_done)
        evs = []
        for bk, terms, first, last, waits in parts:
            def fn(e, i, bk=bk, terms=(), begin=False, end=False):
                g = lambda v: v(i) if callable(v) else v
                o = bank[bk][:, :]
                for n, (blk, h, l) in enumerate(terms):
                    wh = whi[j][:, blk * P:(blk + 1) * P]
                    wl = wlo[j][:, blk * P:(blk + 1) * P]
                    e.matmul(o, wh, g(h), start=begin and n == 0, stop=False)
                    e.matmul(o, wh, g(l), start=False, stop=False)
                    mm = e.matmul(o, wl, g(h), start=False, stop=end and n == len(terms) - 1)
                return mm
            if isinstance(waits, dict):
                for n, term in enumerate(terms):
                    ev = pe(lambda e, i, fn=fn, term=term, n=n, N=len(terms): fn(
                        e, i, terms=(term,), begin=first and n == 0, end=last and n == N - 1), ready, waits[n])
            else:
                ev = pe(lambda e, i, fn=fn, terms=terms, first=first, last=last: fn(
                    e, i, terms=terms, begin=first, end=last), ready, waits)
            evs.append(ev)
        round_unit(j, evs[-1])
        return evs

    def project(bk, hbuf, lbuf, ks, *waits):
        return use_unit([(bk, [(k, hbuf(k), lbuf(k)) for k in range(ks)], True, True,
                          {k: [w, free.get(f"b{bk}")] for k, w in waits[0].items()} if waits and isinstance(waits[0], dict)
                          else list(waits) + [free.get(f"b{bk}")])])[0]

    H = (lambda k: hh[:, k, :]), (lambda k: hl[:, k, :])
    H2 = (lambda k: h2h[:, k, :]), (lambda k: h2l[:, k, :])
    O = (lambda k: oh[:, k, :]), (lambda k: ol[:, k, :])

    sq_turn = [0]

    def add_square(src, bk, first, last, ready, square=True):
        s = sq_turn[0] % 2
        sq_turn[0] += 1
        if square:
            ev = func(tmp[s][:, :], src, ACT.Square, ready, free.get(f"tmp{s}"))
            rhs = tmp[s][:, :]
        else:
            ev, rhs = ready, src
        mm = pe(lambda e, i: e.matmul(bank[bk][:, :], ones, rhs, start=first, stop=last), ev,
                free.get(f"b{bk}") if first else None)
        if square:
            free[f"tmp{s}"] = mm
        return mm

    def inv_rms(dst, bk, n, summed):
        name = f"rs{rs.index(dst)}"
        a = ts(dst[:, :], bank[bk][:, :], 1.0 / n, EPS, ALU.mult, ALU.add, summed, free.get(name))
        free[f"b{bk}"] = a
        b = func(dst[:, :], dst[:, :], ACT.Sqrt, a)
        return dve(lambda e, i: e.reciprocal(dst[:, :], dst[:, :]), b)

    def split(src, hi, lo, ready, gain=None, war=None):
        a = func(hi, src, ACT.Copy, ready, war, scale=1.0 if gain is None else gain)
        if gain is None:
            return tt(lo, src, (lambda i: hi(i).bitcast(F32)) if callable(hi) else hi.bitcast(F32), ALU.subtract, a, war)
        return stt(lo, src, gain, hi.bitcast(F32), ALU.mult, ALU.subtract, a, war)

    EV_mask = q.tick(c_mask)
    EV_small, EV_const, EV_pos = q.tick(c_small), q.tick(c_consts), q.tick(c_pos)
    EV_x = [q.tick(c_x[0]), q.tick(c_x[1])]
    SM = (EV_small, EV_const)
    for j in range(2):
        round_unit(j, None)
    ready_h = {}
    for k in range(KD):
        xe = EV_x[k // 4]
        ready_h[k] = split(x[:, k, :], hh[:, k, :], hl[:, k, :], (xe, SM), gg("pre0", k))
        ssq = add_square(x[:, k, :], 7, k == 0, k == KD - 1, xe)
    rs_main = inv_rms(rs[0], 7, D, ssq)
    free["rs0"] = rs_main

    rel_ev = Event(c_rel, None, 1)
    c_rel.count = 1
    r1 = ts(rel[:, 255:575], rel[:, 255:575], float(CHUNK) ** 0.5, None, ALU.mult, None, rel_ev)
    r2 = dve(lambda e, i: e.tensor_copy(rel[:, 0:255], rel[:, 255:256].to_broadcast([16, 255])), r1)
    r3 = dve(lambda e, i: e.tensor_copy(rel[:, 575:640], rel[:, 574:575].to_broadcast([16, 65])), r1)
    rel_out = q.step("act", lambda e, i: e.dma_start(rel_dram, rel[:, :]), r2, r3, chan=c_rel)
    free["PT"] = rel_out
    free["vtmp"] = None
    shifted = bass.AP(tensor=rel_dram.tensor, offset=P - 1, ap=[[640, 16], [-1, P], [1, T]])
    rel_out = q.step("act", lambda e, i: e.dma_start(bias_dram, shifted), rel_out, chan=c_rel)

    def rope_tables():
        TWO_PI = 2 * np.pi
        c1 = float(np.float32(6.28125))
        c2 = float(np.float32(np.round((TWO_PI - c1) * 2 ** 21) / 2 ** 21))
        c3 = float(np.float32(TWO_PI - c1 - c2))
        MAGIC = 1.5 * 2.0 ** 23
        PI32 = 3.1415925
        ang, kk_, rr = rope_tmp
        e_ = dve(lambda e, i: e.tensor_copy(ang[:, :], pos_i), EV_pos, SM)
        e_ = ts(ang[:, :], ang[:, :], cc("inv"), None, ALU.mult, None, e_)
        for dst, shift in ((sinT, 0.0), (cosT, 0.25)):
            e_ = ts(kk_[:, :], ang[:, :], float(1.0 / TWO_PI), shift, ALU.mult, ALU.add, e_)
            e_ = ts(kk_[:, :], kk_[:, :], MAGIC, None, ALU.add, None, e_)
            e_ = ts(kk_[:, :], kk_[:, :], -MAGIC, None, ALU.add, None, e_)
            e_ = stt(rr[:, :], kk_[:, :], -c1, ang[:, :], ALU.mult, ALU.add, e_)
            e_ = stt(rr[:, :], kk_[:, :], -c2, rr[:, :], ALU.mult, ALU.add, e_)
            e_ = stt(rr[:, :], kk_[:, :], -c3, rr[:, :], ALU.mult, ALU.add, e_)
            if shift:
                e_ = ts(rr[:, :], rr[:, :], float(np.pi / 2), None, ALU.add, None, e_)
            e_ = ts(rr[:, :], rr[:, :], PI32, -PI32, ALU.min, ALU.max, e_)
            e_ = func(dst[:, :], rr[:, :], ACT.Sin, e_)
        e_ = ts(sinT[:, :], sinT[:, :], cc("sgn"), None, ALU.mult, None, e_)
        rope_ready = e_

        return rope_ready

    def rope(src, dst, swap, ready, war):
        evs = []
        for a in range(4):
            b = a ^ 1
            evs.append(func(swap[32 * a:32 * a + 32, :], src[32 * b:32 * b + 32, :], ACT.Copy,
                            ready, free.get("swap")))
        a_ = tt(swap[:, :], swap[:, :], sinT[:, :], ALU.mult, evs, rope_ready)
        b_ = tt(src[:, :], src[:, :], cosT[:, :], ALU.mult, ready, evs)
        c_ = tt(dst[:, :], src[:, :], swap[:, :], ALU.add, a_, b_, war)
        free["swap"] = c_
        return c_

    lat = []
    for m in range(5):
        bk = m % 2
        mm = project(bk, *H, KD, ready_h if m == 0 else None)
        tb = 2 + m % 4
        v = tt(tmp[tb][:, :], bank[bk][:, :], rs[0][:, :], ALU.mult, mm, rs_main, free.get(f"tmp{tb}"))
        free[f"b{bk}"] = v
        g = gg("gq", m) if m < 3 else gg("gkv", m - 3)
        s = split(tmp[tb][:, :], cqh[:, m, :], cql[:, m, :], v, g)
        n = 3 if m < 3 else 2
        sqm = add_square(tmp[tb][:, :], 6 if m < 3 else 7, m in (0, 3), m in (2, 4), v)
        free[f"tmp{tb}"] = (s, sqm)
        lat.append(s)
        if m == 2:
            rs_q = inv_rms(rs[1], 6, QL, sqm)
            rope_ready = rope_tables()
        if m == 4:
            rs_kv = inv_rms(rs[2], 7, KVL, sqm)
    mm = project(1, *H, KD)
    h_read = mm
    v = tt(tmp[6][:, :], bank[1][:, :], rs[0][:, :], ALU.mult, mm, rs_main)
    free["b1"] = v
    kr_ready = rope(tmp[6], krope, swapA, v, None)
    free["tmp6"] = kr_ready

    SPOT = {0: (0, 0), 2: (0, 128), 1: (1, 0), 3: (2, 0)}
    ORDER = (0, 2, 1, 3)
    PO = {0: 0, 1: 128, 2: 384, 3: 768}
    W = lambda t: (t + 1) * P

    def scores(pieces, *ready):
        evs = {}
        for b, tiles in ((0, (0, 2)), (1, (1,)), (2, (3,))):
            def fn(e, i, b=b, tiles=tiles):
                for t in tiles:
                    for n, (qf, kf) in enumerate(pieces):
                        mm = e.matmul(bank[b][:, SPOT[t][1]:SPOT[t][1] + W(t)], qf(t), kf(W(t)),
                                      start=n == 0, stop=n == len(pieces) - 1)
                return mm
            ev = pe(fn, ready, free.get(f"b{b}"))
            for t in tiles:
                evs[t] = ev
        return evs

    def bias_and_min(evs, pb, st, bias, scale, *ready):
        out = {}
        for t in ORDER:
            b, c = SPOT[t]
            out[t] = dve(lambda e, i, t=t, b=b, c=c: e.tensor_tensor_reduce(
                out=pb[:, PO[t]:PO[t] + W(t)], in0=bank[b][:, c:c + W(t)], in1=bias[:, T - W(t):T],
                scale=-scale, scalar=HUGE, op0=ALU.add, op1=ALU.min,
                accum_out=stat[:, st + t:st + t + 1]), evs[t], ready, free.get(pb.name), apart=True)
            free[f"b{b}"] = out[t]
        return out

    def exponent(evs, pb, st):
        out = {}
        for t in ORDER:
            r = pb[:, PO[t]:PO[t] + W(t)]
            out[t] = func(r, r, ACT.Exp, evs[t], free.get(f"sum{st}"), scale=-1.0, bias=stat[:, st + t:st + t + 1],
                          accum=stat[:, st + 4 + t:st + 5 + t])
        return out

    def normalise(evs, pb, st, gate=None, gate_ready=None):
        s = stat[:, st + 4:st + 8]
        r = stat[:, st + 8:st + 12]
        a = dve(lambda e, i: e.reciprocal(r, s), list(evs.values()))
        free[f"sum{st}"] = a
        if gate is not None:
            a = tt(r, r, gate, ALU.mult, a, gate_ready)
        out = {}
        for t in ORDER:
            v = pb[:, PO[t]:PO[t] + W(t)]
            out[t] = ts(v, v, stat[:, st + 8 + t:st + 9 + t], None, ALU.mult, None, a)
        return out

    tr_turn = [0]
    tr_banks = [5, 6]

    def transposes(evs, pb):
        out = []
        for t in ORDER:
            b = tr_banks[tr_turn[0] % len(tr_banks)]
            tr_turn[0] += 1

            def fn(e, i, t=t, b=b):
                for k in range(t + 1):
                    mm = e.transpose(bank[b][:, k * P:(k + 1) * P], pb[:, PO[t] + k * P:PO[t] + (k + 1) * P], ident)
                return mm
            mm = pe(fn, evs[t], free.get(f"b{b}"))
            ev = func(PT[:, 0:t + 1, t * P:(t + 1) * P],
                      bank[b][:, 0:W(t)].rearrange("p (k c) -> p k c", c=P), ACT.Copy, mm, free.get("PT"))
            free[f"b{b}"] = ev
            out.append(ev)
        free[pb.name] = mm
        return out

    def times_v(vf, rows, ready, first=True, last=True, war=None):
        def fn(e, i):
            for k in range(QT):
                mm = e.matmul(bank[7][rows[0]:rows[1], k * P:T], vf(k), PT[:, k, k * P:T],
                              start=first and k == 0, stop=last and k == QT - 1, skip_group_check=not (first and last))
            return mm
        ev = pe(fn, ready, war)
        free["PT"] = ev
        return ev

    def token_major(src, dst, ready, war):
        b = tr_banks[tr_turn[0] % len(tr_banks)]
        tr_turn[0] += 1

        def fn(e, i):
            for t in range(QT):
                mm = e.transpose(bank[b][:, t * P:(t + 1) * P], src[:, t * P:(t + 1) * P], ident)
            return mm
        mm = pe(fn, ready, free.get(f"b{b}"))
        ev = func(dst[:, :, :], bank[b][:, :].rearrange("p (k c) -> p k c", c=P), ACT.Copy, mm, war)
        free[f"b{b}"] = ev
        return mm, ev

    def scaled(bk, r, dst, mm, rready, war):
        ev = tt(dst, bank[bk][:, :], r[:, :], ALU.mult, mm, rready, war)
        free[f"b{bk}"] = ev
        return ev

    CQ = lambda k: cqh[:, k, :]
    CL = lambda k: cql[:, k, :]

    def mla_unit(which, p):
        b = p % 2
        ev = {}

        def part(bk, blk, c0, n):
            return (bk, [(blk + k, CQ(c0 + k), CL(c0 + k)) for k in range(n)], True, True,
                    [free.get(f"b{bk}"), lat])
        war = free.get(f"pair{b}")
        if which == 0:
            m0, m1 = use_unit([part(3, 0, 0, 3), part(4, 3, 0, 3)])
            ev["qn0"] = scaled(3, rs[1], qn[b][0][:, :], m0, rs_q, (war, h_read))
            ev["qn1"] = scaled(4, rs[1], qn[b][1][:, :], m1, rs_q, war)
        elif which == 1:
            m0, m1 = use_unit([part(3, 0, 0, 3), part(4, 3, 3, 2)])
            a = scaled(3, rs[1], tmp[6][:, :], m0, rs_q, free.get("tmp6"))
            ev["kn0"] = scaled(4, rs[2], kn[b][0][:, :], m1, rs_kv, war)
            ev["qr"] = rope(tmp[6], qr[b], swapA, a, war)
            free["tmp6"] = ev["qr"]
        else:
            mla_last_unit(b, war, ev)
        return ev

    def mla_last_unit(b, war, ev):
        j = unit_no[0] % 2
        unit_no[0] += 1
        ready = q.tick(lo_done)

        def grp(bk, blk):
            def fn(e, i):
                for n in range(2):
                    wh, wl = (w_[j][:, (blk + n) * P:(blk + n + 1) * P] for w_ in (whi, wlo))
                    o = bank[bk][:, :]
                    e.matmul(o, wh, CQ(3 + n), start=n == 0, stop=False)
                    e.matmul(o, wh, CL(3 + n), start=False, stop=False)
                    mm = e.matmul(o, wl, CQ(3 + n), start=False, stop=n == 1)
                return mm
            return fn
        m0 = pe(grp(3, 0), ready, free.get("b3"), lat)
        m1 = pe(grp(4, 2), ready, free.get("b4"))
        ev["kn1"] = scaled(3, rs[2], kn[b][1][:, :], m0, rs_kv, war)
        m2 = pe(grp(3, 4), free.get("b3"))
        round_unit(j, m2)
        v0 = scaled(4, rs[2], vtmp[:, :], m1, rs_kv, free.get("vtmp"))
        t0, ev["v0"] = token_major(vtmp, vA[b][0], v0, war)
        v1 = scaled(3, rs[2], tmp[7][:, :], m2, rs_kv, free.get("tmp7"))
        free["vtmp"] = t0
        t1, ev["v1"] = token_major(tmp[7], vA[b][1], v1, war)
        free["tmp7"] = t1

    SCALE_A = float(NOPE + ROPE) ** -0.5
    nxt = {}
    for w_ in range(3):
        nxt.update(mla_unit(w_, 0))
    def mla_pair(p, cur):
        b, nxt = p % 2, {}

        def head_scores(e_):
            rows = slice(64 * e_, 64 * e_ + 64)
            return scores([(lambda t: qn[b][e_][:, t * P:(t + 1) * P], lambda w: kn[b][e_][:, 0:w]),
                           (lambda t: qr[b][rows, t * P:(t + 1) * P], lambda w: krope[rows, 0:w])],
                          cur[f"qn{e_}"], cur[f"kn{e_}"], cur["qr"], kr_ready)
        more = p + 1 < HEADS_A // 2
        s0 = head_scores(0)
        a0 = exponent(bias_and_min(s0, probsA[0], 0, maskA, SCALE_A, EV_mask), probsA[0], 0)
        if more:
            nxt.update(mla_unit(0, p + 1))
        n0 = normalise(a0, probsA[0], 0)
        s1 = head_scores(1)
        a1 = exponent(bias_and_min(s1, probsA[1], 16, maskA, SCALE_A, EV_mask), probsA[1], 16)
        t0 = transposes(n0, probsA[0])
        if more:
            nxt.update(mla_unit(1, p + 1))
        v0 = times_v(lambda k: vA[b][0][:, k, :], (0, P), (t0, cur["v0"]), war=free.get("b7"))
        o0 = split(bank[7][:, :], oh[:, 2 * p, :], ol[:, 2 * p, :], v0)
        free["b7"] = o0
        n1 = normalise(a1, probsA[1], 16)
        t1 = transposes(n1, probsA[1])
        if more:
            nxt.update(mla_unit(2, p + 1))
        v1 = times_v(lambda k: vA[b][1][:, k, :], (0, P), (t1, cur["v1"]), war=free.get("b7"))
        o1 = split(bank[7][:, :], oh[:, 2 * p + 1, :], ol[:, 2 * p + 1, :], v1)
        free["b7"] = o1
        free[f"pair{b}"] = v1
        return nxt, (o0, o1), v1

    for p in range(HEADS_A // 2):
        nxt, attn_done, mixer_read = mla_pair(p, nxt)

    def gather_square(src, first, ready):
        if first:
            ev = func(tmp[7][:, :], src, ACT.Square, ready, free.get("tmp7"))
        else:
            sl = sq_turn[0] % 2
            sq_turn[0] += 1
            a = func(tmp[sl][:, :], src, ACT.Square, ready, free.get(f"tmp{sl}"))
            ev = tt(tmp[7][:, :], tmp[7][:, :], tmp[sl][:, :], ALU.add, a, free["total"])
            free[f"tmp{sl}"] = ev
        free["total"] = ev
        return ev

    def sum_total(bk, first, last):
        mm = pe(lambda e, i: e.matmul(bank[bk][:, :], ones, tmp[7][:, :], start=first, stop=last),
                free["total"], free.get(f"b{bk}") if first else None)
        free["tmp7"] = mm
        return mm

    def out_tiles(inp, ks, in_ready, y_war):
        evs = []
        for m in range(KD):
            bk = m % 2
            mm = project(bk, *inp, ks, in_ready if m == 0 else None)
            ev = dve(lambda e, i, m=m, bk=bk: e.tensor_copy(y[:, m, :], bank[bk][:, :]), mm, y_war)
            free[f"b{bk}"] = ev
            gather_square(y[:, m, :], m == 0, ev)
            evs.append(ev)
        return evs, sum_total(7, True, True)

    def join(evs, ssq, post, nexts, bk=7):
        r = inv_rms(rs[1], bk, D, ssq)
        ready, more = {}, []
        for k in range(KD):
            tb = 2 + k % 4
            a = tt(tmp[tb][:, :], y[:, k, :], rs[1][:, :], ALU.mult, r, evs[k], free.get(f"tmp{tb}"))
            b_ = stt(x[:, k, :], tmp[tb][:, :], gg(post, k), x[:, k, :], ALU.mult, ALU.add, a)
            free[f"tmp{tb}"] = b_
            g, hi, lo, war = nexts[0]
            ready[k] = [split(x[:, k, :], hi[:, k, :], lo[:, k, :], b_, gg(g, k), war)]
            ssq2 = add_square(x[:, k, :], 6, k == 0, k == KD - 1, b_)
        free["rs1"] = b_
        inv = inv_rms(rs[0], 6, D, ssq2)
        for g, hi, lo, war in nexts[1:]:
            more += [split(x[:, k, :], hi[:, k, :], lo[:, k, :], b_, gg(g, k), war) for k in range(KD)]
        return ready, inv, more

    def gate_up(idx, bks, ready, inv, conv):
        evs = []
        for r in range(2):
            mm = project(bks[r], *H, KD, ready if r == 0 else None)
            u, acc = tmp[2 + r], tmp[4 + r]
            ev = tt(u[:, :], bank[bks[r]][:, :], rs[0][:, :], ALU.mult, mm, inv, free.get(f"tmp{2 + r}"))
            free[f"b{bks[r]}"] = ev
            if conv:
                w3 = lambda i, tap, r=r: gdyn("fdw", idx(i) * 3 + (r * 3 * KF + tap))
                a = func(acc[:, :], u[:, :], ACT.Identity, ev, free.get(f"tmp{4 + r}"), scale=lambda i, w3=w3: w3(i, 2),
                         bias=lambda i, r=r: gdyn("fdwb", idx(i) + r * KF))
                b_ = stt(acc[:, 1:T], u[:, 0:T - 1], lambda i, w3=w3: w3(i, 1), acc[:, 1:T], ALU.mult, ALU.add, a)
                ev = stt(acc[:, 2:T], u[:, 0:T - 2], lambda i, w3=w3: w3(i, 0), acc[:, 2:T], ALU.mult, ALU.add, b_)
                free[f"tmp{2 + r}"] = ev
            evs.append(ev)
        g_, u_ = (tmp[4], tmp[5]) if conv else (tmp[2], tmp[3])
        sil = func(g_[:, :], g_[:, :], ACT.Silu, evs[0])
        prod = tt(u_[:, :], u_[:, :], g_[:, :], ALU.mult, sil, evs[1])
        hi = dve(lambda e, i: e.tensor_scalar(tile_of(fh, idx(i)), u_[:, :], 1.0, None, ALU.mult), prod)
        lo = tt(lambda i: tile_of(fl, idx(i)), u_[:, :], lambda i: tile_of(fh, idx(i)).bitcast(F32), ALU.subtract, hi)
        n1, n2 = ("tmp4", "tmp5") if conv else ("tmp2", "tmp3")
        free[n1], free[n2] = prod, lo
        return lo

    def feed_forward(ready, inv, conv):
        gate_up(lambda i: 0, (2, 3), ready, inv, conv)
        q.start_loop(KF - 1)
        hid_ready = gate_up(lambda i: i + 1, (0, 1), None, inv, conv)
        q.end_loop()
        evs = []

        def down_unit(half, base, first, last):
            parts = []
            for r in range(2):
                for m in range(4):
                    bk = 4 * half + m
                    h_ = lambda i, r=r: tile_of(fh, base(i) + r)
                    l_ = lambda i, r=r: tile_of(fl, base(i) + r)
                    parts.append((bk, [(4 * r + m, h_, l_)], first and r == 0, last and r == 1,
                                  [hid_ready] + ([free.get(f"b{bk}")] if first and r == 0 else [])))
            return use_unit(parts)

        for half in range(2):
            down_unit(half, lambda i: 0, True, False)
            if half:
                sum_total(0, True, False)
            q.start_loop(KF // 4 - 1)
            down_unit(half, lambda i: i * 4 + 2, False, False)
            down_unit(half, lambda i: i * 4 + 4, False, False)
            q.end_loop()
            down_unit(half, lambda i: KF - 4, False, False)
            ms = down_unit(half, lambda i: KF - 2, False, True)[4:]
            for m in range(4):
                mi = 4 * half + m
                ev = dve(lambda e, i, mi=mi: e.tensor_copy(y[:, mi, :], bank[mi][:, :]), ms[m])
                free[f"b{mi}"] = ev
                evs.append(ev)
                if half:
                    ssq = add_square(y[:, mi, :], 0, False, m == 3, ev)
                else:
                    gather_square(y[:, mi, :], m == 0, ev)
        return evs, ssq

    evs, ssq = out_tiles(O, KD, [attn_done, mixer_read], mixer_read)
    ready, inv, _ = join(evs, ssq, "post0", [("fpre0", hh, hl, None)])
    evs, ssq = feed_forward(ready, inv, False)
    ready, inv, ready2 = join(evs, ssq, "fpost0", [("kvsrc", hh, hl, None), ("pre1", h2h, h2l, evs[-1])], 0)

    def load_bias(e_, idx):
        def fn(e, i):
            return e.dma_start(biasB[e_][:, :], bias_dram[one(idx(i)), :, :].rearrange("a p t -> p (a t)"))
        return q.step("act", fn, free.get(f"biasB{e_}"), rel_out, chan=c_bias[e_])

    def add_mask(e_, loaded):
        return ts(biasB[e_][0:CHUNK, T - CHUNK:T], biasB[e_][0:CHUNK, T - CHUNK:T], 0.0, MASKED, ALU.mult, ALU.add, loaded)

    def b_unit(which, b, first_ready=None):
        war = free.get(f"pair{b}")
        ev = {}
        if which == 0:
            mm = project(3, *H, KD, first_ready)
            v_ = scaled(3, rs[0], vtmp[:, :], mm, inv, free.get("vtmp"))
            t_, ev["v"] = token_major(vtmp, vB[b], v_, war)
            free["vtmp"] = t_
        elif which == 1:
            mm = project(3, *H, KD)
            ev["k"] = scaled(3, rs[0], kB[b][:, :], mm, inv, war)
        else:
            mm = project(3, *H2, KD, ready2)
            ev["q"] = scaled(3, rs[0], qB[b][:, :], mm, inv, war)
        return ev

    SCALE_B = 64.0 ** -0.5

    def b_pair(b, pidx, cur, more):
        nx = {}
        bias_ev = [add_mask(e_, load_bias(e_, lambda i, e_=e_: pidx(i) * 2 + e_)) for e_ in range(2)]

        def head_scores(e_):
            r = slice(64 * e_, 64 * e_ + 64)
            return scores([(lambda t: qB[b][r, t * P:(t + 1) * P], lambda w: kB[b][r, 0:w])], cur["q"], cur["k"])
        s0 = head_scores(0)
        m0 = bias_and_min(s0, probsB[0], 0, biasB[0], SCALE_B, bias_ev[0])
        free["biasB0"] = m0[ORDER[-1]]
        a0 = exponent(m0, probsB[0], 0)
        if more:
            nx.update(b_unit(0, 1 - b))
        n0 = normalise(a0, probsB[0], 0)
        s1 = head_scores(1)
        m1 = bias_and_min(s1, probsB[1], 16, biasB[1], SCALE_B, bias_ev[1])
        free["biasB1"] = m1[ORDER[-1]]
        a1 = exponent(m1, probsB[1], 16)
        t0 = transposes(n0, probsB[0])
        if more:
            nx.update(b_unit(1, 1 - b))
        v0 = times_v(lambda k: vB[b][:, k, 0:64], (0, 64), (t0, cur["v"]), war=free.get("b7"))
        n1 = normalise(a1, probsB[1], 16)
        t1 = transposes(n1, probsB[1])
        if more:
            nx.update(b_unit(2, 1 - b))
        v1 = times_v(lambda k: vB[b][:, k, 64:128], (64, 128), t1)
        free[f"pair{b}"] = v1
        hi = dve(lambda e, i: e.tensor_scalar(tile_of(oh, pidx(i)), bank[7][:, :], 1.0, None, ALU.mult), v1)
        lo = tt(lambda i: tile_of(ol, pidx(i)), bank[7][:, :], lambda i: tile_of(oh, pidx(i)).bitcast(F32),
                ALU.subtract, hi)
        free["b7"] = lo
        return nx, lo

    tr_banks.insert(0, 4)
    cur = {}
    for w_ in range(3):
        cur.update(b_unit(w_, 0, ready))
    for k_ in ("pair0", "pair1"):
        free[k_] = None
    for k_, ev in cur.items():
        free["B_" + k_] = ev
    q.start_loop(PAIRS_B // 2 - 1)
    cur = {k_: free["B_" + k_] for k_ in ("q", "k", "v")}
    nx, _ = b_pair(0, lambda i: i * 2, cur, True)
    nx2, _ = b_pair(1, lambda i: i * 2 + 1, nx, True)
    for k_ in ("q", "k", "v"):
        free["B_" + k_] = nx2[k_]
    q.end_loop()
    cur = {k_: free["B_" + k_] for k_ in ("q", "k", "v")}
    nx, _ = b_pair(0, lambda i: PAIRS_B - 2, cur, True)
    _, o_done = b_pair(1, lambda i: PAIRS_B - 1, nx, False)

    tr_banks.remove(4)
    evs, ssq = out_tiles(O, KD, [o_done], free["pair1"])
    ready, inv, _ = join(evs, ssq, "post1", [("fpre1", hh, hl, free["pair1"])])
    evs, ssq = feed_forward(ready, inv, False)
    ready, inv, _ = join(evs, ssq, "fpost1", [("norm1", hh, hl, None)], 0)
    flat_ready = flat(list(ready.values()))

    zero_ev = [dve(lambda e, i, j=j: e.memset(zpad[j][:, 0:TAPS - 1], 0.0), evs, ssq) for j in range(2)]
    GS = [(j, (3, 4, 5, 6)[j]) for j in range(4)]
    q.start_loop(2)
    for half in range(2):
        cidx = lambda i, half=half: i * 2 + half
        zp = zpad[half]
        mm = project(0, *H, KD, flat_ready)
        a = tt(tmp[2][:, :], bank[0][:, :], rs[0][:, :], ALU.mult, mm, inv, free.get("tmp2"))
        free["b0"] = a
        mm = project(1, *H, KD)
        g = tt(tmp[3][:, :], bank[1][:, :], rs[0][:, :], ALU.mult, mm, free.get("tmp3"))
        free["b1"] = g
        s = func(tmp[3][:, :], tmp[3][:, :], ACT.Sigmoid, g)
        z = tt(zp[:, TAPS - 1:TAPS - 1 + T], tmp[2][:, :], tmp[3][:, :], ALU.mult, a, s, zero_ev, free.get(f"zpad{half}"))
        free["tmp2"] = free["tmp3"] = z
        taps = list(range(TAPS))
        wt = lambda i, tap, cidx=cidx: gdyn("dw", cidx(i) * TAPS + tap)
        o = lambda i, cidx=cidx: tile_of(zc, cidx(i))
        ev = ts(tmp[4][:, :], zp[:, 0:T], lambda i, wt=wt: wt(i, 0), lambda i, cidx=cidx: gdyn("dwb", cidx(i)),
                ALU.mult, ALU.add, z, free.get("tmp4"))
        done = 1
        for j in range(4):
            mm = project(2 + j % 2, *H, KD)
            gi = lambda i, cidx=cidx, j=j: tile_of(gsig, cidx(i) * 4 + j)
            b_ = tt(gi, bank[2 + j % 2][:, :], rs[0][:, :], ALU.mult, mm)
            free[f"b{2 + j % 2}"] = b_
            free["gsig"] = func(tmp[6][:, :], gi, ACT.Sigmoid, b_, free.get("tmp6"))
            free["tmp6"] = ts(gi, tmp[6][:, :], 1.0, None, ALU.mult, None, free["gsig"])
            n = 8 if j < 3 else TAPS - done
            for _ in range(n):
                if done == TAPS:
                    break
                last_tap = done == TAPS - 1
                dst = o if last_tap else tmp[4][:, :]
                ev = stt(dst, zp[:, done:done + T], lambda i, wt=wt, done=done: wt(i, done), tmp[4][:, :],
                         ALU.mult, ALU.add, ev)
                done += 1
        free["tmp4"] = ev
        free[f"zpad{half}"] = ev
    q.end_loop()
    conv_done, gates_done = ev, free["tmp6"]

    mm = project(0, *H, KD)
    g = scaled(0, rs[0], tmp[5][:, :], mm, inv, free.get("tmp5"))

    def tr4(e, i):
        for t in range(QT):
            mm_ = e.transpose(bank[5][:, t * P:(t + 1) * P], tmp[5][:, t * P:(t + 1) * P], ident)
        return mm_
    mm = pe(tr4, g, free.get("b5"))
    free["tmp5"] = mm
    gt_ready = func(gtok[:, :, :], bank[5][:, :].rearrange("p (k c) -> p k c", c=P)[:, :, 0:24], ACT.Sigmoid, mm)
    free["b5"] = gt_ready

    for c in range(4):
        su = add_square(zc[:, c, :], 7, c == 0, c == 3, conv_done, square=False)
    mu = ts(rs[1][:, :], bank[7][:, :], -1.0 / CONV_C, None, ALU.mult, None, su, free.get("rs1"))
    free["b7"] = mu
    for c in range(4):
        ce = tt(zc[:, c, :], zc[:, c, :], rs[1][:, :], ALU.add, mu)
        s2 = add_square(zc[:, c, :], 7, c == 0, c == 3, ce)
    free["rs2"] = free.get("rs2")
    ln = inv_rms(rs[2], 7, CONV_C, s2)
    for c in range(4):
        tb = 2 + c % 2
        a = tt(zc[:, c, :], zc[:, c, :], rs[2][:, :], ALU.mult, ln, s2)
        b_ = func(tmp[tb][:, :], zc[:, c, :], ACT.Silu, a, free.get(f"tmp{tb}"), scale=gg("lng", c), bias=gg("lnb", c))
        z_done = split(tmp[tb][:, :], oh[:, 4 + c, :], ol[:, 4 + c, :], b_)
        free[f"tmp{tb}"] = z_done

    load_w1 = [q.step("act", lambda e, i, j=j: e.dma_start((w1, w1v)[j][:, :, :], w1_in[j]), a, conv_done, b_, chan=c_w1)
               for j in range(1)]
    w1_ready = load_w1[0]
    load2 = q.step("act", lambda e, i: e.dma_start(w1v[:, :, :], w1_in[1]), w1_ready, chan=c_w1)
    w1_both = (w1_ready, load2)
    kps = (kp, kp2)
    kp_ready = []
    for s_ in range(2):
        mm = project(s_, *H, KD)
        tb = 4 + s_
        v_ = scaled(s_, rs[0], tmp[tb][:, :], mm, inv, free.get(f"tmp{tb}"))
        evs_ = []
        for g_ in range(2):
            r = slice(64 * g_, 64 * g_ + 64)
            evs_.append(func(kps[s_][0:64, g_, :], tmp[tb][r, :], ACT.Copy, v_, conv_done, z_done))
            evs_.append(func(kps[s_][64:128, g_, 0:T - 1], tmp[tb][r, 1:T], ACT.Copy, v_, conv_done))
        free[f"tmp{tb}"] = evs_
        kp_ready.append(evs_)
    kd_ready, vc_ready = [], []
    for br in range(2):
        mm = project(0, *H, KD)
        a = tt(kd[br][0][0:64, :], bank[0][0:64, :], rs[0][0:64, :], ALU.mult, mm, gates_done)
        b_ = tt(kd[br][1][64:128, :], bank[0][64:128, :], rs[0][64:128, :], ALU.mult, mm)
        free["b0"] = b_
        c_ = func(kd[br][0][64:128, :], kd[br][0][0:64, :], ACT.Copy, a)
        d_ = func(kd[br][1][0:64, :], kd[br][1][64:128, :], ACT.Copy, b_)
        kd_ready.append((a, b_, c_, d_))
        mm = project(1, *H, KD)
        v_ = scaled(1, rs[0], tmp[6][:, :], mm, inv, free.get("tmp6"))
        t_, e2 = token_major(tmp[6], vC[br], v_, None)
        free["tmp6"] = t_
        vc_ready.append(e2)

    hid_ready = []
    for s_ in range(2):
        ww, pe_name = ((w1, "pek"), (w1v, "pev"))[s_]

        def cmp_mm(e, i, s_=s_, ww=ww):
            for n in range(16):
                rhs = kps[s_][:, :, 2 * n:2 * n + CMP_STRIDE * (N_CMP - 1) + 1:CMP_STRIDE]
                o = bank[2][:, 0:2 * N_CMP].rearrange("p (g n) -> p g n", g=2)
                e.matmul(o, ww[:, n, :], rhs, start=n == 0, stop=n == 15)
            for n in range(16):
                mm_ = e.matmul(bank[2][:, 64:65], ww[:, n, :], gg((("pek"), ("pev"))[s_], n), start=n == 0, stop=n == 15)
            return mm_
        mm = pe(cmp_mm, kp_ready[s_], w1_both, free.get("b2"))
        pb_ = dve(lambda e, i, s_=s_: e.tensor_copy(stat[:, 60 + s_:61 + s_], bank[2][:, 64:65]), mm)
        hd = func(hid[s_][:, 0:2 * N_CMP], bank[2][:, 0:2 * N_CMP], ACT.Gelu_apprx_tanh, pb_, bias=stat[:, 60 + s_:61 + s_])
        free["b2"] = hd
        hid_ready.append(hd)
    cmp_read = mm
    dist_ready = [q.step("act", lambda e, i, buf=buf, name=name: e.dma_start(
        buf[:, :], consts_in[:, CONST_AT[name][0]:CONST_AT[name][0] + T]), cmp_read, chan=ch)
        for buf, name, ch in ((dist, "dist", c_mask), (maskC, "maskC", c_w1))]
    z0 = dve(lambda e, i: e.memset(vcb[0][:, :], 0.0), cmp_read)
    z1 = dve(lambda e, i: e.memset(vcb[1][:, :], 0.0), cmp_read)
    z2 = dve(lambda e, i: e.memset(pC[:, :, :], 0.0), cmp_read)
    mm = pe(lambda e, i: e.matmul(bank[2][:, 0:2 * N_CMP], gg("w2k", 0, P), hid[0][:, 0:2 * N_CMP], start=True, stop=True),
            hid_ready[0], free["b2"])
    kc_ready = dve(lambda e, i: e.tensor_copy(kcd[:, :, 0:N_CMP], bank[2][:, 0:2 * N_CMP].rearrange("p (g n) -> p g n", g=2)), mm)
    free["b2"] = kc_ready

    def vc_mm(e, i):
        for g_ in range(2):
            for e_ in range(2):
                mm_ = e.matmul(bank[2][32 * e_:32 * e_ + N_CMP, 64 * g_:64 * g_ + 64],
                               hid[1][:, g_ * N_CMP:(g_ + 1) * N_CMP], gg("w2v", 0, 64), start=True, stop=True)
        return mm_
    mm = pe(vc_mm, hid_ready[1], free["b2"])
    vcb_ready = []
    for g_ in range(2):
        for e_ in range(2):
            vcb_ready.append(dve(lambda e, i, g_=g_, e_=e_: e.tensor_copy(
                vcb[g_][32 * e_:32 * e_ + N_CMP, 64 * e_:64 * e_ + 64],
                bank[2][32 * e_:32 * e_ + N_CMP, 64 * g_:64 * g_ + 64]), mm, z0, z1))
    free["b2"] = vcb_ready

    def c_unit(p):
        mm_ = project(3 + p % 2, *H, KD)
        return scaled(3 + p % 2, rs[0], qC[p % 2][:, :], mm_, inv, free.get(f"pair{p % 2}"))

    free["pair0"] = free["pair1"] = None
    free["PT"] = cmp_read
    free["probsC0"] = cmp_read
    free["vtmp"] = None
    q_ready = c_unit(0)
    bc = tmp[7]
    def c_pair(p, q_ready):
        b, g_ = p % 2, p // 2
        bcv = bc[:, 0:QT * 64].rearrange("p (t e n) -> p t e n", t=QT, e=2)
        cd = cc("cdist").rearrange("p (t n) -> p t n", t=QT)
        cm = cc("cmask").rearrange("p (t n) -> p t n", t=QT)
        bce = [stt(bcv[:, :, e_, :], cd, -SLOPES[2 * p + e_], cm, ALU.mult, ALU.add, SM, free.get("tmp7")) for e_ in range(2)]

        def c_scores(e, i, b=b, g_=g_):
            for t in range(QT):
                for e_ in range(2):
                    r = slice(64 * e_, 64 * e_ + 64)
                    mm_ = e.matmul(bank[3 + e_][:, t * 32:t * 32 + N_CMP],
                                   qC[b][r, t * P:(t + 1) * P], kcd[r, g_, 0:N_CMP], start=True, stop=True)
            return mm_
        mm = pe(c_scores, q_ready, kc_ready, free.get("b3"), free.get("b4"))
        pv = pC[:, :, :].rearrange("p t (e n) -> p (t e) n", n=32)[:, :, 0:N_CMP]
        st8, sm8 = stat[:, 32:40], stat[:, 40:48]
        a = []
        for e_ in range(2):
            sv = bank[3 + e_][:, 0:QT * 32].rearrange("p (t n) -> p t n", n=32)[:, :, 0:N_CMP]
            a.append(stt(pC[:, :, 32 * e_:32 * e_ + N_CMP], sv, 0.125, bcv[:, :, e_, 0:N_CMP], ALU.mult, ALU.add,
                         mm, bce, z2, free.get("pC")))
            free[f"b{3 + e_}"] = a[e_]
        free["tmp7"] = a
        m_ = dve(lambda e, i: e.tensor_reduce(st8, pv, AX.X, ALU.max), a)
        s_ = tt(pv, pv, st8.unsqueeze(2).to_broadcast([P, 8, N_CMP]), ALU.subtract, m_)
        x_ = func(pv, pv, ACT.Exp, s_)
        m_ = dve(lambda e, i: e.tensor_reduce(sm8, pv, AX.X, ALU.add), x_)
        r_ = dve(lambda e, i: e.reciprocal(sm8, sm8), m_)
        gate_c = gtok[:, :, 6 * p:6 * p + 6].rearrange("p t (e b) -> p t e b", b=3)[:, :, :, 0]
        r_ = tt(sm8.rearrange("p (t e) -> p t e", e=2), sm8.rearrange("p (t e) -> p t e", e=2), gate_c, ALU.mult, r_, gt_ready)
        valid = cc("cvalid").rearrange("p (t n) -> p t n", t=QT)[:, :, 0:N_CMP]
        v_ = [tt(pC[:, :, 32 * e_:32 * e_ + N_CMP], pC[:, :, 32 * e_:32 * e_ + N_CMP], valid, ALU.mult, r_)
              for e_ in range(2)]
        pc_ready = tt(pv, pv, sm8.unsqueeze(2).to_broadcast([P, 8, N_CMP]), ALU.mult, v_)

        def c_tr(e, i):
            for t in range(QT):
                mm_ = e.transpose(bank[5][0:64, t * P:(t + 1) * P], pC[:, t, :], ident)
            return mm_

        seq = [(e_, br) for e_ in range(2) for br in range(2)]
        bias_ready = {}
        pend = []
        c_pt = None
        nq = None
        for n, (e_, br) in enumerate(seq):
            h = 2 * p + e_
            if br == 0:
                bias_ready[e_] = stt(biasC[:, :], dist[:, :], -8.0 * SLOPES[h], maskC[:, :], ALU.mult, ALU.add,
                                     dist_ready, free.get("biasC"), cmp_read)
            r = slice(64 * e_, 64 * e_ + 64)
            s_ = scores([(lambda t, r=r: qC[b][r, t * P:(t + 1) * P], lambda w, r=r, br=br: kd[br][g_][r, 0:w])],
                        q_ready, kd_ready)
            pb = probsC[n % 2]
            m_ = bias_and_min(s_, pb, 16 * (n % 2), biasC, SCALE_B, bias_ready[e_])
            free["biasC"] = m_[ORDER[-1]]
            a_ = exponent(m_, pb, 16 * (n % 2))
            gate = gtok[:, :, 3 * h + 1 + br:3 * h + 2 + br].rearrange("p t a -> p (t a)")
            if n == 0:
                mm = pe(c_tr, pc_ready, free.get("b5"))
                free["pC"] = mm
                c_pt = func(tmp[6][0:64, :], bank[5][0:64, :], ACT.Copy, mm, free.get("tmp6"))
                free["b5"] = c_pt
                tr_turn[0] = 1
                o_c = pe(lambda e, i: e.matmul(bank[7][:, :], vcb[g_][:, :], tmp[6][0:64, :], start=True, stop=False, skip_group_check=True),
                         c_pt, vcb_ready, free.get("b7"))
                free["tmp6"] = o_c
                if p + 1 < PAIRS_C:
                    nq = c_unit(p + 1)
            pend.append((a_, pb, 16 * (n % 2), gate, e_, br, n))
            if len(pend) == 2 or n == 3:
                todo = pend if n == 3 else [pend.pop(0)]
                for a2, pb2, st2, gate2, e2_, br2, n2 in todo:
                    nn = normalise(a2, pb2, st2, gate2, gt_ready)
                    tr = transposes(nn, pb2)
                    ov = times_v(lambda k, br2=br2: vC[br2][:, k, 64 * g_:64 * g_ + 64],
                                 (64 * e2_, 64 * e2_ + 64), (tr, vc_ready), first=False, last=n2 == 3)
        free[f"pair{b}"] = ov
        o_done = split(bank[7][:, :], oh[:, p, :], ol[:, p, :], ov)
        free["b7"] = o_done
        return nq, o_done

    for p in range(PAIRS_C):
        q_read, (q_ready, o_done) = q_ready, c_pair(p, q_ready)

    h_read2 = q_read
    mready = []
    for m in range(KD):
        ba, bb = 2 * (m % 2), 2 * (m % 2) + 1
        ms = use_unit([(ba, [(k, oh[:, k, :], ol[:, k, :]) for k in range(4)], True, True, [free.get(f"b{ba}"), o_done]),
                       (bb, [(4 + k, oh[:, 4 + k, :], ol[:, 4 + k, :]) for k in range(4)], True, True, [free.get(f"b{bb}"), z_done])])
        ta, tb = 2 + m % 2, 4 + m % 2
        a = tt(tmp[ta][:, :], bank[ba][:, :], gsig[:, m, :], ALU.mult, ms[0], gates_done, free.get(f"tmp{ta}"))
        b_ = tt(tmp[tb][:, :], bank[bb][:, :], gsig[:, 8 + m, :], ALU.mult, ms[1], free.get(f"tmp{tb}"))
        free[f"b{ba}"], free[f"b{bb}"] = a, b_
        c_ = tt(tmp[ta][:, :], tmp[ta][:, :], tmp[tb][:, :], ALU.add, a, b_)
        free[f"tmp{tb}"] = c_
        s_ = split(tmp[ta][:, :], hh[:, m, :], hl[:, m, :], c_, None, h_read2)
        free[f"tmp{ta}"] = s_
        mready.append(s_)

    nready = {}
    for m in range(KD):
        bk = m % 2
        mm = project(bk, *H, KD, mready)
        a = tt(x[:, m, :], bank[bk][:, :], x[:, m, :], ALU.add, mm)
        free[f"b{bk}"] = a
        gather_square(x[:, m, :], m == 0, a)
        nready[m] = a
    last_read = mm
    ssq2 = sum_total(6, True, True)
    ready = {}
    for k in range(KD):
        ready[k] = split(x[:, k, :], hh[:, k, :], hl[:, k, :], nready[k], gg("norm2", k), last_read)
    inv = inv_rms(rs[0], 6, D, ssq2)
    evs, ssq = feed_forward(ready, inv, True)
    ssq3 = None
    for k in range(KD):
        a = tt(x[:, k, :], y[:, k, :], x[:, k, :], ALU.add, evs[k])
        ssq3 = add_square(x[:, k, :], 6, k == 0, k == KD - 1, a)
    r = inv_rms(rs[1], 6, D, ssq3)
    stores = []
    out_v = out.rearrange("(k p) t -> p k t", p=P)
    for k in range(KD):
        a = stt(y[:, k, :], x[:, k, :], gg("final", k), rs[1][:, :], ALU.mult, ALU.mult, r, ssq)
        stores.append(a)
    final = stores
    assert lo_done.count == n_used and hi_done.count == n_units

    block = nc.Block()
    with block:
        @block.sync
        def _(e):
            x_v = x_in.rearrange("(k p) t -> p k t", p=P)

            def load_unit(j, u):
                e.dma_start(raw[j][:, :], stream[u, :, :]).then_inc(raw_in[j].sem, 16)
            e.dma_start(x[:, 0:4, :], x_v[:, 0:4, :]).then_inc(c_x[0].sem, 16)
            load_unit(0, 0)
            e.dma_start(x[:, 4:8, :], x_v[:, 4:8, :]).then_inc(c_x[1].sem, 16)
            load_unit(1, 1)
            with e.Fori(1, n_units // 2) as r:
                for j in range(2):
                    e.wait_ge(lo_done.sem, r * 2 + (j - 1))
                    e.dma_start(raw[j][:, :], stream[bass.ds(r * 2 + j, 1), :, :].rearrange("a p c -> p (a c)"))\
                        .then_inc(raw_in[j].sem, 16)

        @block.gpsimd
        def _(e):
            pad = nc.alloc_semaphore("lo_loop_turns")
            with e.Fori(0, n_units // 2) as r:
                for j in range(2):
                    e.wait_ge(hi_done.sem, r * 2 + (j + 1))
                    e.sem_inc(pad, 1)
                    e.tensor_tensor(wlo[j][:, :], raw[j][:, :], whi[j][:, :].bitcast(F32), ALU.subtract)\
                        .then_inc(lo_done.sem, 1)

        @block.scalar
        def _(e):
            e.sem_inc(chans["act"].sem, START)
            e.dma_start(gn[:, :], gains_in).then_inc(c_small.sem, 16)
            e.dma_start(cst[:, :], consts_in[:, 0:n_fixed]).then_inc(c_consts.sem, 16)
            e.dma_start(pos_i, pos_in.to_broadcast([P, T]) if pos_in.shape[0] == 1 else pos_in).then_inc(c_pos.sem, 16)
            e.dma_start(maskA[:, :], consts_in[:, CONST_AT["maskA"][0]:CONST_AT["maskA"][0] + T]).then_inc(c_mask.sem, 16)
            e.dma_start(rel[:, 255:575], rel_in).then_inc(c_rel.sem, 16)
            q.play("act", e)
            for k, ev in enumerate(final):
                e.wait_ge(ev.chan.sem, ev.n)
                e.dma_start(out_v[:, k, :], y[:, k, :]).then_inc(c_out.sem, 16)
            e.wait_ge(c_out.sem, 16 * KD)

        @block.vector
        def _(e):
            e.sem_inc(chans["dve"].sem, START)
            q.play("dve", e)

        @block.tensor
        def _(e):
            e.sem_inc(chans["pe"].sem, START)
            q.play("pe", e)


def kernel(**inputs):
    import concourse.bacc as bacc
    from concourse.bass_utils import run_bass_kernel_spmd as run
    a = {k: np.asarray(v) for k, v in inputs.items()}

    def cols(v):
        return np.ascontiguousarray(v.reshape(-1, P).T)

    weights = {
        "mla_a": a["mla_w_a"][0], "mla_uq": a["mla_w_uq"][0], "mla_ukv": a["mla_w_ukv"][0], "mla_o": a["mla_w_o"][0],
        "gate0": a["ffn_w_gate"][0], "up0": a["ffn_w_up"][0], "down0": a["ffn_w_down"][0],
        "gate1": a["ffn_w_gate"][1], "up1": a["ffn_w_up"][1], "down1": a["ffn_w_down"][1],
        "kv": a["w_kv_shared"], "b_q": a["b_w_q"][0], "b_o": a["b_w_o"][0],
        "w_in": a["w_in_2"][0], "attn_br": a["w_attn_br_2"][0], "conv_br": a["w_conv_br_2"][0],
        "w_out": a["w_out_2"][0], "ffn_up": a["ffn_w_up_2"][0], "ffn_down": a["ffn_w_down_2"][0],
    }
    stream = weight_units(weights)
    g = {
        "pre0": cols(a["attn_pre_g"][0]), "post0": cols(a["attn_post_g"][0]), "fpre0": cols(a["ffn_pre_g"][0]),
        "fpost0": cols(a["ffn_post_g"][0]), "gq": cols(a["mla_g_q"][0]), "gkv": cols(a["mla_g_kv"][0]),
        "kvsrc": cols(a["kv_src_g"]), "pre1": cols(a["attn_pre_g"][1]), "post1": cols(a["attn_post_g"][1]),
        "fpre1": cols(a["ffn_pre_g"][1]), "fpost1": cols(a["ffn_post_g"][1]), "norm1": cols(a["norm1_g_2"][0]),
        "norm2": cols(a["norm2_g_2"][0]), "final": cols(a["final_g_2"]),
        "dw": a["conv_dw_w_2"][0].reshape(TAPS, 4, P).transpose(2, 1, 0).reshape(P, -1),
        "dwb": cols(a["conv_dw_b_2"][0]), "lng": cols(a["conv_ln_g_2"][0]), "lnb": cols(a["conv_ln_b_2"][0]),
        "fdw": a["ffn_dw_w_2"][0].reshape(3, 2 * KF, P).transpose(2, 1, 0).reshape(P, -1),
        "fdwb": cols(a["ffn_dw_b_2"][0]),
        "pek": cols(a["cmp_pe_k_2"][0]), "pev": cols(a["cmp_pe_v_2"][0]),
        "w2k": np.concatenate([a["cmp_k_w2_2"][0]] * 2, 1), "w2v": a["cmp_v_w2_2"][0],
    }
    gains = np.ascontiguousarray(np.concatenate([g[n] for n, _ in GAINS], 1))
    w1 = np.stack([a[n][0].reshape(16, P, P).transpose(1, 0, 2) for n in ("cmp_k_w1_2", "cmp_v_w1_2")])
    arrays = {
        "x_in": np.ascontiguousarray(a["x"][0].T), "pos_in": a["positions"].reshape(1, T),
        "stream": stream, "gains_in": gains, "consts_in": shape_constants(),
        "rel_in": np.ascontiguousarray(a["b_rel_table"][0][:, ::-1]), "w1_in": np.ascontiguousarray(w1),
    }
    nc = bacc.Bacc("TRN2", target_bir_lowering=False, num_devices=1)
    args = [nc.dram_tensor(n, v.shape, mybir.dt.from_np(v.dtype), kind="ExternalInput").ap() for n, v in arrays.items()]
    args.append(nc.dram_tensor("out", (D, T), F32, kind="ExternalOutput").ap())
    build(nc, *args)
    r = run(nc, [arrays], core_ids=[0])
    return np.ascontiguousarray(r.results[0]["out"].T).reshape(1, T, D)
```

```python
import numpy as np
import concourse.bass as bass
from concourse import mybir
from concourse.alu_op_type import AluOpType as ALU

F32 = mybir.dt.float32
F32R = mybir.dt.float32r
I32 = mybir.dt.int32
ACT = mybir.ActivationFunctionType
AX = mybir.AxisListType

P = 128
T = 512
D = 1024
KD = D // P
FF = 2816
KF = FF // P
QL, KVL = 384, 256
HEADS_A, NOPE, ROPE = 8, 128, 64
PAIRS_B = 8
PAIRS_C = 4
QT = T // P
EPS = 1e-6
CHUNK = 64
N_CMP, CMP_STRIDE, CMP_BLOCK = 31, 16, 32
CONV_C, TAPS = 512, 31
MAX_REL, REL_TABLE = 256, 320
MASKED = -1.0e30
MASKED_DIST = 1.0e33
HUGE = 3.0e38
SLOPES = [2.0 ** -(h + 1) for h in range(8)]


def _block(w, k, cols):
    out = np.zeros((P, P), np.float32)
    at = 0
    for a, b in cols:
        b = min(b, w.shape[1])
        out[:, at:at + b - a] = w[k * P:(k + 1) * P, a:b]
        at += b - a
    return out


def weight_units(w):
    def tile(name, m, ks):
        return [(name, k, [(m * P, (m + 1) * P)]) for k in range(ks)]

    def ffn_units(gate, up, down):
        for j in range(KF):
            yield tile(gate, j, KD)
            yield tile(up, j, KD)
        for half in range(2):
            for kk in range(KF // 2):
                yield [(down, 2 * kk + r, [((4 * half + m) * P, (4 * half + m + 1) * P)])
                       for r in range(2) for m in range(4)]

    def plan():
        for m in range(5):
            yield tile("mla_a", m, KD)
        kr = (QL + KVL, QL + KVL + ROPE)
        yield [("mla_a", k, [kr, kr]) for k in range(KD)]
        for p in range(HEADS_A // 2):
            h0, h1 = 2 * p, 2 * p + 1
            q = lambda h: [("mla_uq", k, [(h * 192, h * 192 + 128)]) for k in range(3)]
            kn = lambda h: [("mla_ukv", k, [(h * 256, h * 256 + 128)]) for k in range(2)]
            v = lambda h: [("mla_ukv", k, [(h * 256 + 128, h * 256 + 256)]) for k in range(2)]
            qr = [("mla_uq", k, [(h * 192 + 128, h * 192 + 192) for h in (h0, h1)]) for k in range(3)]
            yield q(h0) + q(h1)
            yield qr + kn(h0)
            yield kn(h1) + v(h0) + v(h1)
        for m in range(KD):
            yield tile("mla_o", m, KD)
        yield from ffn_units("gate0", "up0", "down0")
        for p in range(PAIRS_B):
            yield tile("kv", KD + p, KD)
            yield tile("kv", p, KD)
            yield tile("b_q", p, KD)
        for m in range(KD):
            yield tile("b_o", m, KD)
        yield from ffn_units("gate1", "up1", "down1")
        c0 = 512 + 6 * 128 + 24
        for c in range(4):
            yield tile_at("w_in", c0 + c * P)
            yield tile_at("w_in", c0 + CONV_C + c * P)
            for j in range(3):
                yield tile_at("w_in", c0 + 2 * CONV_C + (3 * c + j) * P)
        yield [("w_in", k, [(512 + 768, 512 + 768 + 24)]) for k in range(KD)]
        for s in range(6):
            yield tile_at("w_in", 512 + s * P)
        yield tile_at("w_in", 0)
        for p in range(PAIRS_C):
            if p + 1 < PAIRS_C:
                yield tile_at("w_in", (p + 1) * P)
            yield tile_at("w_in", c0 + 2 * CONV_C + (12 + p) * P)
        for m in range(KD):
            yield tile("attn_br", m, 4) + tile("conv_br", m, 4)
        for m in range(KD):
            yield tile("w_out", m, KD)
        for j in range(KF):
            yield tile("ffn_up", j, KD)
            yield tile("ffn_up", KF + j, KD)
        for half in range(2):
            for kk in range(KF // 2):
                yield [("ffn_down", 2 * kk + r, [((4 * half + m) * P, (4 * half + m + 1) * P)])
                       for r in range(2) for m in range(4)]

    def tile_at(name, c):
        return [(name, k, [(c, c + P)]) for k in range(KD)]

    units = list(plan())
    n = len(units) + len(units) % 2
    if w is None:
        return len(units), n
    stream = np.zeros((n, P, KD * P), np.float32)
    for u, blocks in enumerate(units):
        for i, (name, k, cols) in enumerate(blocks):
            stream[u, :, i * P:(i + 1) * P] = _block(w[name], k, cols)
    return stream


def column_map(items):
    at, where = 0, {}
    for name, n in items:
        where[name] = (at, n)
        at += n
    return where, at


GAINS = [("pre0", 8), ("post0", 8), ("fpre0", 8), ("fpost0", 8), ("gq", 3), ("gkv", 2), ("kvsrc", 8),
         ("pre1", 8), ("post1", 8), ("fpre1", 8), ("fpost1", 8), ("norm1", 8), ("norm2", 8), ("final", 8),
         ("dw", 4 * TAPS), ("dwb", 4), ("lng", 4), ("lnb", 4), ("fdw", 2 * KF * 3), ("fdwb", 2 * KF),
         ("pek", 16), ("pev", 16), ("w2k", P), ("w2v", 64)]
GAIN_AT, N_GAIN = column_map(GAINS)
CONSTS = [("ident", P), ("ones", P), ("cdist", 4 * 32), ("cmask", 4 * 32), ("cvalid", 4 * 32), ("inv", 1),
          ("sgn", 1), ("dist", T), ("maskA", T)]
CONST_AT, N_CONST = column_map(CONSTS)


def shape_constants():
    c = np.zeros((P, N_CONST), np.float32)

    def put(name, a):
        at, n = CONST_AT[name]
        c[:, at:at + n] = np.asarray(a, np.float32).reshape(P, n)
    q = np.arange(P)[:, None]
    j = np.arange(T)[None, :]
    put("ident", np.eye(P))
    put("ones", np.ones((P, P)))
    put("maskA", np.where((q < CHUNK) & (j >= T - CHUNK), MASKED, 0.0))
    dist = q + (T - P) - j
    put("dist", np.where(dist < 0, MASKED_DIST, dist))
    end = np.arange(32) * CMP_STRIDE + CMP_BLOCK - 1
    cd = np.stack([q + P * t - end[None, :] for t in range(QT)], 1)
    put("cdist", cd)
    put("cmask", np.where(cd < 0, MASKED, 0.0))
    put("cvalid", cd >= 0)
    half = ROPE // 2
    freq = np.float32(1) / (np.float32(10000) ** (np.arange(0, ROPE, 2, dtype=np.float32) / np.float32(ROPE)))
    put("inv", freq[np.arange(P) % half])
    put("sgn", np.where(np.arange(P) % ROPE < half, -1.0, 1.0))
    return c


class Event:
    def __init__(self, chan, loop, n):
        self.chan, self.loop, self.n = chan, loop, n


class Carried:
    def __init__(self, before):
        self.before, self.last = before, None


class Chan:
    def __init__(self, sem, unit=1, start=0):
        self.sem, self.unit, self.count, self.start = sem, unit, start, start


class Loop:
    def __init__(self, turns, chans):
        self.turns, self.base = turns, {c: c.count for c in chans}
        self.per, self.before = {}, {}


def flat(x):
    if x is None:
        return []
    if isinstance(x, (list, tuple)):
        return [e for y in x for e in flat(y)]
    return [x]


class Queue:
    def __init__(self, engines):
        self.chans = dict(engines)
        self.items = {k: [] for k in engines}
        self.loop = None
        self.free = {}
        self.extra = []

    def all_chans(self):
        return list(self.chans.values()) + self.extra

    def tick(self, chan):
        chan.count += 1
        return Event(chan, self.loop, chan.count)

    def step(self, engine, fn, *waits, chan=None, apart=False):
        chan = chan or self.chans[engine]
        waits = flat(waits)
        if self.loop:
            for w in waits:
                if isinstance(w, Carried):
                    self.loop.before.setdefault(engine, []).extend(flat(w.before))
        ev = self.tick(chan)
        self.items[engine].append((fn, waits, ev, apart))
        return ev

    def start_loop(self, turns):
        chans = self.all_chans()
        self.loop = Loop(turns, chans)
        self.outer = self.items
        self.items = {k: [] for k in self.outer}
        self.carried = {k: Carried(v) for k, v in self.free.items()}
        self.free.update(self.carried)

    def end_loop(self):
        lp = self.loop
        for c in self.all_chans():
            lp.per[c] = c.count - lp.base[c]
            c.count = lp.base[c] + lp.turns * lp.per[c]
        for k, c in self.carried.items():
            if self.free[k] is c:
                self.free[k] = c.before
            else:
                c.last = self.free[k]
        body, self.items, self.loop = self.items, self.outer, None
        for k in body:
            self.items[k].append((lp, body[k]))

    def play(self, engine, e, items=None, loop=None, i=0, seen=None):
        seen = {} if seen is None else seen
        for item in (self.items[engine] if items is None else items):
            if isinstance(item[0], Loop):
                lp, body = item
                self.emit_waits(e, lp.before.get(engine, []), None, 0, seen)
                if body:
                    with e.Fori(0, lp.turns) as turn:
                        self.play(engine, e, body, lp, turn, dict(seen))
                continue
            fn, waits, ev, apart = item
            self.emit_waits(e, waits, loop, i, seen)
            if apart and loop:
                e.sem_inc(self.pads[engine], 1)
            fn(e, i).then_inc(ev.chan.sem, ev.chan.unit)

    def emit_waits(self, e, waits, loop, i, seen):
        fixed, here, back = {}, {}, {}
        for w in waits:
            if isinstance(w, Carried):
                for ev in flat(w.last):
                    if isinstance(ev, Event) and ev.loop is loop:
                        back[ev.chan] = max(back.get(ev.chan, 0), ev.n)
                continue
            if w.loop is not None and w.loop is loop:
                here[w.chan] = max(here.get(w.chan, 0), w.n)
            else:
                n = w.n if w.loop is None else w.n + (w.loop.turns - 1) * w.loop.per[w.chan]
                fixed[w.chan] = max(fixed.get(w.chan, 0), n)
        for c, n in fixed.items():
            if c not in here and seen.get((c, "fixed"), 0) < n:
                seen[c, "fixed"] = n
                e.wait_ge(c.sem, n * c.unit)
        for c, n in back.items():
            if c not in here and (c, "here") not in seen and seen.get((c, "back"), 0) < n:
                seen[c, "back"] = n
                e.wait_ge(c.sem, (i * loop.per[c] + (n - loop.per[c])) * c.unit)
        for c, n in here.items():
            if seen.get((c, "here"), 0) < n:
                seen[c, "here"] = n
                e.wait_ge(c.sem, (i * loop.per[c] + n) * c.unit)


def one(i):
    return bass.ds(i, 1) if not isinstance(i, int) else slice(i, i + 1)


def tile_of(buf, i):
    if isinstance(i, int):
        return buf[:, i, :]
    return buf[:, one(i), :].rearrange("p a t -> p (a t)")


def build(nc, x_in, pos_in, stream, gains_in, consts_in, rel_in, w1_in, out):
    n_used, n_units = weight_units(None)
    KB = 1024
    at = {}

    def sb(name, shape, offset, dt=F32):
        return nc.alloc_sbuf_tensor_at(name, shape, dt, offset=offset)

    base = 16512
    X = base
    HH, HL = X + 16 * KB, X + 32 * KB
    WR = X + 48 * KB
    Y = WR + 24 * KB
    R = Y + 16 * KB
    C = R + 88 * KB
    x = sb("x", [P, KD, T], X)
    hh = sb("hh", [P, KD, T], HH, F32R)
    hl = sb("hl", [P, KD, T], HL, F32R)
    raw = [sb(f"raw{j}", [P, 1024], WR + 4 * KB * j) for j in range(2)]
    whi = [sb(f"whi{j}", [P, 1024], WR + 8 * KB + 4 * KB * j, F32R) for j in range(2)]
    wlo = [sb(f"wlo{j}", [P, 1024], WR + 16 * KB + 4 * KB * j, F32R) for j in range(2)]
    y = sb("y", [P, KD, T], Y)
    fh = sb("fh", [P, KF, T], R, F32R)
    fl = sb("fl", [P, KF, T], R + 44 * KB, F32R)
    oh = sb("oh", [P, KD, T], R, F32R)
    ol = sb("ol", [P, KD, T], R + 16 * KB, F32R)
    R2 = R + 32 * KB
    cqh = sb("cqh", [P, 5, T], R2, F32R)
    cql = sb("cql", [P, 5, T], R2 + 10 * KB, F32R)
    krope = sb("krope", [P, T], R2 + 20 * KB)
    cosT = sb("cosT", [P, T], R2 + 22 * KB)
    sinT = sb("sinT", [P, T], R2 + 24 * KB)
    probsA = [sb(f"probsA{j}", [P, 1280], R2 + 26 * KB + 5 * KB * j) for j in range(2)]
    swapA = sb("swapA", [P, T], R2 + 36 * KB)
    qn = [[sb(f"qn{b}{e}", [P, T], HH + 2 * KB * (2 * b + e)) for e in range(2)] for b in range(2)]
    kn = [[sb(f"kn{b}{e}", [P, T], HH + 8 * KB + 2 * KB * (2 * b + e)) for e in range(2)] for b in range(2)]
    vA = [[sb(f"vA{b}{e}", [P, QT, P], HH + 16 * KB + 2 * KB * (2 * b + e)) for e in range(2)] for b in range(2)]
    qr = [sb(f"qr{b}", [P, T], HH + 24 * KB + 2 * KB * b) for b in range(2)]
    PT = sb("PT", [P, QT, T], Y)
    vtmp = sb("vtmp", [P, T], Y + 8 * KB)
    h2h = sb("h2h", [P, KD, T], R2, F32R)
    h2l = sb("h2l", [P, KD, T], R2 + 16 * KB, F32R)
    R3 = R2 + 32 * KB
    qB = [sb(f"qB{b}", [P, T], R3 + 2 * KB * b) for b in range(2)]
    kB = [sb(f"kB{b}", [P, T], R3 + 4 * KB + 2 * KB * b) for b in range(2)]
    vB = [sb(f"vB{b}", [P, QT, P], R3 + 8 * KB + 2 * KB * b) for b in range(2)]
    probsB = [sb(f"probsB{j}", [P, 1280], R3 + 12 * KB + 5 * KB * j) for j in range(2)]
    biasB = [sb(f"biasB{j}", [P, T], Y + 10 * KB + 2 * KB * j) for j in range(2)]
    gsig = sb("gsig", [P, 16, T], R2)
    kd = [[sb(f"kd{br}{g}", [P, T], R3 + 2 * KB * (2 * br + g)) for g in range(2)] for br in range(2)]
    vC = [sb(f"vC{br}", [P, QT, P], R3 + 8 * KB + 2 * KB * br) for br in range(2)]
    qC = [sb(f"qC{b}", [P, T], R3 + 12 * KB + 2 * KB * b) for b in range(2)]
    R4 = R3 + 16 * KB
    kp = sb("kp", [P, 2, T], R4)
    w1 = sb("w1", [P, 16, P], Y)
    kp2 = sb("kp2", [P, 2, T], R4 + 4 * KB)
    w1v = sb("w1v", [P, 16, P], Y + 8 * KB)
    biasC = sb("biasC", [P, T], Y + 10 * KB)
    probsC = [sb("probsC0", [P, 1280], C + 4 * KB), sb("probsC1", [P, 1280], C + 14 * KB), sb("probsC2", [P, 1280], R4)]
    zpad = [sb(f"zpad{j}", [P, TAPS - 1 + T], (Y, R4)[j]) for j in range(2)]
    zc = sb("zc", [P, 4, T], Y + 4 * KB)
    tmp = [sb(f"tmp{j}", [P, T], C + 2 * KB * j) for j in range(8)]
    rs = [sb(f"rs{j}", [P, T], C + 16 * KB + 2 * KB * ((j + 2) % 3)) for j in range(3)]
    C2 = C + 22 * KB
    n_fixed = CONST_AT["maskA"][0]
    cst = sb("cst", [P, n_fixed], C2)
    gn = sb("gn", [P, N_GAIN], C2 + ((n_fixed * 4 + 31) // 32) * 32)
    C3 = C2 + ((n_fixed * 4 + 31) // 32) * 32 + ((N_GAIN * 4 + 31) // 32) * 32
    pos_i = sb("positions", [P, T], Y + 8 * KB, I32)[:, :]
    rope_tmp = [sb(f"rope_tmp{j}", [P, T], Y + 10 * KB + 2 * KB * j) for j in range(3)]
    maskA = sb("maskA", [P, T], R2 + 38 * KB)
    stat = sb("stat", [P, 64], C3)
    gtok = sb("gtok", [P, QT, 24], C3 + 256)
    pC = sb("pC", [P, QT, 64], Y + 8 * KB)
    vcb = [sb(f"vcb{g}", [64, P], Y + 9 * KB + 512 * g) for g in range(2)]
    kcd = sb("kcd", [P, 2, 32], C3 + 640)
    hid = [sb(f"hid{j}", [P, 64], C3 + 896 + 256 * j) for j in range(2)]
    rel = sb("rel", [16, 640], Y)
    end = C3 + 896 + 512
    assert end <= 229344, end
    bias_dram = nc.dram_tensor("bias_scratch", (16, P, T), F32, kind="Internal").ap()
    rel_dram = nc.dram_tensor("rel_scratch", (16, 640), F32, kind="Internal").ap()

    def cc(name, a=0, n=None):
        o, w = CONST_AT[name]
        return cst[:, o + a:o + a + (w if n is None else n)]

    def gg(name, k=0, n=1):
        return gn[:, GAIN_AT[name][0] + k:GAIN_AT[name][0] + k + n]

    def gdyn(name, k):
        if isinstance(k, int):
            return gg(name, k)
        return gn[:, bass.ds(k + GAIN_AT[name][0], 1)]

    ident = cc("ident")
    ones = cc("ones")

    bank = [nc.alloc_psum_tensor(f"bank{j}", [P, T], F32) for j in range(8)]

    sem = lambda n: nc.alloc_semaphore(n)
    START = 4096
    chans = {k: Chan(sem(f"steps_{k}"), 1, START) for k in ("pe", "act", "dve")}
    q = Queue(chans)
    q.pads = {k: sem(f"apart_{k}") for k in chans}
    raw_in = [Chan(sem(f"raw_loaded{j}"), 16) for j in range(2)]
    hi_done = Chan(sem("weight_hi"))
    lo_done = Chan(sem("weight_lo"))
    c_x = [Chan(sem(f"x_loaded{j}"), 16) for j in range(2)]
    c_small = Chan(sem("small_loaded"), 16)
    c_consts = Chan(sem("consts_loaded"), 16)
    c_pos = Chan(sem("positions_loaded"), 16)
    c_rel = Chan(sem("rel_table"), 16)
    c_mask = Chan(sem("masks_loaded"), 16)
    c_bias = [Chan(sem(f"bias_loaded{j}"), 16) for j in range(2)]
    c_w1 = Chan(sem("w1_loaded"), 16)
    c_out = Chan(sem("out_stored"), 16)
    q.extra = raw_in + [c_mask, hi_done, lo_done, c_rel, c_w1, c_out] + c_bias
    free = q.free

    def pe(fn, *w):
        return q.step("pe", fn, *w)

    def act(fn, *w, **k):
        return q.step("act", fn, *w, **k)

    def dve(fn, *w, **k):
        return q.step("dve", fn, *w, **k)

    def func(o, i_, f, *w, scale=1.0, bias=0.0, accum=None):
        def fn(e, i):
            g = lambda a: a(i) if callable(a) else a
            kw = {} if accum is None else {"accum_out": accum}
            return e.activation(g(o), g(i_), f, bias=g(bias), scale=g(scale), **kw)
        return act(fn, *w, apart=callable(o) or callable(i_) or callable(scale) or callable(bias))

    def tt(o, a, b, op, *w):
        g = lambda v, i: v(i) if callable(v) else v
        return dve(lambda e, i: e.tensor_tensor(g(o, i), g(a, i), g(b, i), op), *w)

    def stt(o, a, s, b, op0, op1, *w):
        g = lambda v, i: v(i) if callable(v) else v
        return dve(lambda e, i: e.scalar_tensor_tensor(g(o, i), g(a, i), g(s, i), g(b, i), op0, op1), *w)

    def ts(o, a, s1, s2, op0, op1, *w):
        g = lambda v, i: v(i) if callable(v) else v
        if s2 is None:
            return dve(lambda e, i: e.tensor_scalar(g(o, i), g(a, i), g(s1, i), None, op0), *w)
        return dve(lambda e, i: e.tensor_scalar(g(o, i), g(a, i), g(s1, i), g(s2, i), op0, op1), *w)

    def round_unit(j, used):
        if q.loop is None and hi_done.count == n_units:
            return
        loaded = q.tick(raw_in[j])
        act(lambda e, i: e.activation(whi[j][:, :], raw[j][:, :], ACT.Copy), loaded, used, chan=hi_done)

    unit_no = [0]

    def use_unit(parts):
        j = unit_no[0] % 2
        unit_no[0] += 1
        ready = q.tick(lo_done)
        evs = []
        for bk, terms, first, last, waits in parts:
            def fn(e, i, bk=bk, terms=(), begin=False, end=False):
                g = lambda v: v(i) if callable(v) else v
                o = bank[bk][:, :]
                for n, (blk, h, l) in enumerate(terms):
                    wh = whi[j][:, blk * P:(blk + 1) * P]
                    wl = wlo[j][:, blk * P:(blk + 1) * P]
                    e.matmul(o, wh, g(h), start=begin and n == 0, stop=False)
                    e.matmul(o, wh, g(l), start=False, stop=False)
                    mm = e.matmul(o, wl, g(h), start=False, stop=end and n == len(terms) - 1)
                return mm
            if isinstance(waits, dict):
                for n, term in enumerate(terms):
                    ev = pe(lambda e, i, fn=fn, term=term, n=n, N=len(terms): fn(
                        e, i, terms=(term,), begin=first and n == 0, end=last and n == N - 1), ready, waits[n])
            else:
                ev = pe(lambda e, i, fn=fn, terms=terms, first=first, last=last: fn(
                    e, i, terms=terms, begin=first, end=last), ready, waits)
            evs.append(ev)
        round_unit(j, evs[-1])
        return evs

    def project(bk, hbuf, lbuf, ks, *waits):
        return use_unit([(bk, [(k, hbuf(k), lbuf(k)) for k in range(ks)], True, True,
                          {k: [w, free.get(f"b{bk}")] for k, w in waits[0].items()} if waits and isinstance(waits[0], dict)
                          else list(waits) + [free.get(f"b{bk}")])])[0]

    H = (lambda k: hh[:, k, :]), (lambda k: hl[:, k, :])
    H2 = (lambda k: h2h[:, k, :]), (lambda k: h2l[:, k, :])
    O = (lambda k: oh[:, k, :]), (lambda k: ol[:, k, :])

    sq_turn = [0]

    def add_square(src, bk, first, last, ready, square=True):
        s = sq_turn[0] % 2
        sq_turn[0] += 1
        if square:
            ev = func(tmp[s][:, :], src, ACT.Square, ready, free.get(f"tmp{s}"))
            rhs = tmp[s][:, :]
        else:
            ev, rhs = ready, src
        mm = pe(lambda e, i: e.matmul(bank[bk][:, :], ones, rhs, start=first, stop=last), ev,
                free.get(f"b{bk}") if first else None)
        if square:
            free[f"tmp{s}"] = mm
        return mm

    def inv_rms(dst, bk, n, summed):
        name = f"rs{rs.index(dst)}"
        a = ts(dst[:, :], bank[bk][:, :], 1.0 / n, EPS, ALU.mult, ALU.add, summed, free.get(name))
        free[f"b{bk}"] = a
        b = func(dst[:, :], dst[:, :], ACT.Sqrt, a)
        return dve(lambda e, i: e.reciprocal(dst[:, :], dst[:, :]), b)

    def split(src, hi, lo, ready, gain=None, war=None):
        a = func(hi, src, ACT.Copy, ready, war, scale=1.0 if gain is None else gain)
        if gain is None:
            return tt(lo, src, (lambda i: hi(i).bitcast(F32)) if callable(hi) else hi.bitcast(F32), ALU.subtract, a, war)
        return stt(lo, src, gain, hi.bitcast(F32), ALU.mult, ALU.subtract, a, war)

    EV_mask = q.tick(c_mask)
    EV_small, EV_const, EV_pos = q.tick(c_small), q.tick(c_consts), q.tick(c_pos)
    EV_x = [q.tick(c_x[0]), q.tick(c_x[1])]
    SM = (EV_small, EV_const)
    for j in range(2):
        round_unit(j, None)
    ready_h = {}
    for k in range(KD):
        xe = EV_x[k // 4]
        ready_h[k] = split(x[:, k, :], hh[:, k, :], hl[:, k, :], (xe, SM), gg("pre0", k))
        ssq = add_square(x[:, k, :], 7, k == 0, k == KD - 1, xe)
    rs_main = inv_rms(rs[0], 7, D, ssq)
    free["rs0"] = rs_main

    rel_ev = Event(c_rel, None, 1)
    c_rel.count = 1
    r1 = ts(rel[:, 255:575], rel[:, 255:575], float(CHUNK) ** 0.5, None, ALU.mult, None, rel_ev)
    r2 = dve(lambda e, i: e.tensor_copy(rel[:, 0:255], rel[:, 255:256].to_broadcast([16, 255])), r1)
    r3 = dve(lambda e, i: e.tensor_copy(rel[:, 575:640], rel[:, 574:575].to_broadcast([16, 65])), r1)
    rel_out = q.step("act", lambda e, i: e.dma_start(rel_dram, rel[:, :]), r2, r3, chan=c_rel)
    free["PT"] = rel_out
    free["vtmp"] = None
    shifted = bass.AP(tensor=rel_dram.tensor, offset=P - 1, ap=[[640, 16], [-1, P], [1, T]])
    rel_out = q.step("act", lambda e, i: e.dma_start(bias_dram, shifted), rel_out, chan=c_rel)

    def rope_tables():
        TWO_PI = 2 * np.pi
        c1 = float(np.float32(6.28125))
        c2 = float(np.float32(np.round((TWO_PI - c1) * 2 ** 21) / 2 ** 21))
        c3 = float(np.float32(TWO_PI - c1 - c2))
        MAGIC = 1.5 * 2.0 ** 23
        PI32 = 3.1415925
        ang, kk_, rr = rope_tmp
        e_ = dve(lambda e, i: e.tensor_copy(ang[:, :], pos_i), EV_pos, SM)
        e_ = ts(ang[:, :], ang[:, :], cc("inv"), None, ALU.mult, None, e_)
        for dst, shift in ((sinT, 0.0), (cosT, 0.25)):
            e_ = ts(kk_[:, :], ang[:, :], float(1.0 / TWO_PI), shift, ALU.mult, ALU.add, e_)
            e_ = ts(kk_[:, :], kk_[:, :], MAGIC, None, ALU.add, None, e_)
            e_ = ts(kk_[:, :], kk_[:, :], -MAGIC, None, ALU.add, None, e_)
            e_ = stt(rr[:, :], kk_[:, :], -c1, ang[:, :], ALU.mult, ALU.add, e_)
            e_ = stt(rr[:, :], kk_[:, :], -c2, rr[:, :], ALU.mult, ALU.add, e_)
            e_ = stt(rr[:, :], kk_[:, :], -c3, rr[:, :], ALU.mult, ALU.add, e_)
            if shift:
                e_ = ts(rr[:, :], rr[:, :], float(np.pi / 2), None, ALU.add, None, e_)
            e_ = ts(rr[:, :], rr[:, :], PI32, -PI32, ALU.min, ALU.max, e_)
            e_ = func(dst[:, :], rr[:, :], ACT.Sin, e_)
        e_ = ts(sinT[:, :], sinT[:, :], cc("sgn"), None, ALU.mult, None, e_)
        rope_ready = e_

        return rope_ready

    def rope(src, dst, swap, ready, war):
        evs = []
        for a in range(4):
            b = a ^ 1
            evs.append(func(swap[32 * a:32 * a + 32, :], src[32 * b:32 * b + 32, :], ACT.Copy,
                            ready, free.get("swap")))
        a_ = tt(swap[:, :], swap[:, :], sinT[:, :], ALU.mult, evs, rope_ready)
        b_ = tt(src[:, :], src[:, :], cosT[:, :], ALU.mult, ready, evs)
        c_ = tt(dst[:, :], src[:, :], swap[:, :], ALU.add, a_, b_, war)
        free["swap"] = c_
        return c_

    lat = []
    for m in range(5):
        bk = m % 2
        mm = project(bk, *H, KD, ready_h if m == 0 else None)
        tb = 2 + m % 4
        v = tt(tmp[tb][:, :], bank[bk][:, :], rs[0][:, :], ALU.mult, mm, rs_main, free.get(f"tmp{tb}"))
        free[f"b{bk}"] = v
        g = gg("gq", m) if m < 3 else gg("gkv", m - 3)
        s = split(tmp[tb][:, :], cqh[:, m, :], cql[:, m, :], v, g)
        n = 3 if m < 3 else 2
        sqm = add_square(tmp[tb][:, :], 6 if m < 3 else 7, m in (0, 3), m in (2, 4), v)
        free[f"tmp{tb}"] = (s, sqm)
        lat.append(s)
        if m == 2:
            rs_q = inv_rms(rs[1], 6, QL, sqm)
            rope_ready = rope_tables()
        if m == 4:
            rs_kv = inv_rms(rs[2], 7, KVL, sqm)
    mm = project(1, *H, KD)
    h_read = mm
    v = tt(tmp[6][:, :], bank[1][:, :], rs[0][:, :], ALU.mult, mm, rs_main)
    free["b1"] = v
    kr_ready = rope(tmp[6], krope, swapA, v, None)
    free["tmp6"] = kr_ready

    SPOT = {0: (0, 0), 2: (0, 128), 1: (1, 0), 3: (2, 0)}
    ORDER = (0, 2, 1, 3)
    PO = {0: 0, 1: 128, 2: 384, 3: 768}
    W = lambda t: (t + 1) * P

    def scores(pieces, *ready, among=None):
        evs = {}
        for b, tiles in ((0, (0, 2)), (1, (1,)), (2, (3,))):
            if among and b < 2:
                among[b]()
            def fn(e, i, b=b, tiles=tiles):
                for t in tiles:
                    for n, (qf, kf) in enumerate(pieces):
                        mm = e.matmul(bank[b][:, SPOT[t][1]:SPOT[t][1] + W(t)], qf(t), kf(W(t)),
                                      start=n == 0, stop=n == len(pieces) - 1)
                return mm
            ev = pe(fn, ready, free.get(f"b{b}"))
            for t in tiles:
                evs[t] = ev
        return evs

    def bias_and_min(evs, pb, st, bias, scale, *ready):
        out = {}
        for t in ORDER:
            b, c = SPOT[t]
            out[t] = dve(lambda e, i, t=t, b=b, c=c: e.tensor_tensor_reduce(
                out=pb[:, PO[t]:PO[t] + W(t)], in0=bank[b][:, c:c + W(t)], in1=bias[:, T - W(t):T],
                scale=-scale, scalar=HUGE, op0=ALU.add, op1=ALU.min,
                accum_out=stat[:, st + t:st + t + 1]), evs[t], ready, free.get(pb.name), apart=True)
            free[f"b{b}"] = out[t]
        return out

    def exponent(evs, pb, st):
        out = {}
        for t in ORDER:
            r = pb[:, PO[t]:PO[t] + W(t)]
            out[t] = func(r, r, ACT.Exp, evs[t], free.get(f"sum{st}"), scale=-1.0, bias=stat[:, st + t:st + t + 1],
                          accum=stat[:, st + 4 + t:st + 5 + t])
        return list(out.values())

    def normalise(evs, pb, st, gate=None, gate_ready=None):
        s = stat[:, st + 4:st + 8]
        r = stat[:, st + 8:st + 12]
        a = dve(lambda e, i: e.reciprocal(r, s), evs)
        free[f"sum{st}"] = a
        if gate is not None:
            a = tt(r, r, gate, ALU.mult, a, gate_ready)
        out = {}
        for t in ORDER:
            v = pb[:, PO[t]:PO[t] + W(t)]
            out[t] = ts(v, v, stat[:, st + 8 + t:st + 9 + t], None, ALU.mult, None, a)
        return out

    tr_turn = [0]
    tr_banks = [5, 6]

    def transposes(evs, pb):
        out = []
        halves = [lambda: transpose_tiles(ORDER[:2], evs, pb, out), lambda: transpose_tiles(ORDER[2:], evs, pb, out)]
        return halves, out

    def transpose_tiles(tiles, evs, pb, out):
        for t in tiles:
            b = tr_banks[tr_turn[0] % len(tr_banks)]
            tr_turn[0] += 1

            def fn(e, i, t=t, b=b):
                for k in range(t + 1):
                    mm = e.transpose(bank[b][:, k * P:(k + 1) * P], pb[:, PO[t] + k * P:PO[t] + (k + 1) * P], ident)
                return mm
            mm = pe(fn, evs[t], free.get(f"b{b}"))
            ev = func(PT[:, 0:t + 1, t * P:(t + 1) * P],
                      bank[b][:, 0:W(t)].rearrange("p (k c) -> p k c", c=P), ACT.Copy, mm, free.get("PT"))
            free[f"b{b}"] = ev
            out.append(ev)
        free[pb.name] = mm

    def times_v(vf, rows, ready, first=True, last=True, war=None):
        def fn(e, i):
            for k in range(QT):
                mm = e.matmul(bank[7][rows[0]:rows[1], k * P:T], vf(k), PT[:, k, k * P:T],
                              start=first and k == 0, stop=last and k == QT - 1, skip_group_check=not (first and last))
            return mm
        ev = pe(fn, ready, war)
        free["PT"] = ev
        return ev

    def token_major(src, dst, ready, war):
        b = tr_banks[tr_turn[0] % len(tr_banks)]
        tr_turn[0] += 1

        def fn(e, i):
            for t in range(QT):
                mm = e.transpose(bank[b][:, t * P:(t + 1) * P], src[:, t * P:(t + 1) * P], ident)
            return mm
        mm = pe(fn, ready, free.get(f"b{b}"))
        ev = func(dst[:, :, :], bank[b][:, :].rearrange("p (k c) -> p k c", c=P), ACT.Copy, mm, war)
        free[f"b{b}"] = ev
        return mm, ev

    def scaled(bk, r, dst, mm, rready, war):
        ev = tt(dst, bank[bk][:, :], r[:, :], ALU.mult, mm, rready, war)
        free[f"b{bk}"] = ev
        return ev

    CQ = lambda k: cqh[:, k, :]
    CL = lambda k: cql[:, k, :]

    def mla_unit(which, p):
        b = p % 2
        ev = {}

        def part(bk, blk, c0, n):
            return (bk, [(blk + k, CQ(c0 + k), CL(c0 + k)) for k in range(n)], True, True,
                    [free.get(f"b{bk}"), lat])
        war = free.get(f"pair{b}")
        if which == 0:
            m0, m1 = use_unit([part(3, 0, 0, 3), part(4, 3, 0, 3)])
            ev["qn0"] = scaled(3, rs[1], qn[b][0][:, :], m0, rs_q, (war, h_read))
            ev["qn1"] = scaled(4, rs[1], qn[b][1][:, :], m1, rs_q, war)
        elif which == 1:
            m0, m1 = use_unit([part(3, 0, 0, 3), part(4, 3, 3, 2)])
            a = scaled(3, rs[1], tmp[6][:, :], m0, rs_q, free.get("tmp6"))
            ev["kn0"] = scaled(4, rs[2], kn[b][0][:, :], m1, rs_kv, war)
            ev["qr"] = rope(tmp[6], qr[b], swapA, a, war)
            free["tmp6"] = ev["qr"]
        else:
            mla_last_unit(b, war, ev)
        return ev

    def mla_last_unit(b, war, ev):
        j = unit_no[0] % 2
        unit_no[0] += 1
        ready = q.tick(lo_done)

        def grp(bk, blk):
            def fn(e, i):
                for n in range(2):
                    wh, wl = (w_[j][:, (blk + n) * P:(blk + n + 1) * P] for w_ in (whi, wlo))
                    o = bank[bk][:, :]
                    e.matmul(o, wh, CQ(3 + n), start=n == 0, stop=False)
                    e.matmul(o, wh, CL(3 + n), start=False, stop=False)
                    mm = e.matmul(o, wl, CQ(3 + n), start=False, stop=n == 1)
                return mm
            return fn
        m0 = pe(grp(3, 0), ready, free.get("b3"), lat)
        m1 = pe(grp(4, 2), ready, free.get("b4"))
        ev["kn1"] = scaled(3, rs[2], kn[b][1][:, :], m0, rs_kv, war)
        m2 = pe(grp(3, 4), free.get("b3"))
        round_unit(j, m2)
        v0 = scaled(4, rs[2], vtmp[:, :], m1, rs_kv, free.get("vtmp"))
        t0, ev["v0"] = token_major(vtmp, vA[b][0], v0, war)
        v1 = scaled(3, rs[2], tmp[7][:, :], m2, rs_kv, free.get("tmp7"))
        free["vtmp"] = t0
        t1, ev["v1"] = token_major(tmp[7], vA[b][1], v1, war)
        free["tmp7"] = t1

    SCALE_A = float(NOPE + ROPE) ** -0.5
    nxt = {}
    for w_ in range(3):
        nxt.update(mla_unit(w_, 0))

    def mla_scores(p, e_, cur, among=None):
        b = p % 2
        rows = slice(64 * e_, 64 * e_ + 64)
        s_ = scores([(lambda t: qn[b][e_][:, t * P:(t + 1) * P], lambda w: kn[b][e_][:, 0:w]),
                     (lambda t: qr[b][rows, t * P:(t + 1) * P], lambda w: krope[rows, 0:w])],
                    cur[f"qn{e_}"], cur[f"kn{e_}"], cur["qr"], kr_ready, among=among)
        return exponent(bias_and_min(s_, probsA[e_], 16 * e_, maskA, SCALE_A, EV_mask), probsA[e_], 16 * e_)

    def mla_pair(p, cur, a0):
        b, nxt = p % 2, {}
        more = p + 1 < HEADS_A // 2
        if more:
            nxt.update(mla_unit(0, p + 1))
        t0, t0_out = transposes(normalise(a0, probsA[0], 0), probsA[0])
        a1 = mla_scores(p, 1, cur, among=t0)
        if more:
            nxt.update(mla_unit(1, p + 1))
        v0 = times_v(lambda k: vA[b][0][:, k, :], (0, P), (t0_out, cur["v0"]), war=free.get("b7"))
        t1, t1_out = transposes(normalise(a1, probsA[1], 16), probsA[1])
        t1[0]()
        o0 = split(bank[7][:, :], oh[:, 2 * p, :], ol[:, 2 * p, :], v0)
        free["b7"] = o0
        if more:
            nxt.update(mla_unit(2, p + 1))
        t1[1]()
        a0 = mla_scores(p + 1, 0, nxt) if more else None
        v1 = times_v(lambda k: vA[b][1][:, k, :], (0, P), (t1_out, cur["v1"]), war=free.get("b7"))
        o1 = split(bank[7][:, :], oh[:, 2 * p + 1, :], ol[:, 2 * p + 1, :], v1)
        free["b7"] = o1
        free[f"pair{b}"] = v1
        return nxt, a0, (o0, o1), v1

    a0 = mla_scores(0, 0, nxt)
    for p in range(HEADS_A // 2):
        nxt, a0, attn_done, mixer_read = mla_pair(p, nxt, a0)

    def gather_square(src, first, ready):
        if first:
            ev = func(tmp[7][:, :], src, ACT.Square, ready, free.get("tmp7"))
        else:
            sl = sq_turn[0] % 2
            sq_turn[0] += 1
            a = func(tmp[sl][:, :], src, ACT.Square, ready, free.get(f"tmp{sl}"))
            ev = tt(tmp[7][:, :], tmp[7][:, :], tmp[sl][:, :], ALU.add, a, free["total"])
            free[f"tmp{sl}"] = ev
        free["total"] = ev
        return ev

    def sum_total(bk, first, last):
        mm = pe(lambda e, i: e.matmul(bank[bk][:, :], ones, tmp[7][:, :], start=first, stop=last),
                free["total"], free.get(f"b{bk}") if first else None)
        free["tmp7"] = mm
        return mm

    def out_tiles(inp, ks, in_ready, y_war):
        evs = []
        for m in range(KD):
            bk = m % 2
            mm = project(bk, *inp, ks, in_ready if m == 0 else None)
            ev = dve(lambda e, i, m=m, bk=bk: e.tensor_copy(y[:, m, :], bank[bk][:, :]), mm, y_war)
            free[f"b{bk}"] = ev
            gather_square(y[:, m, :], m == 0, ev)
            evs.append(ev)
        return evs, sum_total(7, True, True)

    def join(evs, ssq, post, nexts, bk=7):
        r = inv_rms(rs[1], bk, D, ssq)
        ready, more = {}, []
        for k in range(KD):
            tb = 2 + k % 4
            a = tt(tmp[tb][:, :], y[:, k, :], rs[1][:, :], ALU.mult, r, evs[k], free.get(f"tmp{tb}"))
            b_ = stt(x[:, k, :], tmp[tb][:, :], gg(post, k), x[:, k, :], ALU.mult, ALU.add, a)
            free[f"tmp{tb}"] = b_
            g, hi, lo, war = nexts[0]
            ready[k] = [split(x[:, k, :], hi[:, k, :], lo[:, k, :], b_, gg(g, k), war)]
            ssq2 = add_square(x[:, k, :], 6, k == 0, k == KD - 1, b_)
        free["rs1"] = b_
        inv = inv_rms(rs[0], 6, D, ssq2)
        for g, hi, lo, war in nexts[1:]:
            more += [split(x[:, k, :], hi[:, k, :], lo[:, k, :], b_, gg(g, k), war) for k in range(KD)]
        return ready, inv, more

    def gate_up(idx, bks, ready, inv, conv):
        evs = []
        for r in range(2):
            mm = project(bks[r], *H, KD, ready if r == 0 else None)
            u, acc = tmp[2 + r], tmp[4 + r]
            ev = tt(u[:, :], bank[bks[r]][:, :], rs[0][:, :], ALU.mult, mm, inv, free.get(f"tmp{2 + r}"))
            free[f"b{bks[r]}"] = ev
            if conv:
                w3 = lambda i, tap, r=r: gdyn("fdw", idx(i) * 3 + (r * 3 * KF + tap))
                a = func(acc[:, :], u[:, :], ACT.Identity, ev, free.get(f"tmp{4 + r}"), scale=lambda i, w3=w3: w3(i, 2),
                         bias=lambda i, r=r: gdyn("fdwb", idx(i) + r * KF))
                b_ = stt(acc[:, 1:T], u[:, 0:T - 1], lambda i, w3=w3: w3(i, 1), acc[:, 1:T], ALU.mult, ALU.add, a)
                ev = stt(acc[:, 2:T], u[:, 0:T - 2], lambda i, w3=w3: w3(i, 0), acc[:, 2:T], ALU.mult, ALU.add, b_)
                free[f"tmp{2 + r}"] = ev
            evs.append(ev)
        g_, u_ = (tmp[4], tmp[5]) if conv else (tmp[2], tmp[3])
        sil = func(g_[:, :], g_[:, :], ACT.Silu, evs[0])
        prod = tt(u_[:, :], u_[:, :], g_[:, :], ALU.mult, sil, evs[1])
        hi = dve(lambda e, i: e.tensor_scalar(tile_of(fh, idx(i)), u_[:, :], 1.0, None, ALU.mult), prod)
        lo = tt(lambda i: tile_of(fl, idx(i)), u_[:, :], lambda i: tile_of(fh, idx(i)).bitcast(F32), ALU.subtract, hi)
        n1, n2 = ("tmp4", "tmp5") if conv else ("tmp2", "tmp3")
        free[n1], free[n2] = prod, lo
        return lo

    def feed_forward(ready, inv, conv):
        gate_up(lambda i: 0, (2, 3), ready, inv, conv)
        q.start_loop(KF - 1)
        hid_ready = gate_up(lambda i: i + 1, (0, 1), None, inv, conv)
        q.end_loop()
        evs = []

        def down_unit(half, base, first, last):
            parts = []
            for r in range(2):
                for m in range(4):
                    bk = 4 * half + m
                    h_ = lambda i, r=r: tile_of(fh, base(i) + r)
                    l_ = lambda i, r=r: tile_of(fl, base(i) + r)
                    parts.append((bk, [(4 * r + m, h_, l_)], first and r == 0, last and r == 1,
                                  [hid_ready] + ([free.get(f"b{bk}")] if first and r == 0 else [])))
            return use_unit(parts)

        for half in range(2):
            down_unit(half, lambda i: 0, True, False)
            if half:
                sum_total(0, True, False)
            q.start_loop(KF // 4 - 1)
            down_unit(half, lambda i: i * 4 + 2, False, False)
            down_unit(half, lambda i: i * 4 + 4, False, False)
            q.end_loop()
            down_unit(half, lambda i: KF - 4, False, False)
            ms = down_unit(half, lambda i: KF - 2, False, True)[4:]
            for m in range(4):
                mi = 4 * half + m
                ev = dve(lambda e, i, mi=mi: e.tensor_copy(y[:, mi, :], bank[mi][:, :]), ms[m])
                free[f"b{mi}"] = ev
                evs.append(ev)
                if half:
                    ssq = add_square(y[:, mi, :], 0, False, m == 3, ev)
                else:
                    gather_square(y[:, mi, :], m == 0, ev)
        return evs, ssq

    evs, ssq = out_tiles(O, KD, [attn_done, mixer_read], mixer_read)
    ready, inv, _ = join(evs, ssq, "post0", [("fpre0", hh, hl, None)])
    evs, ssq = feed_forward(ready, inv, False)
    ready, inv, ready2 = join(evs, ssq, "fpost0", [("kvsrc", hh, hl, None), ("pre1", h2h, h2l, evs[-1])], 0)

    def load_bias(e_, idx):
        def fn(e, i):
            return e.dma_start(biasB[e_][:, :], bias_dram[one(idx(i)), :, :].rearrange("a p t -> p (a t)"))
        return q.step("act", fn, free.get(f"biasB{e_}"), rel_out, chan=c_bias[e_])

    def add_mask(e_, loaded):
        return ts(biasB[e_][0:CHUNK, T - CHUNK:T], biasB[e_][0:CHUNK, T - CHUNK:T], 0.0, MASKED, ALU.mult, ALU.add, loaded)

    def b_unit(which, b, first_ready=None):
        war = free.get(f"pair{b}")
        ev = {}
        if which == 0:
            mm = project(3, *H, KD, first_ready)
            ev["vtmp"] = scaled(3, rs[0], vtmp[:, :], mm, inv, free.get("vtmp"))
        elif which == 1:
            mm = project(3, *H, KD)
            ev["k"] = scaled(3, rs[0], kB[b][:, :], mm, inv, war)
        else:
            mm = project(3, *H2, KD, ready2)
            ev["q"] = scaled(3, rs[0], qB[b][:, :], mm, inv, war)
        return ev

    def b_values(b, ev):
        free["vtmp"], ev["v"] = token_major(vtmp, vB[b], ev["vtmp"], free.get(f"pair{b}"))

    SCALE_B = 64.0 ** -0.5

    def b_scores(b, e_, cur, loaded, among=None):
        r = slice(64 * e_, 64 * e_ + 64)
        bias_ev = add_mask(e_, loaded)
        s_ = scores([(lambda t: qB[b][r, t * P:(t + 1) * P], lambda w: kB[b][r, 0:w])], cur["q"], cur["k"], among=among)
        m_ = bias_and_min(s_, probsB[e_], 16 * e_, biasB[e_], SCALE_B, bias_ev)
        free[f"biasB{e_}"] = m_[ORDER[-1]]
        return exponent(m_, probsB[e_], 16 * e_)

    def b_pair(b, pidx, cur, more):
        nx = {}
        load1 = load_bias(1, lambda i: pidx(i) * 2 + 1)
        if more:
            load0 = load_bias(0, lambda i: pidx(i) * 2 + 2)
            nx.update(b_unit(0, 1 - b))
        t0, t0_out = transposes(normalise(cur["a0"], probsB[0], 0), probsB[0])
        a1 = b_scores(b, 1, cur, load1, among=t0)
        if more:
            b_values(1 - b, nx)
            nx.update(b_unit(1, 1 - b))
        v0 = times_v(lambda k: vB[b][:, k, 0:64], (0, 64), (t0_out, cur["v"]), war=free.get("b7"))
        t1, t1_out = transposes(normalise(a1, probsB[1], 16), probsB[1])
        t1[0]()
        if more:
            nx.update(b_unit(2, 1 - b))
        t1[1]()
        if more:
            nx["a0"] = b_scores(1 - b, 0, nx, load0)
        v1 = times_v(lambda k: vB[b][:, k, 64:128], (64, 128), t1_out)
        free[f"pair{b}"] = v1
        hi = dve(lambda e, i: e.tensor_scalar(tile_of(oh, pidx(i)), bank[7][:, :], 1.0, None, ALU.mult), v1)
        lo = tt(lambda i: tile_of(ol, pidx(i)), bank[7][:, :], lambda i: tile_of(oh, pidx(i)).bitcast(F32),
                ALU.subtract, hi)
        free["b7"] = lo
        return nx, lo

    tr_banks.insert(0, 4)
    cur = {}
    load0 = load_bias(0, lambda i: 0)
    for w_ in range(3):
        cur.update(b_unit(w_, 0, ready))
        if w_ == 1:
            b_values(0, cur)
    cur["a0"] = b_scores(0, 0, cur, load0)
    for k_ in ("pair0", "pair1"):
        free[k_] = None
    CARRIED_B = ("q", "k", "v", "a0")
    for k_ in CARRIED_B:
        free["B_" + k_] = cur[k_]
    q.start_loop(PAIRS_B // 2 - 1)
    cur = {k_: free["B_" + k_] for k_ in CARRIED_B}
    nx, _ = b_pair(0, lambda i: i * 2, cur, True)
    nx2, _ = b_pair(1, lambda i: i * 2 + 1, nx, True)
    for k_ in CARRIED_B:
        free["B_" + k_] = nx2[k_]
    q.end_loop()
    cur = {k_: free["B_" + k_] for k_ in CARRIED_B}
    nx, _ = b_pair(0, lambda i: PAIRS_B - 2, cur, True)
    _, o_done = b_pair(1, lambda i: PAIRS_B - 1, nx, False)

    tr_banks.remove(4)
    evs, ssq = out_tiles(O, KD, [o_done], free["pair1"])
    ready, inv, _ = join(evs, ssq, "post1", [("fpre1", hh, hl, free["pair1"])])
    evs, ssq = feed_forward(ready, inv, False)
    ready, inv, _ = join(evs, ssq, "fpost1", [("norm1", hh, hl, None)], 0)
    flat_ready = flat(list(ready.values()))

    zero_ev = [dve(lambda e, i, j=j: e.memset(zpad[j][:, 0:TAPS - 1], 0.0), evs, ssq) for j in range(2)]
    def gate_unit(idx, bk):
        mm = project(bk, *H, KD)
        gi = lambda i: tile_of(gsig, idx(i))
        b_ = tt(gi, bank[bk][:, :], rs[0][:, :], ALU.mult, mm)
        free[f"b{bk}"] = b_
        return func(gi, gi, ACT.Sigmoid, b_)

    q.start_loop(2)
    for half in range(2):
        cidx = lambda i, half=half: i * 2 + half
        zp = zpad[half]
        mm = project(0, *H, KD, flat_ready)
        a = tt(tmp[2][:, :], bank[0][:, :], rs[0][:, :], ALU.mult, mm, inv, free.get("tmp2"))
        free["b0"] = a
        mm = project(1, *H, KD)
        g = tt(tmp[3][:, :], bank[1][:, :], rs[0][:, :], ALU.mult, mm, free.get("tmp3"))
        free["b1"] = g
        s = func(tmp[3][:, :], tmp[3][:, :], ACT.Sigmoid, g)
        z = tt(zp[:, TAPS - 1:TAPS - 1 + T], tmp[2][:, :], tmp[3][:, :], ALU.mult, a, s, zero_ev, free.get(f"zpad{half}"))
        free["tmp2"] = free["tmp3"] = z
        taps = list(range(TAPS))
        wt = lambda i, tap, cidx=cidx: gdyn("dw", cidx(i) * TAPS + tap)
        o = lambda i, cidx=cidx: tile_of(zc, cidx(i))
        ev = ts(tmp[4][:, :], zp[:, 0:T], lambda i, wt=wt: wt(i, 0), lambda i, cidx=cidx: gdyn("dwb", cidx(i)),
                ALU.mult, ALU.add, z, free.get("tmp4"))
        done = 1
        for j in range(3):
            free["gsig"] = gate_unit(lambda i, cidx=cidx, j=j: cidx(i) * 3 + j, 2 + j % 2)
            for _ in range(10):
                last_tap = done == TAPS - 1
                dst = o if last_tap else tmp[4][:, :]
                ev = stt(dst, zp[:, done:done + T], lambda i, wt=wt, done=done: wt(i, done), tmp[4][:, :],
                         ALU.mult, ALU.add, ev)
                done += 1
        free["tmp4"] = ev
        free[f"zpad{half}"] = ev
    q.end_loop()
    conv_done, gates_done = ev, free["gsig"]

    mm = project(0, *H, KD)
    g = scaled(0, rs[0], tmp[7][:, :], mm, inv, free.get("tmp7"))

    def tr4(e, i):
        for t in range(QT):
            mm_ = e.transpose(bank[5][:, t * P:(t + 1) * P], tmp[7][:, t * P:(t + 1) * P], ident)
        return mm_
    mm = pe(tr4, g, free.get("b5"))
    free["tmp7"] = mm
    gt_ready = func(gtok[:, :, :], bank[5][:, :].rearrange("p (k c) -> p k c", c=P)[:, :, 0:24], ACT.Sigmoid, mm)
    free["b5"] = gt_ready

    kps = (kp, kp2)
    kp_ready = []

    def compressed_input(s_):
        mm = project(s_, *H, KD)
        tb = 5 + s_
        v_ = scaled(s_, rs[0], tmp[tb][:, :], mm, inv, free.get(f"tmp{tb}"))
        evs_ = []
        for g_ in range(2):
            r = slice(64 * g_, 64 * g_ + 64)
            evs_.append(func(kps[s_][0:64, g_, :], tmp[tb][r, :], ACT.Copy, v_, conv_done))
            evs_.append(func(kps[s_][64:128, g_, 0:T - 1], tmp[tb][r, 1:T], ACT.Copy, v_, conv_done))
        free[f"tmp{tb}"] = evs_
        kp_ready.append(evs_)

    kd_ready, vc_ready = [], []

    def branch_kv(br):
        mm = project(0, *H, KD)
        a = tt(kd[br][0][0:64, :], bank[0][0:64, :], rs[0][0:64, :], ALU.mult, mm)
        b_ = tt(kd[br][1][64:128, :], bank[0][64:128, :], rs[0][64:128, :], ALU.mult, mm)
        free["b0"] = b_
        c_ = func(kd[br][0][64:128, :], kd[br][0][0:64, :], ACT.Copy, a)
        d_ = func(kd[br][1][0:64, :], kd[br][1][64:128, :], ACT.Copy, b_)
        kd_ready.append((a, b_, c_, d_))
        mm = project(1, *H, KD)
        v_ = scaled(1, rs[0], tmp[6][:, :], mm, inv, free.get("tmp6"))
        t_, e2 = token_major(tmp[6], vC[br], v_, None)
        free["tmp6"] = t_
        vc_ready.append(e2)

    compressed_input(0)
    for c in range(4):
        su = add_square(zc[:, c, :], 7, c == 0, c == 3, conv_done, square=False)
    compressed_input(1)
    mu = ts(rs[1][:, :], bank[7][:, :], -1.0 / CONV_C, None, ALU.mult, None, su, free.get("rs1"))
    free["b7"] = mu
    for c in range(4):
        ce = tt(zc[:, c, :], zc[:, c, :], rs[1][:, :], ALU.add, mu)
        s2 = add_square(zc[:, c, :], 7, c == 0, c == 3, ce)
    branch_kv(0)
    ln = inv_rms(rs[2], 7, CONV_C, s2)
    for c in range(4):
        tb = 2 + c % 2
        a = tt(zc[:, c, :], zc[:, c, :], rs[2][:, :], ALU.mult, ln, s2)
        b_ = func(tmp[tb][:, :], zc[:, c, :], ACT.Silu, a, free.get(f"tmp{tb}"), scale=gg("lng", c), bias=gg("lnb", c))
        z_done = split(tmp[tb][:, :], oh[:, 4 + c, :], ol[:, 4 + c, :], b_)
        free[f"tmp{tb}"] = z_done
    load1 = q.step("act", lambda e, i: e.dma_start(w1[:, :, :], w1_in[0]), a, b_, chan=c_w1)
    load2 = q.step("act", lambda e, i: e.dma_start(w1v[:, :, :], w1_in[1]), a, b_, chan=c_mask)
    w1_both = (load1, load2)
    branch_kv(1)

    def c_unit(p):
        mm_ = project(3 + p % 2, *H, KD)
        return scaled(3 + p % 2, rs[0], qC[p % 2][:, :], mm_, inv, free.get(f"pair{p % 2}"))

    free["pair0"] = free["pair1"] = None
    q_ready = {0: c_unit(0)}

    hid_ready = []
    for s_ in range(2):
        ww, pe_name = ((w1, "pek"), (w1v, "pev"))[s_]

        def cmp_mm(e, i, s_=s_, ww=ww):
            for n in range(16):
                rhs = kps[s_][:, :, 2 * n:2 * n + CMP_STRIDE * (N_CMP - 1) + 1:CMP_STRIDE]
                o = bank[2][:, 0:2 * N_CMP].rearrange("p (g n) -> p g n", g=2)
                e.matmul(o, ww[:, n, :], rhs, start=n == 0, stop=n == 15)
            for n in range(16):
                mm_ = e.matmul(bank[2][:, 64:65], ww[:, n, :], gg((("pek"), ("pev"))[s_], n), start=n == 0, stop=n == 15)
            return mm_
        mm = pe(cmp_mm, kp_ready[s_], w1_both, free.get("b2"))
        pb_ = dve(lambda e, i, s_=s_: e.tensor_copy(stat[:, 60 + s_:61 + s_], bank[2][:, 64:65]), mm)
        hd = func(hid[s_][:, 0:2 * N_CMP], bank[2][:, 0:2 * N_CMP], ACT.Gelu_apprx_tanh, pb_, bias=stat[:, 60 + s_:61 + s_])
        free["b2"] = hd
        hid_ready.append(hd)
    cmp_read = mm
    z0 = dve(lambda e, i: e.memset(vcb[0][:, :], 0.0), cmp_read)
    z1 = dve(lambda e, i: e.memset(vcb[1][:, :], 0.0), cmp_read)
    z2 = dve(lambda e, i: e.memset(pC[:, :, :], 0.0), cmp_read)
    mm = pe(lambda e, i: e.matmul(bank[2][:, 0:2 * N_CMP], gg("w2k", 0, P), hid[0][:, 0:2 * N_CMP], start=True, stop=True),
            hid_ready[0], free["b2"])
    kc_ready = dve(lambda e, i: e.tensor_copy(kcd[:, :, 0:N_CMP], bank[2][:, 0:2 * N_CMP].rearrange("p (g n) -> p g n", g=2)), mm)
    free["b2"] = kc_ready

    def vc_mm(e, i):
        for g_ in range(2):
            for e_ in range(2):
                mm_ = e.matmul(bank[2][32 * e_:32 * e_ + N_CMP, 64 * g_:64 * g_ + 64],
                               hid[1][:, g_ * N_CMP:(g_ + 1) * N_CMP], gg("w2v", 0, 64), start=True, stop=True)
        return mm_
    mm = pe(vc_mm, hid_ready[1], free["b2"])
    vcb_ready = []
    for g_ in range(2):
        for e_ in range(2):
            vcb_ready.append(dve(lambda e, i, g_=g_, e_=e_: e.tensor_copy(
                vcb[g_][32 * e_:32 * e_ + N_CMP, 64 * e_:64 * e_ + 64],
                bank[2][32 * e_:32 * e_ + N_CMP, 64 * g_:64 * g_ + 64]), mm, z0, z1))
    free["b2"] = vcb_ready

    free["PT"] = cmp_read
    free["probsC0"] = free["probsC1"] = (z_done, vc_ready, gt_ready)
    free["probsC2"] = cmp_read
    bc = tmp[5]
    pv = pC[:, :, :].rearrange("p t (e n) -> p (t e) n", n=32)[:, :, 0:N_CMP]
    pc_ready, front_of = {}, {}

    def compressed_front(p):
        b, g_ = p % 2, p // 2
        bcv = bc[:, 0:QT * 64].rearrange("p (t e n) -> p t e n", t=QT, e=2)
        cd = cc("cdist").rearrange("p (t n) -> p t n", t=QT)
        cm = cc("cmask").rearrange("p (t n) -> p t n", t=QT)
        bce = [stt(bcv[:, :, e_, :], cd, -SLOPES[2 * p + e_], cm, ALU.mult, ALU.add, SM, free.get("tmp5")) for e_ in range(2)]

        def c_scores(e, i):
            for t in range(QT):
                for e_ in range(2):
                    r = slice(64 * e_, 64 * e_ + 64)
                    mm_ = e.matmul(bank[3 + e_][:, t * 32:t * 32 + N_CMP],
                                   qC[b][r, t * P:(t + 1) * P], kcd[r, g_, 0:N_CMP], start=True, stop=True)
            return mm_
        mm = pe(c_scores, q_ready[p], kc_ready, free.get("b3"), free.get("b4"))
        st8, sm8 = stat[:, 48:56], stat[:, 56:64]
        a = []
        for e_ in range(2):
            sv = bank[3 + e_][:, 0:QT * 32].rearrange("p (t n) -> p t n", n=32)[:, :, 0:N_CMP]
            a.append(stt(pC[:, :, 32 * e_:32 * e_ + N_CMP], sv, 0.125, bcv[:, :, e_, 0:N_CMP], ALU.mult, ALU.add,
                         mm, bce, z2, free.get("pC")))
            free[f"b{3 + e_}"] = a[e_]
        free["tmp5"] = a
        m_ = dve(lambda e, i: e.tensor_reduce(st8, pv, AX.X, ALU.max), a)
        s_ = tt(pv, pv, st8.unsqueeze(2).to_broadcast([P, 8, N_CMP]), ALU.subtract, m_)
        x_ = func(pv, pv, ACT.Exp, s_)
        m_ = dve(lambda e, i: e.tensor_reduce(sm8, pv, AX.X, ALU.add), x_)
        r_ = dve(lambda e, i: e.reciprocal(sm8, sm8), m_)
        gate_c = gtok[:, :, 6 * p:6 * p + 6].rearrange("p t (e b) -> p t e b", b=3)[:, :, :, 0]
        sm = sm8.rearrange("p (t e) -> p t e", e=2)
        r_ = tt(sm, sm, gate_c, ALU.mult, r_, gt_ready)
        valid = cc("cvalid").rearrange("p (t n) -> p t n", t=QT)[:, :, 0:N_CMP]
        v_ = [tt(pC[:, :, 32 * e_:32 * e_ + N_CMP], pC[:, :, 32 * e_:32 * e_ + N_CMP], valid, ALU.mult, r_)
              for e_ in range(2)]
        pc_ready[p] = tt(pv, pv, sm8.unsqueeze(2).to_broadcast([P, 8, N_CMP]), ALU.mult, v_)

    def compressed_back(p):
        def c_tr(e, i):
            for t in range(QT):
                mm_ = e.transpose(bank[5][0:64, t * P:(t + 1) * P], pC[:, t, :], ident)
            return mm_
        mm = pe(c_tr, pc_ready[p], free.get("b5"))
        free["pC"] = mm
        c_pt = func(tmp[6][0:64, :], bank[5][0:64, :], ACT.Copy, mm, free.get("tmp6"))
        free["b5"] = c_pt
        free["tmp6"] = pe(lambda e, i: e.matmul(bank[7][:, :], vcb[p // 2][:, :], tmp[6][0:64, :], start=True,
                                                stop=False, skip_group_check=True), c_pt, vcb_ready, free.get("b7"))

    def front(n, among=None):
        p, e_, br = n // 4, n // 2 % 2, n % 2
        b, g_, h = p % 2, p // 2, 2 * p + e_
        if br == 0:
            free["bias_now"] = ts(biasC[:, :], cc("dist"), -8.0 * SLOPES[h], None, ALU.mult, None, SM,
                                  free.get("biasC"), cmp_read)
        r = slice(64 * e_, 64 * e_ + 64)
        s_ = scores([(lambda t: qC[b][r, t * P:(t + 1) * P], lambda w: kd[br][g_][r, 0:w])], q_ready[p], kd_ready, among=among)
        pb, st = probsC[n % 3], 16 * (n % 3)
        m_ = bias_and_min(s_, pb, st, biasC, SCALE_B, free["bias_now"])
        free["biasC"] = m_[ORDER[-1]]
        free[f"pair{b}"] = s_[3]
        front_of[n] = exponent(m_, pb, st)

    def values_of(br, g_):
        return lambda k: vC[br][:, k, 64 * g_:64 * g_ + 64]

    for n in range(-2, 4 * PAIRS_C):
        p, e_, br = n // 4, n // 2 % 2, n % 2
        if n >= 0:
            h = 2 * p + e_
            gate = gtok[:, :, 3 * h + 1 + br:3 * h + 2 + br].rearrange("p t a -> p (t a)")
            nn = normalise(front_of[n], probsC[n % 3], 16 * (n % 3), gate, gt_ready)
            tr, tr_out = transposes(nn, probsC[n % 3])
        if n + 2 < 4 * PAIRS_C:
            front(n + 2, among=tr if n >= 0 else None)
            if (n + 2) % 4 == 0:
                compressed_front((n + 2) // 4)
        elif n >= 0:
            tr[0]()
            tr[1]()
        if n < 0:
            continue
        if n % 4 == 0:
            if p + 1 < PAIRS_C:
                q_ready[p + 1] = c_unit(p + 1)
            compressed_back(p)
        if n % 4 == 2:
            gates_done2 = gate_unit(lambda i, p=p: 12 + p, 3)
        ov = times_v(values_of(br, p // 2), (64 * e_, 64 * e_ + 64), (tr_out, vc_ready), first=False, last=n % 4 == 3)
        if n % 4 == 3:
            o_done = split(bank[7][:, :], oh[:, p, :], ol[:, p, :], ov)
            free["b7"] = o_done
    q_read = q_ready[3]

    h_read2 = (q_read, gates_done2)
    mready = []
    for m in range(KD):
        ba, bb = 2 * (m % 2), 2 * (m % 2) + 1
        ms = use_unit([(ba, [(k, oh[:, k, :], ol[:, k, :]) for k in range(4)], True, True, [free.get(f"b{ba}"), o_done]),
                       (bb, [(4 + k, oh[:, 4 + k, :], ol[:, 4 + k, :]) for k in range(4)], True, True, [free.get(f"b{bb}"), z_done])])
        ta, tb = 2 + m % 2, 4 + m % 2
        a = tt(tmp[ta][:, :], bank[ba][:, :], gsig[:, m, :], ALU.mult, ms[0], gates_done, free.get(f"tmp{ta}"))
        b_ = tt(tmp[tb][:, :], bank[bb][:, :], gsig[:, 8 + m, :], ALU.mult, ms[1], gates_done2, free.get(f"tmp{tb}"))
        free[f"b{ba}"], free[f"b{bb}"] = a, b_
        c_ = tt(tmp[ta][:, :], tmp[ta][:, :], tmp[tb][:, :], ALU.add, a, b_)
        free[f"tmp{tb}"] = c_
        s_ = split(tmp[ta][:, :], hh[:, m, :], hl[:, m, :], c_, None, h_read2)
        free[f"tmp{ta}"] = s_
        mready.append(s_)

    nready = {}
    for m in range(KD):
        bk = m % 2
        mm = project(bk, *H, KD, mready)
        a = tt(x[:, m, :], bank[bk][:, :], x[:, m, :], ALU.add, mm)
        free[f"b{bk}"] = a
        gather_square(x[:, m, :], m == 0, a)
        nready[m] = a
    last_read = mm
    ssq2 = sum_total(6, True, True)
    ready = {}
    for k in range(KD):
        ready[k] = split(x[:, k, :], hh[:, k, :], hl[:, k, :], nready[k], gg("norm2", k), last_read)
    inv = inv_rms(rs[0], 6, D, ssq2)
    evs, ssq = feed_forward(ready, inv, True)
    ssq3 = None
    for k in range(KD):
        a = tt(x[:, k, :], y[:, k, :], x[:, k, :], ALU.add, evs[k])
        ssq3 = add_square(x[:, k, :], 6, k == 0, k == KD - 1, a)
    r = inv_rms(rs[1], 6, D, ssq3)
    stores = []
    out_v = out.rearrange("(k p) t -> p k t", p=P)
    for k in range(KD):
        a = stt(y[:, k, :], x[:, k, :], gg("final", k), rs[1][:, :], ALU.mult, ALU.mult, r, ssq)
        stores.append(a)
    final = stores
    assert lo_done.count == n_used and hi_done.count == n_units

    block = nc.Block()
    with block:
        @block.sync
        def _(e):
            x_v = x_in.rearrange("(k p) t -> p k t", p=P)

            def load_unit(j, u):
                e.dma_start(raw[j][:, :], stream[u, :, :]).then_inc(raw_in[j].sem, 16)
            e.dma_start(x[:, 0:4, :], x_v[:, 0:4, :]).then_inc(c_x[0].sem, 16)
            load_unit(0, 0)
            e.dma_start(x[:, 4:8, :], x_v[:, 4:8, :]).then_inc(c_x[1].sem, 16)
            load_unit(1, 1)
            with e.Fori(1, n_units // 2) as r:
                for j in range(2):
                    e.wait_ge(lo_done.sem, r * 2 + (j - 1))
                    e.dma_start(raw[j][:, :], stream[bass.ds(r * 2 + j, 1), :, :].rearrange("a p c -> p (a c)"))\
                        .then_inc(raw_in[j].sem, 16)

        @block.gpsimd
        def _(e):
            pad = nc.alloc_semaphore("lo_loop_turns")
            with e.Fori(0, n_units // 2) as r:
                for j in range(2):
                    e.wait_ge(hi_done.sem, r * 2 + (j + 1))
                    e.sem_inc(pad, 1)
                    e.tensor_tensor(wlo[j][:, :], raw[j][:, :], whi[j][:, :].bitcast(F32), ALU.subtract)\
                        .then_inc(lo_done.sem, 1)

        @block.scalar
        def _(e):
            e.sem_inc(chans["act"].sem, START)
            e.dma_start(gn[:, :], gains_in).then_inc(c_small.sem, 16)
            e.dma_start(cst[:, :], consts_in[:, 0:n_fixed]).then_inc(c_consts.sem, 16)
            e.dma_start(pos_i, pos_in.to_broadcast([P, T]) if pos_in.shape[0] == 1 else pos_in).then_inc(c_pos.sem, 16)
            e.dma_start(maskA[:, :], consts_in[:, CONST_AT["maskA"][0]:CONST_AT["maskA"][0] + T]).then_inc(c_mask.sem, 16)
            e.dma_start(rel[:, 255:575], rel_in).then_inc(c_rel.sem, 16)
            q.play("act", e)
            for k, ev in enumerate(final):
                e.wait_ge(ev.chan.sem, ev.n)
                e.dma_start(out_v[:, k, :], y[:, k, :]).then_inc(c_out.sem, 16)
            e.wait_ge(c_out.sem, 16 * KD)

        @block.vector
        def _(e):
            e.sem_inc(chans["dve"].sem, START)
            q.play("dve", e)

        @block.tensor
        def _(e):
            e.sem_inc(chans["pe"].sem, START)
            q.play("pe", e)


def kernel(**inputs):
    import concourse.bacc as bacc
    from concourse.bass_utils import run_bass_kernel_spmd as run
    a = {k: np.asarray(v) for k, v in inputs.items()}

    def cols(v):
        return np.ascontiguousarray(v.reshape(-1, P).T)

    weights = {
        "mla_a": a["mla_w_a"][0], "mla_uq": a["mla_w_uq"][0], "mla_ukv": a["mla_w_ukv"][0], "mla_o": a["mla_w_o"][0],
        "gate0": a["ffn_w_gate"][0], "up0": a["ffn_w_up"][0], "down0": a["ffn_w_down"][0],
        "gate1": a["ffn_w_gate"][1], "up1": a["ffn_w_up"][1], "down1": a["ffn_w_down"][1],
        "kv": a["w_kv_shared"], "b_q": a["b_w_q"][0], "b_o": a["b_w_o"][0],
        "w_in": a["w_in_2"][0], "attn_br": a["w_attn_br_2"][0], "conv_br": a["w_conv_br_2"][0],
        "w_out": a["w_out_2"][0], "ffn_up": a["ffn_w_up_2"][0], "ffn_down": a["ffn_w_down_2"][0],
    }
    stream = weight_units(weights)
    g = {
        "pre0": cols(a["attn_pre_g"][0]), "post0": cols(a["attn_post_g"][0]), "fpre0": cols(a["ffn_pre_g"][0]),
        "fpost0": cols(a["ffn_post_g"][0]), "gq": cols(a["mla_g_q"][0]), "gkv": cols(a["mla_g_kv"][0]),
        "kvsrc": cols(a["kv_src_g"]), "pre1": cols(a["attn_pre_g"][1]), "post1": cols(a["attn_post_g"][1]),
        "fpre1": cols(a["ffn_pre_g"][1]), "fpost1": cols(a["ffn_post_g"][1]), "norm1": cols(a["norm1_g_2"][0]),
        "norm2": cols(a["norm2_g_2"][0]), "final": cols(a["final_g_2"]),
        "dw": a["conv_dw_w_2"][0].reshape(TAPS, 4, P).transpose(2, 1, 0).reshape(P, -1),
        "dwb": cols(a["conv_dw_b_2"][0]), "lng": cols(a["conv_ln_g_2"][0]), "lnb": cols(a["conv_ln_b_2"][0]),
        "fdw": a["ffn_dw_w_2"][0].reshape(3, 2 * KF, P).transpose(2, 1, 0).reshape(P, -1),
        "fdwb": cols(a["ffn_dw_b_2"][0]),
        "pek": cols(a["cmp_pe_k_2"][0]), "pev": cols(a["cmp_pe_v_2"][0]),
        "w2k": np.concatenate([a["cmp_k_w2_2"][0]] * 2, 1), "w2v": a["cmp_v_w2_2"][0],
    }
    gains = np.ascontiguousarray(np.concatenate([g[n] for n, _ in GAINS], 1))
    w1 = np.stack([a[n][0].reshape(16, P, P).transpose(1, 0, 2) for n in ("cmp_k_w1_2", "cmp_v_w1_2")])
    arrays = {
        "x_in": np.ascontiguousarray(a["x"][0].T), "pos_in": a["positions"].reshape(1, T),
        "stream": stream, "gains_in": gains, "consts_in": shape_constants(),
        "rel_in": np.ascontiguousarray(a["b_rel_table"][0][:, ::-1]), "w1_in": np.ascontiguousarray(w1),
    }
    nc = bacc.Bacc("TRN2", target_bir_lowering=False, num_devices=1)
    args = [nc.dram_tensor(n, v.shape, mybir.dt.from_np(v.dtype), kind="ExternalInput").ap() for n, v in arrays.items()]
    args.append(nc.dram_tensor("out", (D, T), F32, kind="ExternalOutput").ap())
    build(nc, *args)
    r = run(nc, [arrays], core_ids=[0])
    return np.ascontiguousarray(r.results[0]["out"].T).reshape(1, T, D)
```

```python
import numpy as np
import concourse.bass as bass
from concourse import mybir
from concourse.alu_op_type import AluOpType as ALU

F32 = mybir.dt.float32
F32R = mybir.dt.float32r
I32 = mybir.dt.int32
ACT = mybir.ActivationFunctionType
AX = mybir.AxisListType

P = 128
T = 512
D = 1024
KD = D // P
FF = 2816
KF = FF // P
QL, KVL = 384, 256
HEADS_A, NOPE, ROPE = 8, 128, 64
PAIRS_B = 8
PAIRS_C = 4
QT = T // P
EPS = 1e-6
CHUNK = 64
N_CMP, CMP_STRIDE, CMP_BLOCK = 31, 16, 32
CONV_C, TAPS = 512, 31
MAX_REL, REL_TABLE = 256, 320
MASKED = -1.0e30
MASKED_DIST = 1.0e33
HUGE = 3.0e38
SLOPES = [2.0 ** -(h + 1) for h in range(8)]


def _block(w, k, cols):
    out = np.zeros((P, P), np.float32)
    at = 0
    for a, b in cols:
        b = min(b, w.shape[1])
        out[:, at:at + b - a] = w[k * P:(k + 1) * P, a:b]
        at += b - a
    return out


def weight_units(w):
    def tile(name, m, ks):
        return [(name, k, [(m * P, (m + 1) * P)]) for k in range(ks)]

    def ffn_units(gate, up, down):
        for j in range(KF):
            yield tile(gate, j, KD)
            yield tile(up, j, KD)
        for half in range(2):
            for kk in range(KF // 2):
                yield [(down, 2 * kk + r, [((4 * half + m) * P, (4 * half + m + 1) * P)])
                       for r in range(2) for m in range(4)]

    def plan():
        for m in range(5):
            yield tile("mla_a", m, KD)
        kr = (QL + KVL, QL + KVL + ROPE)
        yield [("mla_a", k, [kr, kr]) for k in range(KD)]
        for p in range(HEADS_A // 2):
            h0, h1 = 2 * p, 2 * p + 1
            q = lambda h: [("mla_uq", k, [(h * 192, h * 192 + 128)]) for k in range(3)]
            kn = lambda h: [("mla_ukv", k, [(h * 256, h * 256 + 128)]) for k in range(2)]
            v = lambda h: [("mla_ukv", k, [(h * 256 + 128, h * 256 + 256)]) for k in range(2)]
            qr = [("mla_uq", k, [(h * 192 + 128, h * 192 + 192) for h in (h0, h1)]) for k in range(3)]
            yield q(h0) + q(h1)
            yield qr + kn(h0)
            yield kn(h1) + v(h0) + v(h1)
        for m in range(KD):
            yield tile("mla_o", m, KD)
        yield from ffn_units("gate0", "up0", "down0")
        for p in range(PAIRS_B):
            yield tile("kv", KD + p, KD)
            yield tile("kv", p, KD)
            yield tile("b_q", p, KD)
        for m in range(KD):
            yield tile("b_o", m, KD)
        yield from ffn_units("gate1", "up1", "down1")
        c0 = 512 + 6 * 128 + 24
        yield [("w_in", k, [(512 + 768, 512 + 768 + 24)]) for k in range(KD)]
        for c in range(4):
            yield tile_at("w_in", c0 + c * P)
            yield tile_at("w_in", c0 + CONV_C + c * P)
            for j in range(3):
                yield tile_at("w_in", c0 + 2 * CONV_C + (3 * c + j) * P)
        for s in range(6):
            yield tile_at("w_in", 512 + s * P)
        yield tile_at("w_in", 0)
        for p in range(PAIRS_C):
            if p + 1 < PAIRS_C:
                yield tile_at("w_in", (p + 1) * P)
            yield tile_at("w_in", c0 + 2 * CONV_C + (12 + p) * P)
        for m in range(KD):
            yield tile("attn_br", m, 4) + tile("conv_br", m, 4)
        for m in range(KD):
            yield tile("w_out", m, KD)
        for j in range(KF):
            yield tile("ffn_up", j, KD)
            yield tile("ffn_up", KF + j, KD)
        for half in range(2):
            for kk in range(KF // 2):
                yield [("ffn_down", 2 * kk + r, [((4 * half + m) * P, (4 * half + m + 1) * P)])
                       for r in range(2) for m in range(4)]

    def tile_at(name, c):
        return [(name, k, [(c, c + P)]) for k in range(KD)]

    units = list(plan())
    n = len(units) + len(units) % 2
    if w is None:
        return len(units), n
    stream = np.zeros((n, P, KD * P), np.float32)
    for u, blocks in enumerate(units):
        for i, (name, k, cols) in enumerate(blocks):
            stream[u, :, i * P:(i + 1) * P] = _block(w[name], k, cols)
    return stream


def column_map(items):
    at, where = 0, {}
    for name, n in items:
        where[name] = (at, n)
        at += n
    return where, at


GAINS = [("pre0", 8), ("post0", 8), ("fpre0", 8), ("fpost0", 8), ("gq", 3), ("gkv", 2), ("kvsrc", 8),
         ("pre1", 8), ("post1", 8), ("fpre1", 8), ("fpost1", 8), ("norm1", 8), ("norm2", 8), ("final", 8),
         ("dw", 4 * TAPS), ("dwb", 4), ("lng", 4), ("lnb", 4), ("fdw", 2 * KF * 3), ("fdwb", 2 * KF),
         ("pek", 16), ("pev", 16), ("w2k", P), ("w2v", 64)]
GAIN_AT, N_GAIN = column_map(GAINS)
CONSTS = [("ident", P), ("ones", P), ("cdist", 4 * 32), ("cmask", 4 * 32), ("cvalid", 4 * 32), ("inv", 1),
          ("sgn", 1), ("eps", 1), ("dist", T), ("maskA", T)]
CONST_AT, N_CONST = column_map(CONSTS)


def shape_constants():
    c = np.zeros((P, N_CONST), np.float32)

    def put(name, a):
        at, n = CONST_AT[name]
        c[:, at:at + n] = np.asarray(a, np.float32).reshape(P, n)
    q = np.arange(P)[:, None]
    j = np.arange(T)[None, :]
    put("ident", np.eye(P))
    put("ones", np.ones((P, P)))
    put("eps", np.full(P, EPS))
    put("maskA", np.where((q < CHUNK) & (j >= T - CHUNK), MASKED, 0.0))
    dist = q + (T - P) - j
    put("dist", np.where(dist < 0, MASKED_DIST, dist))
    end = np.arange(32) * CMP_STRIDE + CMP_BLOCK - 1
    cd = np.stack([q + P * t - end[None, :] for t in range(QT)], 1)
    put("cdist", cd)
    put("cmask", np.where(cd < 0, MASKED, 0.0))
    put("cvalid", cd >= 0)
    half = ROPE // 2
    freq = np.float32(1) / (np.float32(10000) ** (np.arange(0, ROPE, 2, dtype=np.float32) / np.float32(ROPE)))
    put("inv", freq[np.arange(P) % half])
    put("sgn", np.where(np.arange(P) % ROPE < half, -1.0, 1.0))
    return c


class Event:
    def __init__(self, chan, loop, n):
        self.chan, self.loop, self.n = chan, loop, n


class Carried:
    def __init__(self, before):
        self.before, self.last = before, None


class Chan:
    def __init__(self, sem, unit=1, start=0):
        self.sem, self.unit, self.count, self.start = sem, unit, start, start


class Loop:
    def __init__(self, turns, chans):
        self.turns, self.base = turns, {c: c.count for c in chans}
        self.per, self.before = {}, {}


def flat(x):
    if x is None:
        return []
    if isinstance(x, (list, tuple)):
        return [e for y in x for e in flat(y)]
    return [x]


class Tiles:
    def __init__(self, before, after):
        self.before, self.after = before, after


class Queue:
    def __init__(self, engines):
        self.chans = dict(engines)
        self.items = {k: [] for k in engines}
        self.loop = None
        self.free = {}
        self.extra = []

    def all_chans(self):
        return list(self.chans.values()) + self.extra

    def tick(self, chan):
        chan.count += 1
        return Event(chan, self.loop, chan.count)

    def step(self, engine, fn, *waits, chan=None, apart=False):
        chan = chan or self.chans[engine]
        waits = flat(waits)
        if self.loop:
            for w in waits:
                if isinstance(w, Carried):
                    self.loop.before.setdefault(engine, []).extend(flat(w.before))
        ev = self.tick(chan)
        self.items[engine].append((fn, waits, ev, apart))
        return ev

    def start_loop(self, turns):
        chans = self.all_chans()
        self.loop = Loop(turns, chans)
        self.outer = self.items
        self.items = {k: [] for k in self.outer}
        self.carried = {k: Carried(v) for k, v in self.free.items()}
        self.free.update(self.carried)

    def end_loop(self):
        lp = self.loop
        for c in self.all_chans():
            lp.per[c] = c.count - lp.base[c]
            c.count = lp.base[c] + lp.turns * lp.per[c]
        for k, c in self.carried.items():
            if self.free[k] is c:
                self.free[k] = c.before
            else:
                c.last = self.free[k]
        body, self.items, self.loop = self.items, self.outer, None
        for k in body:
            self.items[k].append((lp, body[k]))

    def play(self, engine, e, items=None, loop=None, i=0, seen=None):
        seen = {} if seen is None else seen
        for item in (self.items[engine] if items is None else items):
            if isinstance(item[0], Loop):
                lp, body = item
                self.emit_waits(e, lp.before.get(engine, []), None, 0, seen)
                if body:
                    with e.Fori(0, lp.turns) as turn:
                        self.play(engine, e, body, lp, turn, dict(seen))
                continue
            fn, waits, ev, apart = item
            self.emit_waits(e, waits, loop, i, seen)
            if apart and loop:
                e.sem_inc(self.pads[engine], 1)
            fn(e, i).then_inc(ev.chan.sem, ev.chan.unit)

    def emit_waits(self, e, waits, loop, i, seen):
        fixed, here, back = {}, {}, {}
        for w in waits:
            if isinstance(w, Carried):
                for ev in flat(w.last):
                    if isinstance(ev, Event) and ev.loop is loop:
                        back[ev.chan] = max(back.get(ev.chan, 0), ev.n)
                continue
            if w.loop is not None and w.loop is loop:
                here[w.chan] = max(here.get(w.chan, 0), w.n)
            else:
                n = w.n if w.loop is None else w.n + (w.loop.turns - 1) * w.loop.per[w.chan]
                fixed[w.chan] = max(fixed.get(w.chan, 0), n)
        for c, n in fixed.items():
            if c not in here and seen.get((c, "fixed"), 0) < n:
                seen[c, "fixed"] = n
                e.wait_ge(c.sem, n * c.unit)
        for c, n in back.items():
            if c not in here and (c, "here") not in seen and seen.get((c, "back"), 0) < n:
                seen[c, "back"] = n
                e.wait_ge(c.sem, (i * loop.per[c] + (n - loop.per[c])) * c.unit)
        for c, n in here.items():
            if seen.get((c, "here"), 0) < n:
                seen[c, "here"] = n
                e.wait_ge(c.sem, (i * loop.per[c] + n) * c.unit)


def one(i):
    return bass.ds(i, 1) if not isinstance(i, int) else slice(i, i + 1)


def tile_of(buf, i):
    if isinstance(i, int):
        return buf[:, i, :]
    return buf[:, one(i), :].rearrange("p a t -> p (a t)")


def build(nc, x_in, pos_in, stream, gains_in, consts_in, rel_in, w1_in, out):
    n_used, n_units = weight_units(None)
    KB = 1024
    at = {}

    def sb(name, shape, offset, dt=F32):
        return nc.alloc_sbuf_tensor_at(name, shape, dt, offset=offset)

    base = 16512
    X = base
    HH, HL = X + 16 * KB, X + 32 * KB
    WR = X + 48 * KB
    Y = WR + 24 * KB
    R = Y + 16 * KB
    C = R + 88 * KB
    x = sb("x", [P, KD, T], X)
    hh = sb("hh", [P, KD, T], HH, F32R)
    hl = sb("hl", [P, KD, T], HL, F32R)
    raw = [sb(f"raw{j}", [P, 1024], WR + 4 * KB * j) for j in range(2)]
    whi = [sb(f"whi{j}", [P, 1024], WR + 8 * KB + 4 * KB * j, F32R) for j in range(2)]
    wlo = [sb(f"wlo{j}", [P, 1024], WR + 16 * KB + 4 * KB * j, F32R) for j in range(2)]
    y = sb("y", [P, KD, T], Y)
    fh = sb("fh", [P, KF, T], R, F32R)
    fl = sb("fl", [P, KF, T], R + 44 * KB, F32R)
    oh = sb("oh", [P, KD, T], R, F32R)
    ol = sb("ol", [P, KD, T], R + 16 * KB, F32R)
    R2 = R + 32 * KB
    cqh = sb("cqh", [P, 5, T], R2, F32R)
    cql = sb("cql", [P, 5, T], R2 + 10 * KB, F32R)
    krope = sb("krope", [P, T], R2 + 20 * KB)
    cosT = sb("cosT", [P, T], R2 + 22 * KB)
    sinT = sb("sinT", [P, T], R2 + 24 * KB)
    probsA = [sb(f"probsA{j}", [P, 1280], R2 + 26 * KB + 5 * KB * j) for j in range(2)]
    swapA = sb("swapA", [P, T], R2 + 36 * KB)
    qn = [[sb(f"qn{b}{e}", [P, T], HH + 2 * KB * (2 * b + e)) for e in range(2)] for b in range(2)]
    kn = [[sb(f"kn{b}{e}", [P, T], HH + 8 * KB + 2 * KB * (2 * b + e)) for e in range(2)] for b in range(2)]
    vA = [[sb(f"vA{b}{e}", [P, QT, P], HH + 16 * KB + 2 * KB * (2 * b + e)) for e in range(2)] for b in range(2)]
    qr = [sb(f"qr{b}", [P, T], HH + 24 * KB + 2 * KB * b) for b in range(2)]
    PT = sb("PT", [P, QT, T], Y)
    vtmp = sb("vtmp", [P, T], Y + 8 * KB)
    h2h = sb("h2h", [P, KD, T], R2, F32R)
    h2l = sb("h2l", [P, KD, T], R2 + 16 * KB, F32R)
    R3 = R2 + 32 * KB
    qB = [sb(f"qB{b}", [P, T], R3 + 2 * KB * b) for b in range(2)]
    kB = [sb(f"kB{b}", [P, T], R3 + 4 * KB + 2 * KB * b) for b in range(2)]
    vB = [sb(f"vB{b}", [P, QT, P], R3 + 8 * KB + 2 * KB * b) for b in range(2)]
    probsB = [sb(f"probsB{j}", [P, 1280], R3 + 12 * KB + 5 * KB * j) for j in range(2)]
    biasB = [sb(f"biasB{j}", [P, T], Y + 10 * KB + 2 * KB * j) for j in range(2)]
    gsig = sb("gsig", [P, 16, T], R2)
    kd = [[sb(f"kd{br}{g}", [P, T], R3 + 2 * KB * (2 * br + g)) for g in range(2)] for br in range(2)]
    vC = [sb(f"vC{br}", [P, QT, P], R3 + 8 * KB + 2 * KB * br) for br in range(2)]
    qC = [sb(f"qC{b}", [P, T], R3 + 12 * KB + 2 * KB * b) for b in range(2)]
    R4 = R3 + 16 * KB
    kp = sb("kp", [P, 2, T], R4)
    w1 = sb("w1", [P, 16, P], R)
    kp2 = sb("kp2", [P, 2, T], R4 + 4 * KB)
    w1v = sb("w1v", [P, 16, P], R + 16 * KB)
    biasC = sb("biasC", [P, T], Y + 10 * KB)
    probsC = [sb("probsC0", [P, 1280], C + 4 * KB), sb("probsC1", [P, 1280], C + 14 * KB), sb("probsC2", [P, 1280], R4)]
    zpad = [sb(f"zpad{j}", [P, TAPS - 1 + T], (Y, R4)[j]) for j in range(2)]
    zc = sb("zc", [P, 4, T], Y + 4 * KB)
    tmp = [sb(f"tmp{j}", [P, T], C + 2 * KB * j) for j in range(8)]
    rs = [sb(f"rs{j}", [P, T], C + 16 * KB + 2 * KB * ((j + 2) % 3)) for j in range(3)]
    C2 = C + 22 * KB
    n_fixed = CONST_AT["maskA"][0]
    cst = sb("cst", [P, n_fixed], C2)
    gn = sb("gn", [P, N_GAIN], C2 + ((n_fixed * 4 + 31) // 32) * 32)
    C3 = C2 + ((n_fixed * 4 + 31) // 32) * 32 + ((N_GAIN * 4 + 31) // 32) * 32
    pos_i = sb("positions", [P, T], Y + 8 * KB, I32)[:, :]
    rope_tmp = [sb(f"rope_tmp{j}", [P, T], Y + 10 * KB + 2 * KB * j) for j in range(3)]
    maskA = sb("maskA", [P, T], R2 + 38 * KB)
    stat = sb("stat", [P, 64], C3)
    gtok = sb("gtok", [P, QT, 24], C3 + 256)
    pC = sb("pC", [P, QT, 64], Y + 8 * KB)
    vcb = [sb(f"vcb{g}", [64, P], Y + 9 * KB + 512 * g) for g in range(2)]
    kcd = sb("kcd", [P, 2, 32], C3 + 640)
    hid = [sb(f"hid{j}", [P, 64], C3 + 896 + 256 * j) for j in range(2)]
    rel = sb("rel", [16, 640], Y)
    end = C3 + 896 + 512
    assert end <= 229344, end
    bias_dram = nc.dram_tensor("bias_scratch", (16, P, T), F32, kind="Internal").ap()
    rel_dram = nc.dram_tensor("rel_scratch", (16, 640), F32, kind="Internal").ap()

    def cc(name, a=0, n=None):
        o, w = CONST_AT[name]
        return cst[:, o + a:o + a + (w if n is None else n)]

    def gg(name, k=0, n=1):
        return gn[:, GAIN_AT[name][0] + k:GAIN_AT[name][0] + k + n]

    def gdyn(name, k):
        if isinstance(k, int):
            return gg(name, k)
        return gn[:, bass.ds(k + GAIN_AT[name][0], 1)]

    ident = cc("ident")
    ones = cc("ones")

    bank = [nc.alloc_psum_tensor(f"bank{j}", [P, T], F32) for j in range(8)]

    sem = lambda n: nc.alloc_semaphore(n)
    START = 4096
    chans = {k: Chan(sem(f"steps_{k}"), 1, START) for k in ("pe", "act", "dve")}
    q = Queue(chans)
    q.pads = {k: sem(f"apart_{k}") for k in chans}
    raw_in = [Chan(sem(f"raw_loaded{j}"), 16) for j in range(2)]
    hi_done = Chan(sem("weight_hi"))
    lo_done = Chan(sem("weight_lo"))
    c_x = [Chan(sem(f"x_loaded{j}"), 16) for j in range(2)]
    c_small = Chan(sem("small_loaded"), 16)
    c_consts = Chan(sem("consts_loaded"), 16)
    c_pos = Chan(sem("positions_loaded"), 16)
    c_rel = Chan(sem("rel_table"), 16)
    c_mask = Chan(sem("masks_loaded"), 16)
    c_bias = [Chan(sem(f"bias_loaded{j}"), 16) for j in range(2)]
    c_w1 = Chan(sem("w1_loaded"), 16)
    c_out = Chan(sem("out_stored"), 16)
    q.extra = raw_in + [c_mask, hi_done, lo_done, c_rel, c_w1, c_out] + c_bias
    free = q.free

    def pe(fn, *w):
        return q.step("pe", fn, *w)

    def act(fn, *w, **k):
        return q.step("act", fn, *w, **k)

    def dve(fn, *w, **k):
        return q.step("dve", fn, *w, **k)

    def func(o, i_, f, *w, scale=1.0, bias=0.0, accum=None):
        def fn(e, i):
            g = lambda a: a(i) if callable(a) else a
            kw = {} if accum is None else {"accum_out": accum}
            return e.activation(g(o), g(i_), f, bias=g(bias), scale=g(scale), **kw)
        return act(fn, *w, apart=callable(o) or callable(i_) or callable(scale) or callable(bias))

    def tt(o, a, b, op, *w):
        g = lambda v, i: v(i) if callable(v) else v
        return dve(lambda e, i: e.tensor_tensor(g(o, i), g(a, i), g(b, i), op), *w)

    def stt(o, a, s, b, op0, op1, *w):
        g = lambda v, i: v(i) if callable(v) else v
        return dve(lambda e, i: e.scalar_tensor_tensor(g(o, i), g(a, i), g(s, i), g(b, i), op0, op1), *w)

    def ts(o, a, s1, s2, op0, op1, *w):
        g = lambda v, i: v(i) if callable(v) else v
        if s2 is None:
            return dve(lambda e, i: e.tensor_scalar(g(o, i), g(a, i), g(s1, i), None, op0), *w)
        return dve(lambda e, i: e.tensor_scalar(g(o, i), g(a, i), g(s1, i), g(s2, i), op0, op1), *w)

    def round_unit(j, used):
        if q.loop is None and hi_done.count == n_units:
            return
        loaded = q.tick(raw_in[j])
        act(lambda e, i: e.activation(whi[j][:, :], raw[j][:, :], ACT.Copy), loaded, used, chan=hi_done)

    unit_no = [0]

    def use_unit(parts):
        j = unit_no[0] % 2
        unit_no[0] += 1
        ready = q.tick(lo_done)
        evs = []
        for bk, terms, first, last, waits in parts:
            def fn(e, i, bk=bk, terms=(), begin=False, end=False):
                g = lambda v: v(i) if callable(v) else v
                o = bank[bk][:, :]
                for n, (blk, h, l) in enumerate(terms):
                    wh = whi[j][:, blk * P:(blk + 1) * P]
                    wl = wlo[j][:, blk * P:(blk + 1) * P]
                    e.matmul(o, wh, g(h), start=begin and n == 0, stop=False)
                    e.matmul(o, wh, g(l), start=False, stop=False)
                    mm = e.matmul(o, wl, g(h), start=False, stop=end and n == len(terms) - 1)
                return mm
            if isinstance(waits, Tiles):
                war = free.get(f"b{bk}")
                for n, term in enumerate(terms):
                    ev = pe(lambda e, i, fn=fn, term=term, n=n, N=len(terms): fn(
                        e, i, terms=(term,), begin=n == 0, end=n == N - 1), ready, waits.before(n), war)
                    waits.after(n)
            elif isinstance(waits, dict):
                for n, term in enumerate(terms):
                    ev = pe(lambda e, i, fn=fn, term=term, n=n, N=len(terms): fn(
                        e, i, terms=(term,), begin=first and n == 0, end=last and n == N - 1), ready, waits[n])
            else:
                ev = pe(lambda e, i, fn=fn, terms=terms, first=first, last=last: fn(
                    e, i, terms=terms, begin=first, end=last), ready, waits)
            evs.append(ev)
        round_unit(j, evs[-1])
        return evs

    def project(bk, hbuf, lbuf, ks, *waits):
        if waits and isinstance(waits[0], Tiles):
            return use_unit([(bk, [(k, hbuf(k), lbuf(k)) for k in range(ks)], True, True, waits[0])])[0]
        return use_unit([(bk, [(k, hbuf(k), lbuf(k)) for k in range(ks)], True, True,
                          {k: [w, free.get(f"b{bk}")] for k, w in waits[0].items()} if waits and isinstance(waits[0], dict)
                          else list(waits) + [free.get(f"b{bk}")])])[0]

    def in_halves(bk, hbuf, lbuf):
        j = unit_no[0] % 2
        unit_no[0] += 1
        ready = q.tick(lo_done)

        def half(ks, *waits):
            def fn(e, i):
                for k in ks:
                    wh, wl = (w_[j][:, k * P:(k + 1) * P] for w_ in (whi, wlo))
                    e.matmul(bank[bk][:, :], wh, hbuf(k), start=k == 0, stop=False)
                    e.matmul(bank[bk][:, :], wh, lbuf(k), start=False, stop=False)
                    mm = e.matmul(bank[bk][:, :], wl, hbuf(k), start=False, stop=k == KD - 1)
                return mm
            return pe(fn, *waits)

        def second():
            mm = half(range(KD // 2, KD))
            round_unit(j, mm)
            return mm
        return lambda: half(range(KD // 2), ready, free.get(f"b{bk}")), second

    H = (lambda k: hh[:, k, :]), (lambda k: hl[:, k, :])
    H2 = (lambda k: h2h[:, k, :]), (lambda k: h2l[:, k, :])
    O = (lambda k: oh[:, k, :]), (lambda k: ol[:, k, :])

    sq_turn = [0]

    def square(src, ready):
        s = sq_turn[0] % 2
        sq_turn[0] += 1
        return s, func(tmp[s][:, :], src, ACT.Square, ready, free.get(f"tmp{s}"))

    def sum_square(sq, bk, first, last):
        s, ev = sq
        mm = pe(lambda e, i: e.matmul(bank[bk][:, :], ones, tmp[s][:, :], start=first, stop=last), ev,
                free.get(f"b{bk}") if first else None)
        free[f"tmp{s}"] = mm
        return mm

    def add_square(src, bk, first, last, ready):
        return sum_square(square(src, ready), bk, first, last)

    def add_plain(src, bk, first, last, ready):
        return pe(lambda e, i: e.matmul(bank[bk][:, :], ones, src, start=first, stop=last), ready,
                  free.get(f"b{bk}") if first else None)

    def inv_rms(dst, bk, n, summed):
        name = f"rs{rs.index(dst)}"
        a = ts(dst[:, :], bank[bk][:, :], 1.0 / n, EPS, ALU.mult, ALU.add, summed, free.get(name))
        free[f"b{bk}"] = a
        b = func(dst[:, :], dst[:, :], ACT.Sqrt, a)
        return dve(lambda e, i: e.reciprocal(dst[:, :], dst[:, :]), b)

    def split(src, hi, lo, ready, gain=None, war=None, between=None):
        a = func(hi, src, ACT.Copy, ready, war, scale=1.0 if gain is None else gain)
        if between:
            between()
        if gain is None:
            return tt(lo, src, (lambda i: hi(i).bitcast(F32)) if callable(hi) else hi.bitcast(F32), ALU.subtract, a, war)
        return stt(lo, src, gain, hi.bitcast(F32), ALU.mult, ALU.subtract, a, war)

    def rope_steps():
        TWO_PI = 2 * np.pi
        c1 = float(np.float32(6.28125))
        c2 = float(np.float32(np.round((TWO_PI - c1) * 2 ** 21) / 2 ** 21))
        c3 = float(np.float32(TWO_PI - c1 - c2))
        MAGIC = 1.5 * 2.0 ** 23
        PI32 = 3.1415925
        ang, kk_, rr = rope_tmp
        e_ = dve(lambda e, i: e.tensor_copy(ang[:, :], pos_i), EV_pos, SM)
        yield e_
        e_ = ts(ang[:, :], ang[:, :], cc("inv"), None, ALU.mult, None, e_)
        yield e_
        for dst, shift in ((sinT, 0.0), (cosT, 0.25)):
            e_ = ts(kk_[:, :], ang[:, :], float(1.0 / TWO_PI), shift, ALU.mult, ALU.add, e_)
            yield e_
            e_ = ts(kk_[:, :], kk_[:, :], MAGIC, None, ALU.add, None, e_)
            yield e_
            e_ = ts(kk_[:, :], kk_[:, :], -MAGIC, None, ALU.add, None, e_)
            yield e_
            e_ = stt(rr[:, :], kk_[:, :], -c1, ang[:, :], ALU.mult, ALU.add, e_)
            yield e_
            e_ = stt(rr[:, :], kk_[:, :], -c2, rr[:, :], ALU.mult, ALU.add, e_)
            yield e_
            e_ = stt(rr[:, :], kk_[:, :], -c3, rr[:, :], ALU.mult, ALU.add, e_)
            yield e_
            if shift:
                e_ = ts(rr[:, :], rr[:, :], float(np.pi / 2), None, ALU.add, None, e_)
            e_ = ts(rr[:, :], rr[:, :], PI32, -PI32, ALU.min, ALU.max, e_)
            yield e_
            e_ = func(dst[:, :], rr[:, :], ACT.Sin, e_)
            yield e_
        yield ts(sinT[:, :], sinT[:, :], cc("sgn"), None, ALU.mult, None, e_)

    EV_mask = q.tick(c_mask)
    EV_small, EV_const, EV_pos = q.tick(c_small), q.tick(c_consts), q.tick(c_pos)
    EV_x = [q.tick(c_x[0]), q.tick(c_x[1])]
    SM = (EV_small, EV_const)
    table_steps = rope_steps()
    round_unit(0, None)
    rs_main, squares = [], {}

    def before_x(k):
        if k == 4:
            round_unit(1, None)
        xe = EV_x[k // 4]
        ev = split(x[:, k, :], hh[:, k, :], hl[:, k, :], (xe, SM), gg("pre0", k))
        squares[k] = square(x[:, k, :], xe)
        return ev

    def after_x(k):
        ssq = sum_square(squares[k], 7, k == 0, k == KD - 1)
        for _ in range(2):
            next(table_steps)
        if k == KD - 1:
            rs_main.append(inv_rms(rs[0], 7, D, ssq))

    def rope(src, dst, swap, ready, war):
        evs = []
        for a in range(4):
            b = a ^ 1
            evs.append(func(swap[32 * a:32 * a + 32, :], src[32 * b:32 * b + 32, :], ACT.Copy,
                            ready, free.get("swap")))
        a_ = tt(swap[:, :], swap[:, :], sinT[:, :], ALU.mult, evs, rope_ready)
        b_ = tt(src[:, :], src[:, :], cosT[:, :], ALU.mult, ready, evs)
        c_ = tt(dst[:, :], src[:, :], swap[:, :], ALU.add, a_, b_, war)
        free["swap"] = c_
        return c_

    lat, waiting, rope_ready = [], None, None
    for m in range(5):
        bk = m % 3
        mm = project(bk, *H, KD, Tiles(before_x, after_x) if m == 0 else None)
        if waiting:
            sqm = sum_square(*waiting)
        if m == 3:
            rs_q = inv_rms(rs[1], 6, QL, sqm)
        tb = 2 + m % 4
        v = tt(tmp[tb][:, :], bank[bk][:, :], rs[0][:, :], ALU.mult, mm, rs_main, free.get(f"tmp{tb}"))
        free[f"b{bk}"] = v
        g = gg("gq", m) if m < 3 else gg("gkv", m - 3)
        s = split(tmp[tb][:, :], cqh[:, m, :], cql[:, m, :], v, g)
        sq = square(tmp[tb][:, :], v)
        waiting = (sq, 6 if m < 3 else 7, m in (0, 3), m in (2, 4))
        free[f"tmp{tb}"] = (s, sq[1])
        lat.append(s)
        for _ in range(2):
            rope_ready = next(table_steps, rope_ready)
    rel_ev = Event(c_rel, None, 1)
    c_rel.count = 1
    r1 = ts(rel[:, 255:575], rel[:, 255:575], float(CHUNK) ** 0.5, None, ALU.mult, None, rel_ev)
    r2 = dve(lambda e, i: e.tensor_copy(rel[:, 0:255], rel[:, 255:256].to_broadcast([16, 255])), r1)
    r3 = dve(lambda e, i: e.tensor_copy(rel[:, 575:640], rel[:, 574:575].to_broadcast([16, 65])), r1)
    rel_out = q.step("act", lambda e, i: e.dma_start(rel_dram, rel[:, :]), r2, r3, chan=c_rel)
    free["PT"] = rel_out
    free["vtmp"] = None
    mm = project(0, *H, KD)
    h_read = mm
    kv_sum = sum_square(*waiting)

    SPOT = {0: (0, 0), 2: (0, 128), 1: (1, 0), 3: (2, 0)}
    ORDER = (0, 2, 1, 3)
    PO = {0: 0, 1: 128, 2: 384, 3: 768}
    W = lambda t: (t + 1) * P

    def scores(pieces, *ready, among=None):
        evs = {}
        for b, tiles in ((0, (0, 2)), (1, (1,)), (2, (3,))):
            if among and b < 2:
                among[b]()
            def fn(e, i, b=b, tiles=tiles):
                for t in tiles:
                    for n, (qf, kf) in enumerate(pieces):
                        mm = e.matmul(bank[b][:, SPOT[t][1]:SPOT[t][1] + W(t)], qf(t), kf(W(t)),
                                      start=n == 0, stop=n == len(pieces) - 1)
                return mm
            ev = pe(fn, ready, free.get(f"b{b}"))
            for t in tiles:
                evs[t] = ev
        return evs

    def bias_and_min(evs, pb, st, bias, scale, *ready):
        out = {}
        for t in ORDER:
            b, c = SPOT[t]
            out[t] = dve(lambda e, i, t=t, b=b, c=c: e.tensor_tensor_reduce(
                out=pb[:, PO[t]:PO[t] + W(t)], in0=bank[b][:, c:c + W(t)], in1=bias[:, T - W(t):T],
                scale=-scale, scalar=HUGE, op0=ALU.add, op1=ALU.min,
                accum_out=stat[:, st + t:st + t + 1]), evs[t], ready, free.get(pb.name), apart=True)
            free[f"b{b}"] = out[t]
        return out

    def exponent(evs, pb, st):
        out = {}
        for t in ORDER:
            r = pb[:, PO[t]:PO[t] + W(t)]
            out[t] = func(r, r, ACT.Exp, evs[t], free.get(f"sum{st}"), scale=-1.0, bias=stat[:, st + t:st + t + 1],
                          accum=stat[:, st + 4 + t:st + 5 + t])
        return list(out.values())

    def normalise(evs, pb, st, gate=None, gate_ready=None):
        s = stat[:, st + 4:st + 8]
        r = stat[:, st + 8:st + 12]
        a = dve(lambda e, i: e.reciprocal(r, s), evs)
        free[f"sum{st}"] = a
        if gate is not None:
            a = tt(r, r, gate, ALU.mult, a, gate_ready)
        out = {}
        for t in ORDER:
            v = pb[:, PO[t]:PO[t] + W(t)]
            out[t] = ts(v, v, stat[:, st + 8 + t:st + 9 + t], None, ALU.mult, None, a)
        return out

    tr_turn = [0]
    tr_banks = [5, 6]

    def transposes(evs, pb):
        out = []
        halves = [lambda: transpose_tiles(ORDER[:2], evs, pb, out), lambda: transpose_tiles(ORDER[2:], evs, pb, out)]
        return halves, out

    def transpose_tiles(tiles, evs, pb, out):
        for t in tiles:
            b = tr_banks[tr_turn[0] % len(tr_banks)]
            tr_turn[0] += 1

            def fn(e, i, t=t, b=b):
                for k in range(t + 1):
                    mm = e.transpose(bank[b][:, k * P:(k + 1) * P], pb[:, PO[t] + k * P:PO[t] + (k + 1) * P], ident)
                return mm
            mm = pe(fn, evs[t], free.get(f"b{b}"))
            ev = func(PT[:, 0:t + 1, t * P:(t + 1) * P],
                      bank[b][:, 0:W(t)].rearrange("p (k c) -> p k c", c=P), ACT.Copy, mm, free.get("PT"))
            free[f"b{b}"] = ev
            out.append(ev)
        free[pb.name] = mm

    def times_v(vf, rows, ready, first=True, last=True, war=None):
        def fn(e, i):
            for k in range(QT):
                mm = e.matmul(bank[7][rows[0]:rows[1], k * P:T], vf(k), PT[:, k, k * P:T],
                              start=first and k == 0, stop=last and k == QT - 1, skip_group_check=not (first and last))
            return mm
        ev = pe(fn, ready, war)
        free["PT"] = ev
        return ev

    def token_major(src, dst, ready, war):
        b = tr_banks[tr_turn[0] % len(tr_banks)]
        tr_turn[0] += 1

        def fn(e, i):
            for t in range(QT):
                mm = e.transpose(bank[b][:, t * P:(t + 1) * P], src[:, t * P:(t + 1) * P], ident)
            return mm
        mm = pe(fn, ready, free.get(f"b{b}"))
        ev = func(dst[:, :, :], bank[b][:, :].rearrange("p (k c) -> p k c", c=P), ACT.Copy, mm, war)
        free[f"b{b}"] = ev
        return mm, ev

    def scaled(bk, r, dst, mm, rready, war):
        ev = tt(dst, bank[bk][:, :], r[:, :], ALU.mult, mm, rready, war)
        free[f"b{bk}"] = ev
        return ev

    CQ = lambda k: cqh[:, k, :]
    CL = lambda k: cql[:, k, :]

    def mla_unit(which, p):
        b = p % 2
        ev = {}

        def part(bk, blk, c0, n):
            return (bk, [(blk + k, CQ(c0 + k), CL(c0 + k)) for k in range(n)], True, True,
                    [free.get(f"b{bk}"), lat])
        war = free.get(f"pair{b}")
        if which == 0:
            m0, m1 = use_unit([part(3, 0, 0, 3), part(4, 3, 0, 3)])
            ev["qn0"] = scaled(3, rs[1], qn[b][0][:, :], m0, rs_q, (war, h_read))
            ev["qn1"] = scaled(4, rs[1], qn[b][1][:, :], m1, rs_q, war)
        elif which == 1:
            m0, m1 = use_unit([part(3, 0, 0, 3), part(4, 3, 3, 2)])
            a = scaled(3, rs[1], tmp[6][:, :], m0, rs_q, free.get("tmp6"))
            ev["kn0"] = scaled(4, rs[2], kn[b][0][:, :], m1, rs_kv, war)
            ev["qr"] = rope(tmp[6], qr[b], swapA, a, war)
            free["tmp6"] = ev["qr"]
        else:
            mla_last_unit(b, war, ev)
        return ev

    def mla_last_unit(b, war, ev):
        j = unit_no[0] % 2
        unit_no[0] += 1
        ready = q.tick(lo_done)

        def grp(bk, blk):
            def fn(e, i):
                for n in range(2):
                    wh, wl = (w_[j][:, (blk + n) * P:(blk + n + 1) * P] for w_ in (whi, wlo))
                    o = bank[bk][:, :]
                    e.matmul(o, wh, CQ(3 + n), start=n == 0, stop=False)
                    e.matmul(o, wh, CL(3 + n), start=False, stop=False)
                    mm = e.matmul(o, wl, CQ(3 + n), start=False, stop=n == 1)
                return mm
            return fn
        m0 = pe(grp(3, 0), ready, free.get("b3"), lat)
        m1 = pe(grp(4, 2), ready, free.get("b4"))
        ev["kn1"] = scaled(3, rs[2], kn[b][1][:, :], m0, rs_kv, war)
        m2 = pe(grp(3, 4), free.get("b3"))
        round_unit(j, m2)
        v0 = scaled(4, rs[2], vtmp[:, :], m1, rs_kv, free.get("vtmp"))
        t0, ev["v0"] = token_major(vtmp, vA[b][0], v0, war)
        v1 = scaled(3, rs[2], tmp[7][:, :], m2, rs_kv, free.get("tmp7"))
        free["vtmp"] = t0
        t1, ev["v1"] = token_major(tmp[7], vA[b][1], v1, war)
        free["tmp7"] = t1

    SCALE_A = float(NOPE + ROPE) ** -0.5
    v = tt(tmp[6][:, :], bank[0][:, :], rs[0][:, :], ALU.mult, h_read, rs_main)
    free["b0"] = v
    kr_ready = rope(tmp[6], krope, swapA, v, None)
    free["tmp6"] = kr_ready
    nxt = mla_unit(0, 0)
    rs_kv = inv_rms(rs[2], 7, KVL, kv_sum)
    for w_ in range(1, 3):
        nxt.update(mla_unit(w_, 0))


    def mla_scores(p, e_, cur, among=None):
        b = p % 2
        rows = slice(64 * e_, 64 * e_ + 64)
        s_ = scores([(lambda t: qn[b][e_][:, t * P:(t + 1) * P], lambda w: kn[b][e_][:, 0:w]),
                     (lambda t: qr[b][rows, t * P:(t + 1) * P], lambda w: krope[rows, 0:w])],
                    cur[f"qn{e_}"], cur[f"kn{e_}"], cur["qr"], kr_ready, among=among)
        return exponent(bias_and_min(s_, probsA[e_], 16 * e_, maskA, SCALE_A, EV_mask), probsA[e_], 16 * e_)

    def mla_pair(p, cur, a0):
        b, nxt = p % 2, {}
        more = p + 1 < HEADS_A // 2
        n0 = normalise(a0, probsA[0], 0)
        if more:
            nxt.update(mla_unit(0, p + 1))
        t0, t0_out = transposes(n0, probsA[0])
        a1 = mla_scores(p, 1, cur, among=t0)
        n1 = normalise(a1, probsA[1], 16)
        if more:
            nxt.update(mla_unit(1, p + 1))
        v0 = times_v(lambda k: vA[b][0][:, k, :], (0, P), (t0_out, cur["v0"]), war=free.get("b7"))
        t1, t1_out = transposes(n1, probsA[1])
        t1[0]()
        o0 = split(bank[7][:, :], oh[:, 2 * p, :], ol[:, 2 * p, :], v0)
        free["b7"] = o0
        if more:
            nxt.update(mla_unit(2, p + 1))
        t1[1]()
        a0 = mla_scores(p + 1, 0, nxt) if more else None
        v1 = times_v(lambda k: vA[b][1][:, k, :], (0, P), (t1_out, cur["v1"]), war=free.get("b7"))
        o1 = split(bank[7][:, :], oh[:, 2 * p + 1, :], ol[:, 2 * p + 1, :], v1)
        free["b7"] = o1
        free[f"pair{b}"] = v1
        return nxt, a0, (o0, o1), v1

    a0 = mla_scores(0, 0, nxt)
    shifted = bass.AP(tensor=rel_dram.tensor, offset=P - 1, ap=[[640, 16], [-1, P], [1, T]])
    rel_out = q.step("act", lambda e, i: e.dma_start(bias_dram, shifted), rel_out, chan=c_rel)

    for p in range(HEADS_A // 2):
        nxt, a0, attn_done, mixer_read = mla_pair(p, nxt, a0)

    to_add = []

    def gather_square(src, first, ready):
        add_gathered()
        if first:
            free["total"] = func(tmp[7][:, :], src, ACT.Square, ready, free.get("tmp7"))
        else:
            to_add.append(square(src, ready))

    def add_gathered():
        while to_add:
            sl, a = to_add.pop()
            free["total"] = free[f"tmp{sl}"] = tt(tmp[7][:, :], tmp[7][:, :], tmp[sl][:, :], ALU.add, a, free["total"])

    def sum_total(bk, first, last):
        add_gathered()
        mm = pe(lambda e, i: e.matmul(bank[bk][:, :], ones, tmp[7][:, :], start=first, stop=last),
                free["total"], free.get(f"b{bk}") if first else None)
        free["tmp7"] = mm
        return mm

    def keep_clock(n):
        for _ in range(n):
            pe(lambda e, i: e.matmul(bank[5][:, :], ones, cst[:, 0:T], start=True, stop=True), free.get("b5"))

    def inv_rms_per_token(last_tile, ready):
        sums, r = bank[7][:, 0:QT], stat[:, 12:12 + QT]
        func(stat[:, 28:29], cc("eps"), ACT.Sqrt)
        sl, sq_ev = square(last_tile, ready)
        add_gathered()

        def column_sums(src, first):
            def fn(e, i):
                for t in range(QT):
                    mm = e.matmul(bank[7][:, t:t + 1], src[:, t * P:(t + 1) * P], ones[:, 0:1], start=first and t == 0,
                                  stop=not first and t == QT - 1, skip_group_check=True)
                return mm
            return fn
        keep_clock(2)
        mm = pe(column_sums(tmp[7], True), free["total"], free.get("b7"))
        mm = pe(column_sums(tmp[sl], False), sq_ev)
        free[f"tmp{sl}"] = mm
        keep_clock(2)
        a = func(r, sums, ACT.Sqrt, mm, scale=1.0 / D, bias=cc("eps"))
        b_ = dve(lambda e, i: e.reciprocal(r, r), a)
        c_ = tt(tmp[7][:, :].rearrange("p (t c) -> p t c", t=QT), ident.unsqueeze(1).to_broadcast([P, QT, P]),
                r.unsqueeze(2).to_broadcast([P, QT, P]), ALU.mult, b_, mm)
        mm = pe(lambda e, i: e.matmul(bank[7][:, :], ones, tmp[7][:, :], start=True, stop=True), c_, a)
        free["tmp7"] = mm
        keep_clock(2)
        return mm

    def out_tiles(inp, ks, in_ready, y_war):
        evs = []
        for m in range(KD):
            bk = m % 2
            mm = project(bk, *inp, ks, in_ready if m == 0 else None)
            ev = dve(lambda e, i, m=m, bk=bk: e.tensor_copy(y[:, m, :], bank[bk][:, :]), mm, y_war)
            free[f"b{bk}"] = ev
            if m < KD - 1:
                gather_square(y[:, m, :], m == 0, ev)
            evs.append(ev)
        return evs, inv_rms_per_token(y[:, KD - 1, :], ev)

    def join(evs, inv_ready, post, nexts):
        inv, squares, joined = [], {}, {}

        def join_tile(k):
            if k == KD:
                return
            tb = 2 + k % 4
            a = tt(tmp[tb][:, :], y[:, k, :], bank[7][:, :], ALU.mult, inv_ready, evs[k], free.get(f"tmp{tb}"))
            joined[k] = stt(x[:, k, :], tmp[tb][:, :], gg(post, k), x[:, k, :], ALU.mult, ALU.add, a)
            free[f"tmp{tb}"], free["b7"] = joined[k], a

        def before(k):
            if k == 0:
                join_tile(0)
            g, hi, lo, war = nexts[0]
            ev = split(x[:, k, :], hi[:, k, :], lo[:, k, :], joined[k], gg(g, k), war, lambda: join_tile(k + 1))
            squares[k] = square(x[:, k, :], joined[k])
            return [ev]

        def after(k):
            ssq = sum_square(squares[k], 6, k == 0, k == KD - 1)
            if k == KD - 1:
                inv.append(inv_rms(rs[0], 6, D, ssq))

        def before_second(k):
            g, hi, lo, war = nexts[1]
            return split(x[:, k, :], hi[:, k, :], lo[:, k, :], joined[k], gg(g, k), war)
        return Tiles(before, after), inv, Tiles(before_second, lambda k: None)

    def gate_up(idx, bks, ready, inv, conv):
        evs = []
        for r in range(2):
            mm = project(bks[r], *H, KD, ready if r == 0 else None)
            u, acc = tmp[2 + r], tmp[4 + r]
            ev = tt(u[:, :], bank[bks[r]][:, :], rs[0][:, :], ALU.mult, mm, inv, free.get(f"tmp{2 + r}"))
            free[f"b{bks[r]}"] = ev
            if conv:
                w3 = lambda i, tap, r=r: gdyn("fdw", idx(i) * 3 + (r * 3 * KF + tap))
                a = func(acc[:, :], u[:, :], ACT.Identity, ev, free.get(f"tmp{4 + r}"), scale=lambda i, w3=w3: w3(i, 2),
                         bias=lambda i, r=r: gdyn("fdwb", idx(i) + r * KF))
                b_ = stt(acc[:, 1:T], u[:, 0:T - 1], lambda i, w3=w3: w3(i, 1), acc[:, 1:T], ALU.mult, ALU.add, a)
                ev = stt(acc[:, 2:T], u[:, 0:T - 2], lambda i, w3=w3: w3(i, 0), acc[:, 2:T], ALU.mult, ALU.add, b_)
                free[f"tmp{2 + r}"] = ev
            evs.append(ev)
        g_, u_ = (tmp[4], tmp[5]) if conv else (tmp[2], tmp[3])
        sil = func(g_[:, :], g_[:, :], ACT.Silu, evs[0])
        prod = tt(u_[:, :], u_[:, :], g_[:, :], ALU.mult, sil, evs[1])
        hi = dve(lambda e, i: e.tensor_scalar(tile_of(fh, idx(i)), u_[:, :], 1.0, None, ALU.mult), prod)
        lo = tt(lambda i: tile_of(fl, idx(i)), u_[:, :], lambda i: tile_of(fh, idx(i)).bitcast(F32), ALU.subtract, hi)
        n1, n2 = ("tmp4", "tmp5") if conv else ("tmp2", "tmp3")
        free[n1], free[n2] = prod, lo
        return lo

    def feed_forward(ready, inv, conv):
        gate_up(lambda i: 0, (2, 3), ready, inv, conv)
        q.start_loop(KF - 1)
        hid_ready = gate_up(lambda i: i + 1, (0, 1), None, inv, conv)
        q.end_loop()
        chan, loop = hid_ready.chan, hid_ready.loop
        most_ready = Event(chan, loop, hid_ready.n - loop.per[chan])
        evs = []
        res = x if conv else y

        def down_unit(half, base, first, last):
            parts = []
            if last:
                order = [(r, m) for m in range(4) for r in range(2)]
            else:
                order = [(r, m) for r in range(2) for m in (2, 3, 0, 1)]
            for r, m in order:
                bk = 4 * half + m
                h_ = lambda i, r=r: tile_of(fh, base(i) + r)
                l_ = lambda i, r=r: tile_of(fl, base(i) + r)
                parts.append((bk, [(4 * r + m, h_, l_)], first and r == 0, last and r == 1,
                              [hid_ready if last else most_ready] + ([free.get(f"b{bk}")] if first and r == 0 else [])))
            return use_unit(parts)

        for half in range(2):
            down_unit(half, lambda i: 0, True, False)
            q.start_loop(KF // 4 - 1)
            down_unit(half, lambda i: i * 4 + 2, False, False)
            down_unit(half, lambda i: i * 4 + 4, False, False)
            q.end_loop()
            down_unit(half, lambda i: KF - 4, False, False)
            ms = down_unit(half, lambda i: KF - 2, False, True)[1::2]
            for m in range(4):
                mi = 4 * half + m
                if conv:
                    ev = tt(x[:, mi, :], bank[mi][:, :], x[:, mi, :], ALU.add, ms[m])
                else:
                    ev = dve(lambda e, i, mi=mi: e.tensor_copy(y[:, mi, :], bank[mi][:, :]), ms[m])
                free[f"b{mi}"] = ev
                evs.append(ev)
                if mi < KD - 1:
                    gather_square(res[:, mi, :], mi == 0, ev)
            if not half:
                add_gathered()
        return evs, inv_rms_per_token(res[:, KD - 1, :], ev)

    evs, ssq = out_tiles(O, KD, [attn_done, mixer_read], mixer_read)
    ready, inv, _ = join(evs, ssq, "post0", [("fpre0", hh, hl, None)])
    evs, ssq = feed_forward(ready, inv, False)
    ready, inv, ready2 = join(evs, ssq, "fpost0", [("kvsrc", hh, hl, None), ("pre1", h2h, h2l, evs[-1])])

    def load_bias(e_, idx):
        def fn(e, i):
            return e.dma_start(biasB[e_][:, :], bias_dram[one(idx(i)), :, :].rearrange("a p t -> p (a t)"))
        return q.step("act", fn, free.get(f"biasB{e_}"), rel_out, chan=c_bias[e_])

    def add_mask(e_, loaded):
        return ts(biasB[e_][0:CHUNK, T - CHUNK:T], biasB[e_][0:CHUNK, T - CHUNK:T], 0.0, MASKED, ALU.mult, ALU.add, loaded)

    def b_unit(which, b, first=None, bk=3):
        war = free.get(f"pair{b}")
        ev = {}
        if which == 0:
            mm = project(bk, *H, KD, first)
            ev["vtmp"] = scaled(bk, rs[0], vtmp[:, :], mm, inv, free.get("vtmp"))
        elif which == 1:
            mm = project(bk, *H, KD)
            ev["k"] = scaled(bk, rs[0], kB[b][:, :], mm, inv, war)
        else:
            mm = project(bk, *H2, KD, first)
            ev["q"] = scaled(bk, rs[0], qB[b][:, :], mm, inv, war)
        return ev

    def b_values(b, ev):
        free["vtmp"], ev["v"] = token_major(vtmp, vB[b], ev["vtmp"], free.get(f"pair{b}"))

    SCALE_B = 64.0 ** -0.5

    def b_scores(b, e_, cur, loaded, among=None):
        r = slice(64 * e_, 64 * e_ + 64)
        bias_ev = add_mask(e_, loaded)
        s_ = scores([(lambda t: qB[b][r, t * P:(t + 1) * P], lambda w: kB[b][r, 0:w])], cur["q"], cur["k"], among=among)
        m_ = bias_and_min(s_, probsB[e_], 16 * e_, biasB[e_], SCALE_B, bias_ev)
        free[f"biasB{e_}"] = m_[ORDER[-1]]
        return exponent(m_, probsB[e_], 16 * e_)

    def b_pair(b, pidx, cur, more):
        nx = {}
        load1 = load_bias(1, lambda i: pidx(i) * 2 + 1)
        n0 = normalise(cur["a0"], probsB[0], 0)
        if more:
            load0 = load_bias(0, lambda i: pidx(i) * 2 + 2)
            nx.update(b_unit(0, 1 - b))
        t0, t0_out = transposes(n0, probsB[0])
        a1 = b_scores(b, 1, cur, load1, among=t0)
        n1 = normalise(a1, probsB[1], 16)
        if more:
            b_values(1 - b, nx)
            nx.update(b_unit(1, 1 - b))
        v0 = times_v(lambda k: vB[b][:, k, 0:64], (0, 64), (t0_out, cur["v"]), war=free.get("b7"))
        t1, t1_out = transposes(n1, probsB[1])
        t1[0]()
        if more:
            nx.update(b_unit(2, 1 - b))
        t1[1]()
        if more:
            nx["a0"] = b_scores(1 - b, 0, nx, load0)
        v1 = times_v(lambda k: vB[b][:, k, 64:128], (64, 128), t1_out)
        free[f"pair{b}"] = v1
        hi = dve(lambda e, i: e.tensor_scalar(tile_of(oh, pidx(i)), bank[7][:, :], 1.0, None, ALU.mult), v1)
        lo = tt(lambda i: tile_of(ol, pidx(i)), bank[7][:, :], lambda i: tile_of(oh, pidx(i)).bitcast(F32),
                ALU.subtract, hi)
        free["b7"] = lo
        return nx, lo

    tr_banks.insert(0, 4)
    cur = {}
    for w_ in range(3):
        cur.update(b_unit(w_, 0, (ready, None, ready2)[w_], (3, 0, 1)[w_]))
        if w_ == 0:
            free["biasB0"] = free["biasB1"] = inv
            load0 = load_bias(0, lambda i: 0)
    b_values(0, cur)
    cur["a0"] = b_scores(0, 0, cur, load0)
    for k_ in ("pair0", "pair1"):
        free[k_] = None
    CARRIED_B = ("q", "k", "v", "a0")
    for k_ in CARRIED_B:
        free["B_" + k_] = cur[k_]
    q.start_loop(PAIRS_B // 2 - 1)
    cur = {k_: free["B_" + k_] for k_ in CARRIED_B}
    nx, _ = b_pair(0, lambda i: i * 2, cur, True)
    nx2, _ = b_pair(1, lambda i: i * 2 + 1, nx, True)
    for k_ in CARRIED_B:
        free["B_" + k_] = nx2[k_]
    q.end_loop()
    cur = {k_: free["B_" + k_] for k_ in CARRIED_B}
    nx, _ = b_pair(0, lambda i: PAIRS_B - 2, cur, True)
    _, o_done = b_pair(1, lambda i: PAIRS_B - 1, nx, False)

    tr_banks.remove(4)
    evs, ssq = out_tiles(O, KD, [o_done], free["pair1"])
    ready, inv, _ = join(evs, ssq, "post1", [("fpre1", hh, hl, free["pair1"])])
    evs, ssq = feed_forward(ready, inv, False)
    ready, inv, _ = join(evs, ssq, "fpost1", [("norm1", hh, hl, None)])

    mm = project(4, *H, KD, ready)
    g = scaled(4, rs[0], tmp[7][:, :], mm, inv, free.get("tmp7"))

    zero_ev = [dve(lambda e, i, j=j: e.memset(zpad[j][:, 0:TAPS - 1], 0.0), evs, inv) for j in range(2)]
    def gate_unit(idx, bk):
        return gate_sigmoid(idx, bk, project(bk, *H, KD))

    def gate_sigmoid(idx, bk, mm):
        gi = lambda i: tile_of(gsig, idx(i))
        b_ = tt(gi, bank[bk][:, :], rs[0][:, :], ALU.mult, mm)
        free[f"b{bk}"] = b_
        return func(gi, gi, ACT.Sigmoid, b_)

    w1_both = [q.step("act", lambda e, i, buf=buf, n=n: e.dma_start(buf[:, :, :], w1_in[n]), evs, chan=ch)
               for n, (buf, ch) in enumerate(((w1, c_w1), (w1v, c_mask)))]
    q.start_loop(2)
    for half in range(2):
        cidx = lambda i, half=half: i * 2 + half
        zp = zpad[half]
        mm = project(0, *H, KD)
        a = tt(tmp[2][:, :], bank[0][:, :], rs[0][:, :], ALU.mult, mm, inv, free.get("tmp2"))
        free["b0"] = a
        mm = project(1, *H, KD)
        g = tt(tmp[3][:, :], bank[1][:, :], rs[0][:, :], ALU.mult, mm, free.get("tmp3"))
        free["b1"] = g
        s = func(tmp[3][:, :], tmp[3][:, :], ACT.Sigmoid, g)
        z = tt(zp[:, TAPS - 1:TAPS - 1 + T], tmp[2][:, :], tmp[3][:, :], ALU.mult, a, s, zero_ev, free.get(f"zpad{half}"))
        free["tmp2"] = free["tmp3"] = z
        taps = list(range(TAPS))
        wt = lambda i, tap, cidx=cidx: gdyn("dw", cidx(i) * TAPS + tap)
        o = lambda i, cidx=cidx: tile_of(zc, cidx(i))
        sums = [tmp[4][:, :], tmp[5][:, :]]
        w_ = [free.get("tmp4"), free.get("tmp5")]
        evs_ = [ts(sums[0], zp[:, 0:T], lambda i, wt=wt: wt(i, 0), lambda i, cidx=cidx: gdyn("dwb", cidx(i)),
                   ALU.mult, ALU.add, z, w_),
                ts(sums[1], zp[:, 1:1 + T], lambda i, wt=wt: wt(i, 1), None, ALU.mult, None, z, w_)]
        done = 2
        for j in range(3):
            free["gsig"] = gate_unit(lambda i, cidx=cidx, j=j: cidx(i) * 3 + j, 2 + j % 2)
            for _ in range((9, 10, 10)[j]):
                s_ = sums[done % 2]
                evs_[done % 2] = stt(s_, zp[:, done:done + T], lambda i, wt=wt, done=done: wt(i, done), s_,
                                     ALU.mult, ALU.add, evs_[done % 2])
                done += 1
        assert done == TAPS
        ev = tt(o, sums[0], sums[1], ALU.add, evs_)
        free["tmp4"] = free["tmp5"] = ev
        free[f"zpad{half}"] = ev
    q.end_loop()
    conv_done, gates_done = ev, free["gsig"]

    def tr4(e, i):
        for t in range(QT):
            mm_ = e.transpose(bank[5][:, t * P:(t + 1) * P], tmp[7][:, t * P:(t + 1) * P], ident)
        return mm_
    mm = pe(tr4, g, free.get("b5"))
    free["tmp7"] = mm
    gt_ready = func(gtok[:, :, :], bank[5][:, :].rearrange("p (k c) -> p k c", c=P)[:, :, 0:24], ACT.Sigmoid, mm)
    free["b5"] = gt_ready

    kps = (kp, kp2)
    kp_ready = []

    def compressed_input(s_):
        mm = project(s_, *H, KD)
        tb = 5 + s_
        v_ = scaled(s_, rs[0], tmp[tb][:, :], mm, inv, free.get(f"tmp{tb}"))
        evs_ = []
        for g_ in range(2):
            r = slice(64 * g_, 64 * g_ + 64)
            evs_.append(func(kps[s_][0:64, g_, :], tmp[tb][r, :], ACT.Copy, v_, conv_done))
            evs_.append(func(kps[s_][64:128, g_, 0:T - 1], tmp[tb][r, 1:T], ACT.Copy, v_, conv_done))
        free[f"tmp{tb}"] = evs_
        kp_ready.append(evs_)

    kd_ready, vc_ready = [], []

    def branch_kv(br):
        mm = project(0, *H, KD)
        a = tt(kd[br][0][0:64, :], bank[0][0:64, :], rs[0][0:64, :], ALU.mult, mm)
        b_ = tt(kd[br][1][64:128, :], bank[0][64:128, :], rs[0][64:128, :], ALU.mult, mm)
        free["b0"] = b_
        c_ = func(kd[br][0][64:128, :], kd[br][0][0:64, :], ACT.Copy, a)
        d_ = func(kd[br][1][0:64, :], kd[br][1][64:128, :], ACT.Copy, b_)
        kd_ready.append((a, b_, c_, d_))
        mm = project(1, *H, KD)
        v_ = scaled(1, rs[0], tmp[6][:, :], mm, inv, free.get("tmp6"))
        t_, e2 = token_major(tmp[6], vC[br], v_, None)
        free["tmp6"] = t_
        vc_ready.append(e2)

    def compress(s_):
        ww, pe_name = ((w1, "pek"), (w1v, "pev"))[s_]

        def cmp_mm(e, i):
            for n in range(16):
                rhs = kps[s_][:, :, 2 * n:2 * n + CMP_STRIDE * (N_CMP - 1) + 1:CMP_STRIDE]
                o = bank[2][:, 0:2 * N_CMP].rearrange("p (g n) -> p g n", g=2)
                e.matmul(o, ww[:, n, :], rhs, start=n == 0, stop=n == 15)
            for n in range(16):
                mm_ = e.matmul(bank[2][:, 64:65], ww[:, n, :], gg(pe_name, n), start=n == 0, stop=n == 15)
            return mm_
        mm = pe(cmp_mm, kp_ready[s_], w1_both, free.get("b2"))
        pb_ = dve(lambda e, i: e.tensor_copy(stat[:, 60 + s_:61 + s_], bank[2][:, 64:65]), mm)
        free["b2"] = func(hid[s_][:, 0:2 * N_CMP], bank[2][:, 0:2 * N_CMP], ACT.Gelu_apprx_tanh, pb_,
                          bias=stat[:, 60 + s_:61 + s_])
        return free["b2"], mm

    compressed_input(0)
    compressed_input(1)
    for c in range(4):
        su = add_plain(zc[:, c, :], 7, c == 0, c == 3, conv_done)
    mu = ts(rs[1][:, :], bank[7][:, :], -1.0 / CONV_C, None, ALU.mult, None, su, free.get("rs1"))
    free["b7"] = mu
    ce = [tt(zc[:, c, :], zc[:, c, :], rs[1][:, :], ALU.add, mu) for c in range(4)]
    hid0, _ = compress(0)
    for c in range(4):
        s2 = add_square(zc[:, c, :], 7, c == 0, c == 3, ce[c])
    hid1, cmp_read = compress(1)
    branch_kv(0)
    ln = inv_rms(rs[2], 7, CONV_C, s2)
    a = [tt(zc[:, c, :], zc[:, c, :], rs[2][:, :], ALU.mult, ln, s2) for c in range(4)]
    branch_kv(1)
    z_done = []
    for c in range(4):
        tb = 2 + c % 2
        b_ = func(tmp[tb][:, :], zc[:, c, :], ACT.Silu, a[c], free.get(f"tmp{tb}"), scale=gg("lng", c), bias=gg("lnb", c))
        free[f"tmp{tb}"] = split(tmp[tb][:, :], oh[:, 4 + c, :], ol[:, 4 + c, :], b_)
        z_done.append(free[f"tmp{tb}"])
    z_read = b_

    def c_queries(p, mm_):
        return scaled(3 + p % 2, rs[0], qC[p % 2][:, :], mm_, inv, free.get(f"pair{p % 2}"))

    free["pair0"] = free["pair1"] = None
    q_ready = {0: c_queries(0, project(3, *H, KD))}

    z0 = dve(lambda e, i: e.memset(vcb[0][:, :], 0.0), z_read)
    z1 = dve(lambda e, i: e.memset(vcb[1][:, :], 0.0), z_read)
    z2 = dve(lambda e, i: e.memset(pC[:, :, :], 0.0), z_read)
    mm = pe(lambda e, i: e.matmul(bank[2][:, 0:2 * N_CMP], gg("w2k", 0, P), hid[0][:, 0:2 * N_CMP], start=True, stop=True),
            hid0, free["b2"])
    kc_ready = dve(lambda e, i: e.tensor_copy(kcd[:, :, 0:N_CMP], bank[2][:, 0:2 * N_CMP].rearrange("p (g n) -> p g n", g=2)), mm)
    free["b2"] = kc_ready

    def vc_mm(e, i):
        for g_ in range(2):
            for e_ in range(2):
                mm_ = e.matmul(bank[2][32 * e_:32 * e_ + N_CMP, 64 * g_:64 * g_ + 64],
                               hid[1][:, g_ * N_CMP:(g_ + 1) * N_CMP], gg("w2v", 0, 64), start=True, stop=True)
        return mm_
    mm = pe(vc_mm, hid1, free["b2"])
    vcb_ready = []
    for g_ in range(2):
        for e_ in range(2):
            vcb_ready.append(dve(lambda e, i, g_=g_, e_=e_: e.tensor_copy(
                vcb[g_][32 * e_:32 * e_ + N_CMP, 64 * e_:64 * e_ + 64],
                bank[2][32 * e_:32 * e_ + N_CMP, 64 * g_:64 * g_ + 64]), mm, z0, z1))
    free["b2"] = vcb_ready

    free["PT"] = z_read
    free["probsC0"] = free["probsC1"] = (z_done, vc_ready, gt_ready)
    free["probsC2"] = cmp_read
    bc = tmp[5]
    pv = pC[:, :, :].rearrange("p t (e n) -> p (t e) n", n=32)[:, :, 0:N_CMP]
    pc_ready, front_of = {}, {}

    def compressed_front(p):
        b, g_ = p % 2, p // 2
        bcv = bc[:, 0:QT * 64].rearrange("p (t e n) -> p t e n", t=QT, e=2)
        cd = cc("cdist").rearrange("p (t n) -> p t n", t=QT)
        cm = cc("cmask").rearrange("p (t n) -> p t n", t=QT)
        bce = [stt(bcv[:, :, e_, :], cd, -SLOPES[2 * p + e_], cm, ALU.mult, ALU.add, SM, free.get("tmp5")) for e_ in range(2)]

        def c_scores(e, i):
            for t in range(QT):
                for e_ in range(2):
                    r = slice(64 * e_, 64 * e_ + 64)
                    mm_ = e.matmul(bank[3 + e_][:, t * 32:t * 32 + N_CMP],
                                   qC[b][r, t * P:(t + 1) * P], kcd[r, g_, 0:N_CMP], start=True, stop=True)
            return mm_
        mm = pe(c_scores, q_ready[p], kc_ready, free.get("b3"), free.get("b4"))
        st8, sm8 = stat[:, 48:56], stat[:, 56:64]
        a = []
        for e_ in range(2):
            sv = bank[3 + e_][:, 0:QT * 32].rearrange("p (t n) -> p t n", n=32)[:, :, 0:N_CMP]
            a.append(stt(pC[:, :, 32 * e_:32 * e_ + N_CMP], sv, 0.125, bcv[:, :, e_, 0:N_CMP], ALU.mult, ALU.add,
                         mm, bce, z2, free.get("pC")))
            free[f"b{3 + e_}"] = a[e_]
        free["tmp5"] = a
        m_ = dve(lambda e, i: e.tensor_reduce(st8, pv, AX.X, ALU.max), a)
        s_ = tt(pv, pv, st8.unsqueeze(2).to_broadcast([P, 8, N_CMP]), ALU.subtract, m_)
        x_ = func(pv, pv, ACT.Exp, s_)
        m_ = dve(lambda e, i: e.tensor_reduce(sm8, pv, AX.X, ALU.add), x_)
        r_ = dve(lambda e, i: e.reciprocal(sm8, sm8), m_)
        gate_c = gtok[:, :, 6 * p:6 * p + 6].rearrange("p t (e b) -> p t e b", b=3)[:, :, :, 0]
        sm = sm8.rearrange("p (t e) -> p t e", e=2)
        r_ = tt(sm, sm, gate_c, ALU.mult, r_, gt_ready)
        valid = cc("cvalid").rearrange("p (t n) -> p t n", t=QT)[:, :, 0:N_CMP]
        v_ = [tt(pC[:, :, 32 * e_:32 * e_ + N_CMP], pC[:, :, 32 * e_:32 * e_ + N_CMP], valid, ALU.mult, r_)
              for e_ in range(2)]
        pc_ready[p] = tt(pv, pv, sm8.unsqueeze(2).to_broadcast([P, 8, N_CMP]), ALU.mult, v_)

    def compressed_back(p):
        def c_tr(e, i):
            for t in range(QT):
                mm_ = e.transpose(bank[5][0:64, t * P:(t + 1) * P], pC[:, t, :], ident)
            return mm_
        mm = pe(c_tr, pc_ready[p], free.get("b5"))
        free["pC"] = mm
        c_pt = func(tmp[6][0:64, :], bank[5][0:64, :], ACT.Copy, mm, free.get("tmp6"))
        free["b5"] = c_pt
        return c_pt

    def compressed_product(p, c_pt):
        free["tmp6"] = pe(lambda e, i: e.matmul(bank[7][:, :], vcb[p // 2][:, :], tmp[6][0:64, :], start=True,
                                                stop=False, skip_group_check=True), c_pt, vcb_ready, free.get("b7"))

    def front(n, among=None):
        p, e_, br = n // 4, n // 2 % 2, n % 2
        b, g_, h = p % 2, p // 2, 2 * p + e_
        if br == 0:
            free["bias_now"] = ts(biasC[:, :], cc("dist"), -8.0 * SLOPES[h], None, ALU.mult, None, SM,
                                  free.get("biasC"), z_read)
        r = slice(64 * e_, 64 * e_ + 64)
        s_ = scores([(lambda t: qC[b][r, t * P:(t + 1) * P], lambda w: kd[br][g_][r, 0:w])], q_ready[p], kd_ready, among=among)
        pb, st = probsC[n % 3], 16 * (n % 3)
        m_ = bias_and_min(s_, pb, st, biasC, SCALE_B, free["bias_now"])
        free["biasC"] = m_[ORDER[-1]]
        free[f"pair{b}"] = s_[3]
        front_of[n] = exponent(m_, pb, st)

    def normalised(n):
        h, br = n // 2, n % 2
        gate = gtok[:, :, 3 * h + 1 + br:3 * h + 2 + br].rearrange("p t a -> p (t a)")
        return normalise(front_of[n], probsC[n % 3], 16 * (n % 3), gate, gt_ready)

    def values_of(br, g_):
        return lambda k: vC[br][:, k, 64 * g_:64 * g_ + 64]

    for n in range(-2, 4 * PAIRS_C):
        p, e_, br = n // 4, n // 2 % 2, n % 2
        if n >= 0:
            tr, tr_out = transposes(nn, probsC[n % 3])
        if n + 2 < 4 * PAIRS_C:
            front(n + 2, among=tr if n >= 0 else None)
            if n + 1 >= 0:
                nn = normalised(n + 1)
            if (n + 2) % 4 == 0:
                compressed_front((n + 2) // 4)
        elif n >= 0:
            tr[0]()
            tr[1]()
            if n + 1 < 4 * PAIRS_C:
                nn = normalised(n + 1)
        if n < 0:
            continue
        if n % 4 == 0:
            c_pt = compressed_back(p)
            if p + 1 < PAIRS_C:
                first_half, second_half = in_halves(3 + (p + 1) % 2, *H)
                first_half()
            compressed_product(p, c_pt)
        elif n % 4 == 1 and p + 1 < PAIRS_C:
            q_ready[p + 1] = c_queries(p + 1, second_half())
        elif n % 4 == 2:
            first_half, second_half = in_halves(3, *H)
            first_half()
        elif n % 4 == 3:
            gates_done2 = gate_sigmoid(lambda i, p=p: 12 + p, 3, second_half())
        ov = times_v(values_of(br, p // 2), (64 * e_, 64 * e_ + 64), (tr_out, vc_ready), first=False, last=n % 4 == 3)
        if n % 4 == 3:
            o_done = split(bank[7][:, :], oh[:, p, :], ol[:, p, :], ov)
            free["b7"] = o_done
    q_read = q_ready[3]

    h_read2 = (q_read, gates_done2)
    mready = {}
    for m in range(KD):
        ba, bb = 2 * (m % 2), 2 * (m % 2) + 1
        ms = use_unit([(bb, [(4 + k, oh[:, 4 + k, :], ol[:, 4 + k, :]) for k in range(4)], True, True, [free.get(f"b{bb}"), z_done]),
                       (ba, [(k, oh[:, k, :], ol[:, k, :]) for k in range(4)], True, True, [free.get(f"b{ba}"), o_done])])[::-1]
        ta, tb = 2 + m % 2, 4 + m % 2
        a = tt(tmp[ta][:, :], bank[ba][:, :], gsig[:, m, :], ALU.mult, ms[0], gates_done, free.get(f"tmp{ta}"))
        b_ = tt(tmp[tb][:, :], bank[bb][:, :], gsig[:, 8 + m, :], ALU.mult, ms[1], gates_done2, free.get(f"tmp{tb}"))
        free[f"b{ba}"], free[f"b{bb}"] = a, b_
        c_ = tt(tmp[ta][:, :], tmp[ta][:, :], tmp[tb][:, :], ALU.add, a, b_)
        free[f"tmp{tb}"] = c_
        s_ = split(tmp[ta][:, :], hh[:, m, :], hl[:, m, :], c_, None, h_read2)
        free[f"tmp{ta}"] = s_
        mready[m] = s_

    nready = {}
    for m in range(KD):
        bk = m % 2
        mm = project(bk, *H, KD, mready if m == 0 else None)
        a = tt(x[:, m, :], bank[bk][:, :], x[:, m, :], ALU.add, mm)
        free[f"b{bk}"] = a
        gather_square(x[:, m, :], m == 0, a)
        nready[m] = a
    last_read = mm
    ssq2 = sum_total(6, True, True)
    ready = {}
    for k in range(KD):
        ready[k] = split(x[:, k, :], hh[:, k, :], hl[:, k, :], nready[k], gg("norm2", k), last_read)
    inv = inv_rms(rs[0], 6, D, ssq2)
    evs, r = feed_forward(ready, inv, True)
    out_v = out.rearrange("(k p) t -> p k t", p=P)
    final = [stt(y[:, k, :], x[:, k, :], gg("final", k), bank[7][:, :], ALU.mult, ALU.mult, r) for k in range(KD)]
    assert lo_done.count == n_used and hi_done.count == n_units

    block = nc.Block()
    with block:
        @block.sync
        def _(e):
            x_v = x_in.rearrange("(k p) t -> p k t", p=P)

            def load_unit(j, u):
                e.dma_start(raw[j][:, :], stream[u, :, :]).then_inc(raw_in[j].sem, 16)
            e.dma_start(x[:, 0:4, :], x_v[:, 0:4, :]).then_inc(c_x[0].sem, 16)
            load_unit(0, 0)
            e.dma_start(x[:, 4:8, :], x_v[:, 4:8, :]).then_inc(c_x[1].sem, 16)
            load_unit(1, 1)
            with e.Fori(1, n_units // 2) as r:
                for j in range(2):
                    e.wait_ge(lo_done.sem, r * 2 + (j - 1))
                    e.dma_start(raw[j][:, :], stream[bass.ds(r * 2 + j, 1), :, :].rearrange("a p c -> p (a c)"))\
                        .then_inc(raw_in[j].sem, 16)

        @block.gpsimd
        def _(e):
            pad = nc.alloc_semaphore("lo_loop_turns")
            with e.Fori(0, n_units // 2) as r:
                for j in range(2):
                    e.wait_ge(hi_done.sem, r * 2 + (j + 1))
                    e.sem_inc(pad, 1)
                    e.tensor_tensor(wlo[j][:, :], raw[j][:, :], whi[j][:, :].bitcast(F32), ALU.subtract)\
                        .then_inc(lo_done.sem, 1)

        @block.scalar
        def _(e):
            e.sem_inc(chans["act"].sem, START)
            e.dma_start(gn[:, :], gains_in).then_inc(c_small.sem, 16)
            e.dma_start(cst[:, :], consts_in[:, 0:n_fixed]).then_inc(c_consts.sem, 16)
            e.dma_start(pos_i, pos_in.to_broadcast([P, T]) if pos_in.shape[0] == 1 else pos_in).then_inc(c_pos.sem, 16)
            e.dma_start(maskA[:, :], consts_in[:, CONST_AT["maskA"][0]:CONST_AT["maskA"][0] + T]).then_inc(c_mask.sem, 16)
            e.dma_start(rel[:, 255:575], rel_in).then_inc(c_rel.sem, 16)
            q.play("act", e)
            for k, ev in enumerate(final):
                e.wait_ge(ev.chan.sem, ev.n)
                e.dma_start(out_v[:, k, :], y[:, k, :]).then_inc(c_out.sem, 16)
            e.wait_ge(c_out.sem, 16 * KD)

        @block.vector
        def _(e):
            e.sem_inc(chans["dve"].sem, START)
            q.play("dve", e)

        @block.tensor
        def _(e):
            e.sem_inc(chans["pe"].sem, START)
            q.play("pe", e)


def kernel(**inputs):
    import concourse.bacc as bacc
    from concourse.bass_utils import run_bass_kernel_spmd as run
    a = {k: np.asarray(v) for k, v in inputs.items()}

    def cols(v):
        return np.ascontiguousarray(v.reshape(-1, P).T)

    weights = {
        "mla_a": a["mla_w_a"][0], "mla_uq": a["mla_w_uq"][0], "mla_ukv": a["mla_w_ukv"][0], "mla_o": a["mla_w_o"][0],
        "gate0": a["ffn_w_gate"][0], "up0": a["ffn_w_up"][0], "down0": a["ffn_w_down"][0],
        "gate1": a["ffn_w_gate"][1], "up1": a["ffn_w_up"][1], "down1": a["ffn_w_down"][1],
        "kv": a["w_kv_shared"], "b_q": a["b_w_q"][0], "b_o": a["b_w_o"][0],
        "w_in": a["w_in_2"][0], "attn_br": a["w_attn_br_2"][0], "conv_br": a["w_conv_br_2"][0],
        "w_out": a["w_out_2"][0], "ffn_up": a["ffn_w_up_2"][0], "ffn_down": a["ffn_w_down_2"][0],
    }
    stream = weight_units(weights)
    g = {
        "pre0": cols(a["attn_pre_g"][0]), "post0": cols(a["attn_post_g"][0]), "fpre0": cols(a["ffn_pre_g"][0]),
        "fpost0": cols(a["ffn_post_g"][0]), "gq": cols(a["mla_g_q"][0]), "gkv": cols(a["mla_g_kv"][0]),
        "kvsrc": cols(a["kv_src_g"]), "pre1": cols(a["attn_pre_g"][1]), "post1": cols(a["attn_post_g"][1]),
        "fpre1": cols(a["ffn_pre_g"][1]), "fpost1": cols(a["ffn_post_g"][1]), "norm1": cols(a["norm1_g_2"][0]),
        "norm2": cols(a["norm2_g_2"][0]), "final": cols(a["final_g_2"]),
        "dw": a["conv_dw_w_2"][0].reshape(TAPS, 4, P).transpose(2, 1, 0).reshape(P, -1),
        "dwb": cols(a["conv_dw_b_2"][0]), "lng": cols(a["conv_ln_g_2"][0]), "lnb": cols(a["conv_ln_b_2"][0]),
        "fdw": a["ffn_dw_w_2"][0].reshape(3, 2 * KF, P).transpose(2, 1, 0).reshape(P, -1),
        "fdwb": cols(a["ffn_dw_b_2"][0]),
        "pek": cols(a["cmp_pe_k_2"][0]), "pev": cols(a["cmp_pe_v_2"][0]),
        "w2k": np.concatenate([a["cmp_k_w2_2"][0]] * 2, 1), "w2v": a["cmp_v_w2_2"][0],
    }
    gains = np.ascontiguousarray(np.concatenate([g[n] for n, _ in GAINS], 1))
    w1 = np.stack([a[n][0].reshape(16, P, P).transpose(1, 0, 2) for n in ("cmp_k_w1_2", "cmp_v_w1_2")])
    arrays = {
        "x_in": np.ascontiguousarray(a["x"][0].T), "pos_in": a["positions"].reshape(1, T),
        "stream": stream, "gains_in": gains, "consts_in": shape_constants(),
        "rel_in": np.ascontiguousarray(a["b_rel_table"][0][:, ::-1]), "w1_in": np.ascontiguousarray(w1),
    }
    nc = bacc.Bacc("TRN2", target_bir_lowering=False, num_devices=1)
    args = [nc.dram_tensor(n, v.shape, mybir.dt.from_np(v.dtype), kind="ExternalInput").ap() for n, v in arrays.items()]
    args.append(nc.dram_tensor("out", (D, T), F32, kind="ExternalOutput").ap())
    build(nc, *args)
    r = run(nc, [arrays], core_ids=[0])
    return np.ascontiguousarray(r.results[0]["out"].T).reshape(1, T, D)
```
